# Optimizing a Trainium2 kernel written in Bass

```python
import functools
import jax, jax.numpy as jnp
from jax import lax
import numpy as np

D_MODEL = 1024
BATCH = 1
SEQ = 1024
DEPTH = 1

GRID_W = 64
CTX_LEN = 256
CHUNK = 64
EPS = 1e-6
NEG_BIG = -1e30
ML_HEADS = 4
ML_QK = D_MODEL // 8
ML_V = D_MODEL // 4
GLA_HEADS = 4
GLA_QK = D_MODEL // 8
GLA_V = D_MODEL // 4
GLA_RANK = 16
GLA_TAU = 16.0
CONV_K = 3
N_GROUPS = 4
EXPERTS_PER_GROUP = 4
N_EXPERTS = N_GROUPS * EXPERTS_PER_GROUP
TOP_K = 2
D_EXPERT = D_MODEL // 2
MOE_BLOCK = 128
ML_QK_W = ML_HEADS * ML_QK
ML_V_W = ML_HEADS * ML_V
GLA_QK_W = GLA_HEADS * GLA_QK
GLA_V_W = GLA_HEADS * GLA_V
IN_SIZES = (ML_QK_W, ML_QK_W, ML_V_W, ML_V_W, 4 * ML_HEADS,
            GLA_QK_W, GLA_QK_W, GLA_V_W, GLA_V_W, 2 * GLA_RANK,
            D_MODEL, D_MODEL)
IN_WIDTH = sum(IN_SIZES)

kernel_name = 'hybrid_mlstm_gla_hmoe_dit'

def rms_norm(x, g):
    xf = x.astype(jnp.float32)
    xf = xf * lax.rsqrt(jnp.mean(xf * xf, axis=-1, keepdims=True) + EPS)
    return xf.astype(x.dtype) * g

def split_heads(a, n_heads):
    bn, t, w = a.shape
    return a.reshape(bn, t, n_heads, w // n_heads).transpose(0, 2, 1, 3)

def merge_heads_rms(h, g, dtype):
    bn, nh, t, dh = h.shape
    h = h.transpose(0, 2, 1, 3)
    h = h * lax.rsqrt(jnp.mean(h * h, axis=-1, keepdims=True) + EPS)
    return h.reshape(bn, t, nh * dh).astype(dtype) * g

def flip_t(a):
    return jnp.flip(a, axis=2)

def dw_conv_silu(u, w, b, rows, cols):
    bn, t, ch = u.shape
    img = u.reshape(bn, rows, cols, ch)
    out = lax.conv_general_dilated(img, w[:, :, None, :], window_strides=(1, 1), padding='SAME',
                                   dimension_numbers=('NHWC', 'HWIO', 'NHWC'), feature_group_count=ch)
    return jax.nn.silu(out.reshape(bn, t, ch) + b)

def to_chunks(a):
    bn, nh, t = a.shape[:3]
    return jnp.moveaxis(a.reshape(bn, nh, t // CHUNK, CHUNK, *a.shape[3:]), 2, 0)

def from_chunks(a):
    nc, bn, nh, l = a.shape[:4]
    return jnp.moveaxis(a, 0, 2).reshape(bn, nh, nc * l, *a.shape[4:])

def mlstm_scan(q, k, v, i_pre, f_pre, state, with_output):
    tri = jnp.arange(CHUNK)[:, None] >= jnp.arange(CHUNK)[None, :]
    log_f = jax.nn.log_sigmoid(f_pre)

    def step(carry, xs):
        c_mat, n_vec, m = carry
        qc, kc, vc, ic, fc = xs
        b = jnp.cumsum(fc, axis=-1)
        b_end = b[..., -1]
        log_w = b_end[..., None] - b + ic
        m_new = jnp.maximum(b_end + m, jnp.max(log_w, axis=-1))
        w = jnp.exp(log_w - m_new[..., None])
        decay = jnp.exp(b_end + m - m_new)
        c_new = decay[..., None, None] * c_mat + jnp.einsum('bhs,bhsd,bhsv->bhdv', w, kc, vc)
        n_new = decay[..., None] * n_vec + jnp.einsum('bhs,bhsd->bhd', w, kc)
        if not with_output:
            return (c_new, n_new, m_new), None
        log_d = jnp.where(tri, b[..., :, None] - b[..., None, :] + ic[..., None, :], -jnp.inf)
        log_inter = b + m[..., None]
        m_t = jnp.maximum(log_inter, jnp.max(log_d, axis=-1))
        s = jnp.einsum('bhtd,bhsd->bhts', qc, kc) * jnp.exp(log_d - m_t[..., None])
        w_inter = jnp.exp(log_inter - m_t)
        num = jnp.einsum('bhts,bhsv->bhtv', s, vc) + w_inter[..., None] * jnp.einsum('bhtd,bhdv->bhtv', qc, c_mat)
        den = jnp.abs(jnp.sum(s, axis=-1) + w_inter * jnp.einsum('bhtd,bhd->bht', qc, n_vec))
        h = num / jnp.maximum(den, jnp.exp(-m_t))[..., None]
        return (c_new, n_new, m_new), h

    state, hs = lax.scan(step, state, (to_chunks(q), to_chunks(k), to_chunks(v), to_chunks(i_pre), to_chunks(log_f)))
    return (from_chunks(hs) if with_output else None), state

def gla_scan(q, k, v, log_a, state, with_output):
    tri = jnp.arange(CHUNK)[:, None] >= jnp.arange(CHUNK)[None, :]

    def step(s_mat, xs):
        qc, kc, vc, ac = xs
        b = jnp.cumsum(ac, axis=2)
        b_end = b[:, :, -1]
        s_new = jnp.exp(b_end)[..., None] * s_mat + jnp.einsum('bhsd,bhsv->bhdv', kc * jnp.exp(b_end[:, :, None] - b), vc)
        if not with_output:
            return s_new, None
        rel = jnp.where(tri[:, :, None], b[:, :, :, None] - b[:, :, None], -jnp.inf)
        scores = jnp.einsum('bhtd,bhsd,bhtsd->bhts', qc, kc, jnp.exp(rel))
        o = jnp.einsum('bhts,bhsv->bhtv', scores, vc) + jnp.einsum('bhtd,bhdv->bhtv', qc * jnp.exp(b), s_mat)
        return s_new, o

    state, os_ = lax.scan(step, state, (to_chunks(q), to_chunks(k), to_chunks(v), to_chunks(log_a)))
    return (from_chunks(os_) if with_output else None), state

def empty_states(bn):
    ml = (jnp.zeros((bn, ML_HEADS, ML_QK, ML_V), jnp.float32),
          jnp.zeros((bn, ML_HEADS, ML_QK), jnp.float32),
          jnp.full((bn, ML_HEADS), NEG_BIG, jnp.float32))
    gla = jnp.zeros((bn, GLA_HEADS, GLA_QK, GLA_V), jnp.float32)
    return (ml, ml, gla, gla)

def token_mixers(h, conv_fn, init_states, with_output, w_in, ml_conv, ml_conv_b, b_mgate, ml_norm,
                 gla_w2, gla_b2, gla_norm, w_proj_m, w_proj_g, w_out):
    bn, t, _ = h.shape
    f32 = jnp.float32
    cuts = [int(s) for s in np.cumsum(IN_SIZES)[:-1]]
    (q_m, k_m, v_m, o_m, gate_m, q_g, k_g, v_g, r_g, lr_g, mg_m, mg_g) = jnp.split(h @ w_in, cuts, axis=-1)
    st_mf, st_mb, st_gf, st_gb = init_states

    qk = conv_fn(jnp.concatenate([q_m, k_m], axis=-1), ml_conv, ml_conv_b)
    q_m, k_m = jnp.split(qk, 2, axis=-1)
    qm = split_heads(q_m, ML_HEADS).astype(f32)
    km = split_heads(k_m, ML_HEADS).astype(f32) * (ML_QK ** -0.5)
    vm = split_heads(v_m, ML_HEADS).astype(f32)
    gm = (gate_m + b_mgate).astype(f32).reshape(bn, t, 2, 2, ML_HEADS).transpose(2, 3, 0, 4, 1)
    hm_f, st_mf = mlstm_scan(qm, km, vm, gm[0, 0], gm[0, 1], st_mf, with_output)
    hm_b, st_mb = mlstm_scan(flip_t(qm), flip_t(km), flip_t(vm), flip_t(gm[1, 0]), flip_t(gm[1, 1]), st_mb, with_output)

    qg = split_heads(q_g, GLA_HEADS).astype(f32) * (GLA_QK ** -0.5)
    kg = split_heads(k_g, GLA_HEADS).astype(f32)
    vg = split_heads(v_g, GLA_HEADS).astype(f32)
    lr = lr_g.astype(f32).reshape(bn, t, 2, GLA_RANK)
    log_a = jax.nn.log_sigmoid(jnp.einsum('btdr,dre->dbte', lr, gla_w2.astype(f32)) + gla_b2.astype(f32)[:, None, None, :]) / GLA_TAU
    og_f, st_gf = gla_scan(qg, kg, vg, split_heads(log_a[0], GLA_HEADS), st_gf, with_output)
    og_b, st_gb = gla_scan(flip_t(qg), flip_t(kg), flip_t(vg), flip_t(split_heads(log_a[1], GLA_HEADS)), st_gb, with_output)

    states = (st_mf, st_mb, st_gf, st_gb)
    if not with_output:
        return None, states
    y_m = merge_heads_rms(hm_f + flip_t(hm_b), ml_norm, h.dtype) * jax.nn.sigmoid(o_m)
    y_g = merge_heads_rms(og_f + flip_t(og_b), gla_norm, h.dtype) * jax.nn.silu(r_g)
    y = jax.nn.sigmoid(mg_m) * (y_m @ w_proj_m) + jax.nn.sigmoid(mg_g) * (y_g @ w_proj_g)
    return y @ w_out, states

def hier_moe(h, w_grp, b_grp, w_rexp, b_rexp, w_up, w_down):
    bn, t, d = h.shape
    n_tok = bn * t
    hf = h.reshape(n_tok, d)
    p_grp = jax.nn.softmax((hf @ w_grp + b_grp).astype(jnp.float32), axis=-1)
    grp_p, grp = lax.top_k(p_grp, 1)
    e_logits = (hf @ w_rexp + b_rexp).astype(jnp.float32).reshape(n_tok, N_GROUPS, EXPERTS_PER_GROUP)
    p_in = jax.nn.softmax(e_logits[jnp.arange(n_tok), grp[:, 0]], axis=-1)
    top_p, top_i = lax.top_k(p_in, TOP_K)
    weights = grp_p * top_p / jnp.sum(top_p, axis=-1, keepdims=True)
    expert = grp * EXPERTS_PER_GROUP + top_i

    n_assign = n_tok * TOP_K
    flat_e = expert.reshape(n_assign)
    flat_t = jnp.repeat(jnp.arange(n_tok, dtype=jnp.int32), TOP_K)
    flat_w = weights.reshape(n_assign)
    order = jnp.argsort(flat_e)
    se, st, sw = flat_e[order], flat_t[order], flat_w[order]
    counts = jnp.zeros((N_EXPERTS,), jnp.int32).at[flat_e].add(1)
    padded = (counts + MOE_BLOCK - 1) // MOE_BLOCK * MOE_BLOCK
    pad_end = jnp.cumsum(padded)
    dest = (pad_end - padded)[se] + jnp.arange(n_assign, dtype=jnp.int32) - (jnp.cumsum(counts) - counts)[se]
    n_blocks = -(-n_assign // MOE_BLOCK) + N_EXPERTS
    n_rows = n_blocks * MOE_BLOCK
    row_tok = jnp.full((n_rows,), n_tok, jnp.int32).at[dest].set(st)
    row_w = jnp.zeros((n_rows,), jnp.float32).at[dest].set(sw)
    block_e = jnp.minimum(jnp.searchsorted(pad_end, jnp.arange(n_blocks, dtype=jnp.int32) * MOE_BLOCK, side='right'), N_EXPERTS - 1)
    x_rows = jnp.concatenate([hf, jnp.zeros((1, d), h.dtype)], axis=0)[row_tok].reshape(n_blocks, MOE_BLOCK, d)

    def expert_block(args):
        xb, e = args
        gate, up = jnp.split(xb @ w_up[e], 2, axis=-1)
        return (jax.nn.silu(gate) * up) @ w_down[e]

    y_rows = lax.map(expert_block, (x_rows, block_e)).reshape(n_rows, d)
    y = jnp.zeros((n_tok + 1, d), h.dtype).at[row_tok].add(y_rows * row_w[:, None].astype(h.dtype))
    return y[:n_tok].reshape(bn, t, d)

def setup_inputs(seed: int = 0) -> dict:
    key = jax.random.key(seed)
    ks = jax.random.split(key, 26)

    def nrm(k, shape, scale):
        return jax.random.normal(k, shape, jnp.float32) * scale

    L = DEPTH
    d = D_MODEL
    inv = d ** -0.5
    gate_offset = jnp.array([0.0, 3.0], jnp.float32)[None, None, :, None]
    return {
        'x': nrm(ks[0], (BATCH, SEQ, d), 1.0),
        'c': nrm(ks[1], (BATCH, d), 1.0),
        'ctx': nrm(ks[2], (BATCH, CTX_LEN, d), 1.0),
        'c_ctx': nrm(ks[3], (d,), 1.0),
        'w_mod': nrm(ks[4], (L, d, 6 * d), 0.5 * inv),
        'b_mod': nrm(ks[5], (L, 6 * d), 0.01),
        'g_norm1': 1.0 + nrm(ks[6], (L, d), 0.1),
        'w_in': nrm(ks[7], (L, d, IN_WIDTH), inv),
        'ml_conv': nrm(ks[8], (L, CONV_K, CONV_K, 2 * ML_QK_W), 1.0 / CONV_K),
        'ml_conv_b': nrm(ks[9], (L, 2 * ML_QK_W), 0.01),
        'b_mgate': (nrm(ks[10], (L, 2, 2, ML_HEADS), 0.1) + gate_offset).reshape(L, 4 * ML_HEADS),
        'ml_norm': 1.0 + nrm(ks[11], (L, ML_V_W), 0.1),
        'gla_w2': nrm(ks[12], (L, 2, GLA_RANK, GLA_QK_W), GLA_RANK ** -0.5),
        'gla_b2': nrm(ks[13], (L, 2, GLA_QK_W), 0.01),
        'gla_norm': 1.0 + nrm(ks[14], (L, GLA_V_W), 0.1),
        'w_proj_m': nrm(ks[15], (L, ML_V_W, d), ML_V_W ** -0.5),
        'w_proj_g': nrm(ks[16], (L, GLA_V_W, d), GLA_V_W ** -0.5),
        'w_out': nrm(ks[17], (L, d, d), inv),
        'g_norm2': 1.0 + nrm(ks[18], (L, d), 0.1),
        'w_grp': nrm(ks[19], (L, d, N_GROUPS), inv),
        'b_grp': nrm(ks[20], (L, N_GROUPS), 0.01),
        'w_rexp': nrm(ks[21], (L, d, N_EXPERTS), inv),
        'b_rexp': nrm(ks[22], (L, N_EXPERTS), 0.01),
        'w_up': nrm(ks[23], (L, N_EXPERTS, d, 2 * D_EXPERT), inv),
        'w_down': nrm(ks[24], (L, N_EXPERTS, D_EXPERT, d), D_EXPERT ** -0.5),
        'g_final': 1.0 + nrm(ks[25], (d,), 0.1),
    }

def reference(x, c, ctx, c_ctx, w_mod, b_mod, g_norm1, w_in, ml_conv, ml_conv_b, b_mgate, ml_norm,
              gla_w2, gla_b2, gla_norm, w_proj_m, w_proj_g, w_out, g_norm2, w_grp, b_grp, w_rexp, b_rexp,
              w_up, w_down, g_final):
    bn, t, _ = x.shape
    rows = t // GRID_W
    conv_lat = functools.partial(dw_conv_silu, rows=rows, cols=GRID_W)
    conv_ctx = functools.partial(dw_conv_silu, rows=1, cols=ctx.shape[1])
    h_ctx = ctx
    for l in range(DEPTH):
        last = l == DEPTH - 1
        sh1, sc1, gt1, sh2, sc2, gt2 = [m[:, None, :] for m in jnp.split(jax.nn.silu(c) @ w_mod[l] + b_mod[l], 6, axis=-1)]
        sh1c, sc1c, gt1c, sh2c, sc2c, gt2c = jnp.split(jax.nn.silu(c_ctx) @ w_mod[l] + b_mod[l], 6, axis=-1)
        mix = functools.partial(token_mixers, w_in=w_in[l], ml_conv=ml_conv[l], ml_conv_b=ml_conv_b[l],
                                b_mgate=b_mgate[l], ml_norm=ml_norm[l], gla_w2=gla_w2[l], gla_b2=gla_b2[l],
                                gla_norm=gla_norm[l], w_proj_m=w_proj_m[l], w_proj_g=w_proj_g[l], w_out=w_out[l])
        ffn = functools.partial(hier_moe, w_grp=w_grp[l], b_grp=b_grp[l], w_rexp=w_rexp[l], b_rexp=b_rexp[l],
                                w_up=w_up[l], w_down=w_down[l])
        hc = rms_norm(h_ctx, g_norm1[l]) * (1.0 + sc1c) + sh1c
        ctx_out, ctx_states = mix(hc, conv_fn=conv_ctx, init_states=empty_states(bn), with_output=not last)
        hx = rms_norm(x, g_norm1[l]) * (1.0 + sc1) + sh1
        x_mix, _ = mix(hx, conv_fn=conv_lat, init_states=ctx_states, with_output=True)
        x = x + gt1 * x_mix
        x = x + gt2 * ffn(rms_norm(x, g_norm2[l]) * (1.0 + sc2) + sh2)
        if not last:
            h_ctx = h_ctx + gt1c * ctx_out
            h_ctx = h_ctx + gt2c * ffn(rms_norm(h_ctx, g_norm2[l]) * (1.0 + sc2c) + sh2c)
    return rms_norm(x, g_final)


_drawn_inputs = setup_inputs


def setup_inputs(seed=0):
    import zlib

    import numpy as np

    out = dict(_drawn_inputs(seed))
    spreads = {}
    factors = {'ctx': 4.483,
     'c_ctx': 6.714,
     'b_mod': 4.567,
     'ml_conv_b': 23.532,
     'ml_norm': 4.913,
     'gla_w2': 2.827,
     'gla_b2': 27.295,
     'gla_norm': 4.153,
     'b_grp': 36.402,
     'b_rexp': 33.886}
    for name, (base, spread) in spreads.items():
        noise = np.random.default_rng([zlib.crc32(name.encode()), seed]).standard_normal(out[name].shape)
        drawn = base * np.exp(spread * noise) if base else spread * noise
        out[name] = __import__('jax').numpy.asarray(drawn.astype(out[name].dtype))
    for name, factor in factors.items():
        out[name] = (out[name] * factor).astype(out[name].dtype)
    return out
```

```python
from contextlib import ExitStack

import concourse.bass as bass
from concourse import mybir

F32 = mybir.dt.float32
F32R = mybir.dt.float32r
I32 = mybir.dt.int32
ALU = mybir.AluOpType
ACT = mybir.ActivationFunctionType
AX = mybir.AxisListType

P = 128
D = 1024
KD = D // P
SEQ = 1024
CTX = 256
T = CTX + SEQ
NT = T // P
NC = CTX // P
NL = SEQ // P
GRID_W = 64
GRID_H = SEQ // GRID_W
HEADS = 4
DK = 128
DV = 256
RANK = 16
TAU = 16.0
EPS = 1e-6
NEG_BIG = -1e30
LEVELS = 7
GROUPS = 4
PER_GROUP = 4
EXPERTS = GROUPS * PER_GROUP
FF = 512
TOP_K = 2
BLOCKS = (SEQ * TOP_K + EXPERTS * (P - 1)) // P

QM, KM, VM, OM = 0, 512, 1024, 2048
GATE = 3072
QG, KG, VG, RG = 3088, 3600, 4112, 5136
LR = 6160
MGM, MGG = 6192, 7216
COLS = 512

GATE_ROWS = 36
SMALL = 100
CONV_B, GN1, B2, NORM_M, NORM_G, NVEC = 9, 10, 11, 12, 13, 14


class Shared:
    pass


def constants(nc, m, sem, w):
    with ExitStack() as ctx:
        rows = ctx.enter_context(nc.sbuf_tensor("vec_rows", [NVEC, D], F32))
        ps = ctx.enter_context(nc.psum_tensor("vec_ps", [P, KD * NVEC], F32))
        built = sem("const_built")
        ident_ready = sem("ident_ready")
        rows_loaded = sem("vec_rows_loaded")
        turned = sem("vec_turned")
        moved = sem("vec_moved")
        block = ctx.enter_context(nc.Block())

        @block.sync
        def _(sp):
            loads = [
                (rows[0:9, :], w["ml_conv"][0].rearrange("a b n -> (a b) n")),
                (rows[CONV_B:CONV_B + 1, :], w["ml_conv_b"]),
                (rows[GN1:GN1 + 1, :], w["g_norm1"]),
                (rows[B2:B2 + 1, :], w["gla_b2"].rearrange("a d e -> a (d e)")),
                (rows[NORM_M:NORM_M + 1, :], w["ml_norm"]),
                (rows[NORM_G:NORM_G + 1, :], w["gla_norm"]),
            ]
            for dst, src in loads:
                sp.dma_start(dst, src).then_inc(rows_loaded, 16)

        @block.gpsimd
        def _(pool):
            n = [0]

            def step(ins):
                n[0] += 1
                ins.then_inc(built, 1)
                pool.wait_ge(built, n[0])

            step(pool.memset(m.ident[:, :], 0.0))
            pool.affine_select(out=m.ident[:, :], in_=m.ident[:, :], compare_op=ALU.not_equal, fill=1.0,
                               base=0, pattern=[[-1, P]], channel_multiplier=1).then_inc(ident_ready, 1)
            step(pool.memset(m.ones[:, :], 1.0))
            step(pool.memset(m.eps[:, :], EPS))
            step(pool.affine_select(out=m.before[:, :], in_=m.ones[:, :], compare_op=ALU.is_gt, fill=0.0,
                                    base=0, pattern=[[1, P]], channel_multiplier=-1))
            step(pool.memset(m.row_of[:, :, :], 0.0))
            v = m.row_of[:, :, :].rearrange("p (d h) t -> p d h t", d=2)
            step(pool.affine_select(out=v, in_=v, compare_op=ALU.not_equal, fill=1.0, base=0,
                                    pattern=[[-32, 2], [-1, HEADS], [0, P]], channel_multiplier=1))
            step(pool.memset(m.level_mask[:, :, :, :], 1))
            for d in range(2):
                for l in range(LEVELS):
                    h = 1 << l
                    nj = P // 2 // h
                    v = m.level_mask[:, d, l, :].rearrange("p (n j i) -> p n j i", n=HEADS, i=h)
                    step(pool.affine_select(out=v, in_=v, compare_op=ALU.is_ge, fill=0.0, base=-h * d,
                                            pattern=[[0, HEADS], [-2 * h, nj], [0, h]], channel_multiplier=1))
                    step(pool.affine_select(out=v, in_=v, compare_op=ALU.is_ge, fill=0.0, base=h - 1 + h * d,
                                            pattern=[[0, HEADS], [2 * h, nj], [0, h]], channel_multiplier=-1))
            step(pool.memset(m.restart[:, :, :], 1.0))
            v = m.restart[:, :, :].rearrange("p d (c t) -> p d c t", t=P)
            step(pool.memset(v[:, 0, :, 0:1], 0.0))
            step(pool.memset(v[:, 1, :, P - 1:P], 0.0))

        @block.tensor
        def _(pe):
            pe.wait_ge(ident_ready, 1)
            pe.wait_ge(rows_loaded, 16 * 6)
            for k in range(KD):
                last = pe.transpose(ps[:, k * NVEC:(k + 1) * NVEC], rows[:, k * P:(k + 1) * P],
                                    m.ident[0:NVEC, 0:NVEC])
            last.then_inc(turned, 1)

        @block.vector
        def _(dve):
            dve.wait_ge(turned, 1)
            dve.tensor_copy(m.vec[:, :, :], ps[:, :].rearrange("p (k n) -> p k n", k=KD)).then_inc(moved, 1)
            dve.wait_ge(moved, 1)


def modulation(nc, m, sem, w):
    GM = 6 * D // COLS
    with ExitStack() as ctx:
        sb = lambda n, s: ctx.enter_context(nc.sbuf_tensor(n, s, F32))
        wt = sb("mod_w", [P, 4, KD, COLS])
        c_raw = sb("mod_c_raw", [P, 2, KD])
        c_act = sb("mod_c", [P, 2, KD])
        bias = sb("mod_bias", [2, 6 * D])
        row = sb("mod_row", [2, 2, COLS])
        first = sb("mod_first", [2, P])
        mod_all = sb("mod_all", [P, 4 * D])
        rows_ps = [ctx.enter_context(nc.psum_tensor(f"mod_rows_ps{j}", [2, COLS], F32)) for j in range(2)]
        out_ps = [ctx.enter_context(nc.psum_tensor(f"mod_out_ps{j}", [P, COLS], F32)) for j in range(2)]
        c_loaded, bias_loaded = sem("mod_c_loaded"), sem("mod_bias_loaded")
        c_ready = sem("mod_c_ready")
        first_ready = sem("mod_first_ready")
        w_loaded = [sem(f"mod_w_loaded{j}") for j in range(4)]
        rows_done = sem("mod_rows_done")
        row_ready = sem("mod_row_ready")
        out_done = sem("mod_out_done")
        out_moved = sem("mod_out_moved")
        block = ctx.enter_context(nc.Block())
        wsrc = w["w_mod"][0].rearrange("(p k) n -> p k n", k=KD)

        @block.sync
        def _(sp):
            for j in range(4):
                sp.dma_start(wt[:, j, :, :], wsrc[:, :, j * COLS:(j + 1) * COLS]).then_inc(w_loaded[j], 16)
            with sp.Fori(1, GM // 4) as i:
                for j in range(4):
                    sp.wait_ge(rows_done, 4 * i + j - 3)
                    sp.dma_start(wt[:, j, :, :], wsrc[:, :, bass.ds((4 * i + j) * COLS, COLS)])\
                        .then_inc(w_loaded[j], 16)

        @block.scalar
        def _(act):
            act.dma_start(c_raw[:, 0, :], w["c"][0].rearrange("(p k) -> p k", k=KD)).then_inc(c_loaded, 16)
            act.dma_start(c_raw[:, 1, :], w["c_ctx"].rearrange("(p k) -> p k", k=KD)).then_inc(c_loaded, 16)
            act.dma_start(bias[0:1, :], w["b_mod"]).then_inc(bias_loaded, 16)
            act.dma_start(bias[1:2, :], w["b_mod"]).then_inc(bias_loaded, 16)
            act.wait_ge(c_loaded, 32)
            act.activation(c_act[:, :, :], c_raw[:, :, :], ACT.Silu).then_inc(c_ready, 1)
            for g in range(4):
                act.wait_ge(out_done, g + 1)
                act.activation(m.mod_col[:, 4 * g:4 * g + 4, :],
                               out_ps[g % 2][:, 0:8].rearrange("p (c s) -> p c s", s=2), ACT.Copy)\
                    .then_inc(out_moved, 1)
            with act.Fori(0, (GM - 4) // 2) as i:
                for j in range(2):
                    act.wait_ge(out_done, 2 * i + j + 5)
                    act.activation(mod_all[:, bass.ds((2 * i + j) * COLS, COLS)], out_ps[j][:, :], ACT.Copy)\
                        .then_inc(out_moved, 1)
            act.wait_ge(out_moved, GM)
            act.dma_start(m.mod_rows, mod_all[:, :]).then_inc(bias_loaded, 16)
            act.wait_ge(bias_loaded, 48)

        @block.gpsimd
        def _(pool):
            pool.affine_select(out=first[:, :], in_=m.ones[0:2, :], compare_op=ALU.is_equal, fill=0.0,
                               base=0, pattern=[[0, P]], channel_multiplier=1).then_inc(first_ready, 1)
            pool.wait_ge(first_ready, 1)

        @block.tensor
        def _(pe):
            pe.wait_ge(c_ready, 1)
            pe.wait_ge(first_ready, 1)

            def rows(slot, round_, j, n):
                pe.wait_ge(w_loaded[slot], 16 * round_ + 16)
                for k in range(KD):
                    last = pe.matmul(rows_ps[j][:, :], c_act[:, :, k], wt[:, slot, k, :],
                                     start=(k == 0), stop=(k == KD - 1))
                last.then_inc(rows_done, 1)

            def columns(j, n):
                pe.wait_ge(row_ready, n + 1)
                if n >= 2:
                    pe.wait_ge(out_moved, n - 1)
                for q in range(4):
                    last = pe.transpose(out_ps[j][:, 2 * q:2 * q + 2], row[:, j, q * P:(q + 1) * P],
                                        m.ident[0:2, 0:2])
                last.then_inc(out_done, 1)

            def spread(j, n):
                pe.wait_ge(row_ready, n + 1)
                pe.wait_ge(out_moved, n - 1)
                pe.matmul(out_ps[j][:, :], first[:, :], row[:, j, :], start=True, stop=True)\
                    .then_inc(out_done, 1)

            for n in range(4):
                rows(n, 0, n % 2, n)
                columns(n % 2, n)
            with pe.Fori(1, GM // 4) as i:
                for j in range(4):
                    rows(j, i, j % 2, 4 * i + j)
                    spread(j % 2, 4 * i + j)

        @block.vector
        def _(dve):
            dve.wait_ge(bias_loaded, 32)
            with dve.Fori(0, GM // 2) as i:
                for j in range(2):
                    dve.wait_ge(rows_done, 2 * i + j + 1)
                    dve.tensor_tensor(row[:, j, :], rows_ps[j][:, :],
                                      bias[:, bass.ds((2 * i + j) * COLS, COLS)], ALU.add).then_inc(row_ready, 1)
            dve.wait_ge(out_moved, 4)
            dve.scalar_tensor_tensor(out=m.a1[:, :, :], in0=m.mod_col[:, KD:2 * KD, :], scalar=1.0,
                                     in1=m.vec[:, :, GN1:GN1 + 1].to_broadcast([P, KD, 2]),
                                     op0=ALU.add, op1=ALU.mult).then_inc(row_ready, 1)
            dve.wait_ge(row_ready, GM + 1)


def norm_in(nc, m, sem, w):
    with ExitStack() as ctx:
        sb = lambda n, s: ctx.enter_context(nc.sbuf_tensor(n, s, F32))
        xt = sb("nin_x", [P, 2, D])
        sq = sb("nin_sq", [P, 2, D])
        xn = sb("nin_xn", [P, 2, D])
        st = sb("nin_stat", [P, 2, 3])
        ps = [ctx.enter_context(nc.psum_tensor(f"nin_ps{j}", [P, D], F32)) for j in range(2)]
        x_loaded = [sem(f"nin_x_loaded{j}") for j in range(2)]
        stat, xn_ready, turned, moved = (sem(f"nin_{n}") for n in
                                                 ("stat", "xn_ready", "turned", "moved"))
        block = ctx.enter_context(nc.Block())

        @block.sync
        def _(sp):
            def load(src, pair, tile):
                for j in range(2):
                    if not isinstance(pair, int):
                        sp.wait_ge(xn_ready, 2 * pair + j - 1)
                    sp.dma_start(xt[:, j, :], src[bass.ds((tile + j) * P, P), :]).then_inc(x_loaded[j], 16)
            load(w["ctx"][0], 0, 0)
            with sp.Fori(1, NT // 2) as i:
                load(w["x"][0], i, 2 * i - 2)

        @block.scalar
        def _(act):
            def normalise(i):
                for j in range(2):
                    n = 2 * i + j
                    act.wait_ge(x_loaded[j], 16 * i + 16)
                    act.activation(sq[:, j, :], xt[:, j, :], ACT.Square, accum_out=st[:, j, 0:1]).then_inc(stat, 1)
                    act.wait_ge(stat, 3 * n + 1)
                    act.activation(st[:, j, 1:2], st[:, j, 0:1], ACT.Ln, bias=m.eps[:, 0:1], scale=1.0 / D).then_inc(stat, 1)
                    act.wait_ge(stat, 3 * n + 2)
                    act.activation(st[:, j, 2:3], st[:, j, 1:2], ACT.Exp, scale=-0.5).then_inc(stat, 1)
                    act.wait_ge(stat, 3 * n + 3)
                    if not isinstance(i, int):
                        act.wait_ge(turned, n - 1)
                    act.activation(xn[:, j, :], xt[:, j, :], ACT.Copy, scale=st[:, j, 2:3]).then_inc(xn_ready, 1)
            normalise(0)
            with act.Fori(1, NT // 2) as i:
                normalise(i)

        @block.tensor
        def _(pe):
            def turn(i):
                for j in range(2):
                    pe.wait_ge(xn_ready, 2 * i + j + 1)
                    if not isinstance(i, int):
                        pe.wait_ge(moved, 2 * i + j - 1)
                    for k in range(KD):
                        last = pe.transpose(ps[j][:, k * P:(k + 1) * P], xn[:, j, k * P:(k + 1) * P], m.ident[:, :])
                    last.then_inc(turned, 1)
            turn(0)
            with pe.Fori(1, NT // 2) as i:
                turn(i)

        @block.vector
        def _(dve):

            def leave(i, stream):
                for j in range(2):
                    dve.wait_ge(turned, 2 * i + j + 1)
                    for k in range(KD):
                        last = dve.tensor_scalar(m.h_t[:, k, bass.ds((2 * i + j) * P, P)], ps[j][:, k * P:(k + 1) * P],
                                                 m.a1[:, k, stream:stream + 1], m.mod_col[:, k, stream:stream + 1],
                                                 ALU.mult, ALU.add)
                    last.then_inc(moved, 1)
            leave(0, 1)
            with dve.Fori(1, NT // 2) as i:
                leave(i, 0)
            dve.wait_ge(moved, NT)


def project_qk(nc, m, sem, w):
    LAT, C0 = SEQ, SEQ
    IW = GRID_W + 2
    with ExitStack() as ctx:
        sb = lambda n, s: ctx.enter_context(nc.sbuf_tensor(n, s, F32))
        wt = sb("qk_w", [P, 2, KD, P])
        img = sb("qk_img", [P, 2, (GRID_H + 2) * IW])
        line = sb("qk_line", [P, 2, CTX + 2])
        acc = sb("qk_acc", [P, 2, T])
        ps = [ctx.enter_context(nc.psum_tensor(f"qk_ps{j}", [P, 3 * 512], F32)) for j in range(2)]
        w_loaded = [sem(f"qk_w_loaded{j}") for j in range(2)]
        made, left_m, left_g, tap, conv, done = (sem(f"qk_{n}") for n in
                                                 ("made", "left_m", "left_g", "tap", "conv", "done"))
        cleared = sem("qk_cleared")
        block = ctx.enter_context(nc.Block())
        wsrc = w["w_in"][0].rearrange("(k p) n -> p k n", p=P)
        PLAN = [(0, 0, 0), (0, 0, 1), (0, 1, (2, 4)), (1, 0, 4), (1, 0, 5), (1, 1, (6, 8))]

        def each(eng, body):
            for mixer, is_k, pairs in PLAN:
                if isinstance(pairs, int):
                    body(pairs, mixer, is_k, pairs)
                else:
                    with eng.Fori(*pairs) as i:
                        body(i, mixer, is_k, pairs[0])

        @block.sync
        def _(sp):
            def load(i, mixer, is_k, first):
                for j in range(2):
                    if first > 0:
                        sp.wait_ge(made, 2 * i + j - 1)
                    col = (2 * i + j) * P + (QG - 2 * COLS if mixer else QM)
                    sp.dma_start(wt[:, j, :, :], wsrc[:, :, bass.ds(col, P)]).then_inc(w_loaded[j], 16)
            each(sp, load)

        @block.gpsimd
        def _(pool):
            pool.memset(img[:, :, :], 0.0).then_inc(cleared, 1)
            pool.memset(line[:, :, :], 0.0).then_inc(cleared, 1)

        @block.tensor
        def _(pe):
            def multiply(i, mixer, is_k, first):
                for j in range(2):
                    pe.wait_ge(w_loaded[j], 16 * i + 16)
                    if first == 4:
                        pe.wait_ge(left_m, 8)
                    elif mixer:
                        pe.wait_ge(left_g, 2 * i + j - 9)
                    elif first > 0:
                        pe.wait_ge(left_m, 2 * i + j - 1)
                    parts = [(0, CTX, 512), (512, CTX + 512, 512)] + ([(C0, 0, CTX)] if is_k else [])
                    for at, t0, n in parts:
                        for k in range(KD):
                            last = pe.matmul(ps[j][:, at:at + n], wt[:, j, k, :], m.h_t[:, k, t0:t0 + n],
                                             start=(k == 0), stop=(k == KD - 1))
                    last.then_inc(made, 1)
            each(pe, multiply)

        @block.vector
        def _(dve):
            dve.wait_ge(cleared, 2)

            def convolve(i, mixer, is_k, first):
                if mixer:
                    return
                for j in range(2):
                    n = 2 * i + j
                    dve.wait_ge(made, n + 1)
                    v = img[:, j, :].rearrange("p (y x) -> p y x", x=IW)
                    dve.tensor_copy(v[:, 1:GRID_H + 1, 1:GRID_W + 1],
                                    ps[j][:, 0:LAT].rearrange("p (y x) -> p y x", x=GRID_W)).then_inc(tap, 1)
                    if is_k:
                        dve.tensor_copy(line[:, j, 1:CTX + 1], ps[j][:, C0:C0 + CTX]).then_inc(tap, 1)
                    before = 10 * n if not is_k else 40 + 14 * (n - 4)
                    dve.wait_ge(tap, before + 1 + is_k)
                    dve.sem_inc(left_m, 1)
                    if first > 0:
                        dve.wait_ge(done, n - 1)
                    out = acc[:, j, CTX:T].rearrange("p (y x) -> p y x", x=GRID_W)
                    taps = [(out, v[:, dy:dy + GRID_H, dx:dx + GRID_W], 3 * dy + dx, dy == 0 and dx == 0)
                            for dy in range(3) for dx in range(3)]
                    if is_k:
                        taps += [(acc[:, j, 0:CTX], line[:, j, dx:dx + CTX], 3 + dx, dx == 0) for dx in range(3)]
                    count = before + 1 + is_k
                    for o, src, tp, start in taps:
                        wcol = m.vec[:, bass.ds(n, 1), tp:tp + 1].rearrange("p a b -> p (a b)")
                        if start:
                            ins = dve.tensor_scalar(o, src, wcol, None, ALU.mult)
                        else:
                            dve.wait_ge(tap, count)
                            ins = dve.scalar_tensor_tensor(out=o, in0=src, scalar=wcol, in1=o,
                                                           op0=ALU.mult, op1=ALU.add)
                        ins.then_inc(tap, 1)
                        count = count + 1
                    dve.wait_ge(tap, count)
                    dve.sem_inc(conv, 1)
            each(dve, convolve)

        @block.scalar
        def _(act):
            def finish(i, mixer, is_k, first):
                for j in range(2):
                    n = 2 * i + j
                    ch = n - (4 if is_k else 0) - (8 if mixer else 0)
                    dst = [[m.qm, m.km], [m.qg, m.kg]][mixer][is_k]
                    if not mixer:
                        act.wait_ge(conv, n + 1)
                        t0, t1 = (0, T) if is_k else (CTX, T)
                        act.activation(dst[:, bass.ds(ch, 1), :].rearrange("p a t -> p (a t)"), acc[:, j, t0:t1],
                                       ACT.Silu, bias=m.vec[:, bass.ds(n, 1), CONV_B:CONV_B + 1]
                                       .rearrange("p a b -> p (a b)")).then_inc(done, 1)
                    else:
                        act.wait_ge(made, n + 1)
                        scale = 1.0 if is_k else float(DK) ** -0.5
                        off = CTX if is_k else 0
                        ins = act.activation(dst[:, bass.ds(ch, 1), off:off + SEQ].rearrange("p a t -> p (a t)"),
                                             ps[j][:, 0:LAT], ACT.Copy, scale=scale)
                        if is_k:
                            ins = act.activation(dst[:, bass.ds(ch, 1), 0:CTX].rearrange("p a t -> p (a t)"),
                                                 ps[j][:, C0:C0 + CTX], ACT.Copy)
                        ins.then_inc(left_g, 1)
            each(act, finish)
            act.wait_ge(done, 8)
            act.wait_ge(left_g, 8)


def project_small(nc, m, sem, w):
    with ExitStack() as ctx:
        sb = lambda n, s: ctx.enter_context(nc.sbuf_tensor(n, s, F32))
        wt = sb("small_w", [P, KD, SMALL])
        bias = sb("small_bias", [GATE_ROWS, 2])
        ps = ctx.enter_context(nc.psum_tensor("small_ps", [P, 3 * 512], F32))
        cleared, loaded, bias_loaded, made, done = (sem(f"small_{n}") for n in
                                                    ("cleared", "loaded", "bias_loaded", "made", "done"))
        block = ctx.enter_context(nc.Block())
        wsrc = w["w_in"][0].rearrange("(k p) n -> p k n", p=P)

        @block.gpsimd
        def _(pool):
            pool.memset(wt[:, :, :], 0.0).then_inc(cleared, 1)
            pool.memset(bias[:, :], 0.0).then_inc(cleared, 1)
            pool.memset(m.w2[:, :, :], 0.0).then_inc(cleared, 1)

        @block.sync
        def _(sp):
            sp.wait_ge(cleared, 3)
            for at, col, n in [(0, GATE, 4), (16, LR, RANK), (32, GATE + 8, 4), (48, LR + RANK, RANK),
                               (64, GATE + 4, 4), (96, GATE + 12, 4)]:
                sp.dma_start(wt[:, :, at:at + n], wsrc[:, :, col:col + n]).then_inc(loaded, 16)
            for row, c, at in [(0, 0, 0), (32, 0, 8), (0, 1, 4), (32, 1, 12)]:
                sp.dma_start(bias[row:row + 4, c:c + 1],
                             w["b_mgate"][0, at:at + 4].rearrange("(p a) -> p a", a=1)).then_inc(bias_loaded, 16)
            for d in range(2):
                sp.dma_start(m.w2[16:32, d, :], w["gla_w2"][0, d]).then_inc(bias_loaded, 16)

        @block.tensor
        def _(pe):
            pe.wait_ge(loaded, 16 * 6)
            for t0, n in [(0, 512), (512, 512), (1024, 256)]:
                for k in range(KD):
                    last = pe.matmul(ps[0:SMALL, t0:t0 + n], wt[:, k, :], m.h_t[:, k, t0:t0 + n],
                                     start=(k == 0), stop=(k == KD - 1))
            last.then_inc(made, 1)

        @block.scalar
        def _(act):
            act.wait_ge(made, 1)
            act.wait_ge(bias_loaded, 16 * 6)
            act.activation(m.gate_i[:, :], ps[0:GATE_ROWS, 0:T], ACT.Identity, bias=bias[:, 0:1]).then_inc(done, 1)
            act.activation(m.gate_f[:, :], ps[64:64 + GATE_ROWS, 0:T], ACT.Identity, bias=bias[:, 1:2]).then_inc(done, 1)
            act.wait_ge(done, 4)

        @block.vector
        def _(dve):
            dve.wait_ge(done, 2)
            for d in range(2):
                dve.tensor_copy(m.lr[:, d, :], ps[32 * d:32 * d + 32, 0:T]).then_inc(done, 1)


def split_h(nc, m, sem, w):
    with ExitStack() as ctx:
        split_hi, split_lo, stored = (sem(f"sh_{n}") for n in ("hi", "lo", "stored"))
        block = ctx.enter_context(nc.Block())

        @block.sync
        def _(sp):
            sp.dma_start(m.h_kept, m.h_t[:, :, :]).then_inc(stored, 16)
            sp.wait_ge(stored, 16)

        @block.scalar
        def _(act):
            for k in range(KD):
                act.activation(m.h_hi[:, k, :], m.h_t[:, k, :], ACT.Copy).then_inc(split_hi, 1)

        @block.vector
        def _(dve):
            for k in range(KD):
                dve.wait_ge(split_hi, k + 1)
                dve.tensor_tensor(m.h_lo[:, k, :], m.h_t[:, k, :], m.h_hi[:, k, :].bitcast(F32), ALU.subtract)\
                    .then_inc(split_lo, 1)
            dve.wait_ge(split_lo, KD)


def reload_h(nc, m, sem, w):
    with ExitStack() as ctx:
        loaded = sem("rh_loaded")
        block = ctx.enter_context(nc.Block())

        @block.sync
        def _(sp):
            sp.dma_start(m.h_t[:, :, :], m.h_kept).then_inc(loaded, 16)
            sp.wait_ge(loaded, 16)


def project_rows(nc, m, sem, w, name, tiles, plan):
    PS = 4
    with ExitStack() as ctx:
        sb = lambda n, s, dt=F32: ctx.enter_context(nc.sbuf_tensor(n, s, dt))
        raw = sb(f"{name}_w", [P, KD, COLS])
        w_hi = sb(f"{name}_w_hi", [P, 2, KD, COLS], F32R)
        w_lo = sb(f"{name}_w_lo", [P, 2, KD, COLS], F32R)
        stage = sb(f"{name}_stage", [P, PS, COLS])
        ps = [ctx.enter_context(nc.psum_tensor(f"{name}_ps{j}", [P, COLS], F32)) for j in range(PS)]
        w_loaded, hi_done, lo_done = (sem(f"{name}_{n}") for n in ("w_loaded", "hi_done", "lo_done"))
        stored = [sem(f"{name}_stored{j}") for j in range(PS)]
        made, moved = sem(f"{name}_made"), sem(f"{name}_moved")
        block = ctx.enter_context(nc.Block())
        wsrc = w["w_in"][0].rearrange("(k p) n -> p k n", p=P)
        nt = len(tiles)
        per = 2 * nt
        assert per % PS == 0
        rounds = sum(n for _, _, n, _, _ in plan)

        def each(eng, body):
            at = 0
            for col, step, n, func, dst in plan:
                if n == 1:
                    body(at, 0, col, step, func, dst)
                else:
                    with eng.Fori(0, n) as i:
                        body(at + i, i, col, step, func, dst)
                at += n

        @block.sync
        def _(sp):
            def load(r, i, col, step, func, dst):
                for j in range(2):
                    if j or not (isinstance(r, int) and r == 0):
                        sp.wait_ge(lo_done, 2 * r + j)
                    sp.dma_start(raw[:, :, :], wsrc[:, :, bass.ds(col + step * i + COLS * j, COLS)])\
                        .then_inc(w_loaded, 16)
            each(sp, load)

        @block.tensor
        def _(pe):
            def multiply(r, i, col, step, func, dst):
                for j in range(2):
                    pe.wait_ge(lo_done, 2 * r + j + 1)
                    for q, t in enumerate(tiles):
                        n = per * r + nt * j + q
                        s = (nt * j + q) % PS
                        if not (isinstance(n, int) and n < PS):
                            pe.wait_ge(moved, n - PS + 1)
                        for k in range(KD):
                            h_hi, h_lo = (h[:, k, t * P:(t + 1) * P] for h in (m.h_hi, m.h_lo))
                            pe.matmul(ps[s][:, :], h_hi, w_hi[:, j, k, :], start=(k == 0), stop=False)
                            pe.matmul(ps[s][:, :], h_hi, w_lo[:, j, k, :], start=False, stop=False)
                            last = pe.matmul(ps[s][:, :], h_lo, w_hi[:, j, k, :], start=False, stop=(k == KD - 1))
                        last.then_inc(made, 1)
            each(pe, multiply)

        @block.vector
        def _(dve):
            def split(r, i, col, step, func, dst):
                for j in range(2):
                    dve.wait_ge(w_loaded, 32 * r + 16 * j + 16)
                    if not (isinstance(r, int) and r == 0):
                        dve.wait_ge(made, per * r - per + nt * (j + 1))
                    dve.tensor_copy(w_hi[:, j, :, :], raw[:, :, :]).then_inc(hi_done, 1)
                    dve.wait_ge(hi_done, 2 * r + j + 1)
                    dve.tensor_tensor(w_lo[:, j, :, :], raw[:, :, :], w_hi[:, j, :, :].bitcast(F32), ALU.subtract)\
                        .then_inc(lo_done, 1)
            each(dve, split)

        @block.scalar
        def _(act):
            def move(r, i, col, step, func, dst):
                for j in range(2):
                    for q in range(nt):
                        n = per * r + nt * j + q
                        s = (nt * j + q) % PS
                        act.wait_ge(made, n + 1)
                        if not (isinstance(n, int) and n < PS):
                            act.wait_ge(stored[s], 16 * (r * (per // PS) + (nt * j + q) // PS))
                        act.activation(stage[:, s, :], ps[s][:, :], func).then_inc(moved, 1)
            each(act, move)

        @block.gpsimd
        def _(pool):
            def store(r, i, col, step, func, dst):
                for j in range(2):
                    for q in range(nt):
                        n = per * r + nt * j + q
                        s = (nt * j + q) % PS
                        pool.wait_ge(moved, n + 1)
                        rows = dst[bass.ds(i, 1), q * P:(q + 1) * P, j * COLS:(j + 1) * COLS]
                        pool.dma_start(rows.rearrange("a p n -> p (a n)"), stage[:, s, :]).then_inc(stored[s], 16)
            each(pool, store)
            for s in range(PS):
                pool.wait_ge(stored[s], 16 * (rounds * per // PS))


def project_values(nc, m, sem, w):
    project_rows(nc, m, sem, w, "val", list(range(NT)), [(VM, 0, 1, ACT.Copy, m.vals[0:1]), (VG, 0, 1, ACT.Copy, m.vals[1:2])])


def project_gates(nc, m, sem, w):
    project_rows(nc, m, sem, w, "og", list(range(NC, NT)),
                 [(OM, 0, 1, ACT.Sigmoid, m.gates[0:1]), (RG, 0, 1, ACT.Silu, m.gates[1:2]),
                  (MGM, MGG - MGM, 2, ACT.Sigmoid, m.gates[2:4])])


def gate_rows(nc, m, sem, w):
    R = GATE_ROWS
    with ExitStack() as ctx:
        sb = lambda n, s: ctx.enter_context(nc.sbuf_tensor(n, s, F32))
        lf = sb("gr_logf", [R, T])
        tmp = sb("gr_tmp", [R, T])
        b = sb("gr_b", [R, T])
        mx = sb("gr_max", [R, T])
        wsrc = sb("gr_wstate", [R, T])
        emt = sb("gr_emt", [R, T])
        prev = sb("gr_prev", [R, NT])
        end = sb("gr_end", [R, NT])
        dec = sb("gr_dec", [R, NT])
        cols = [ctx.enter_context(nc.psum_tensor(f"gr_cols{q}", [P, NT, GATE_ROWS], F32)) for q in range(3)]
        decps = ctx.enter_context(nc.psum_tensor("gr_decps", [P, 2 * HEADS, NT], F32))
        step, actd, turned, moved = (sem(f"gr_{n}") for n in ("step", "act_step", "turned", "moved"))
        block = ctx.enter_context(nc.Block())
        FW, BW = slice(0, HEADS), slice(32, 32 + HEADS)
        chunks = lambda a: a[:, :].rearrange("p (c t) -> p c t", t=P)
        across = lambda a: a[:, :].rearrange("p (c a) -> p c a", a=1).to_broadcast([R, NT, P])

        @block.scalar
        def _(act):
            n = [0]

            def then(ins):
                n[0] += 1
                ins.then_inc(actd, 1)
                act.wait_ge(actd, n[0])
            then(act.activation(tmp[:, :], m.gate_f[:, :], ACT.Abs))
            then(act.activation(tmp[:, :], tmp[:, :], ACT.Exp, scale=-1.0))
            then(act.activation(tmp[:, :], tmp[:, :], ACT.Ln, bias=1.0))
            act.wait_ge(step, 13)
            then(act.activation(emt[:, :], mx[:, :], ACT.Exp, scale=-1.0))
            act.wait_ge(step, 18)
            then(act.activation(m.w_inter[:, :], m.w_inter[:, :], ACT.Exp))
            then(act.activation(wsrc[:, :], wsrc[:, :], ACT.Exp))
            then(act.activation(dec[:, :], dec[:, :], ACT.Exp))

        @block.vector
        def _(dve):
            n = [0]

            def then(ins):
                n[0] += 1
                ins.then_inc(step, 1)
                dve.wait_ge(step, n[0])
            then(dve.memset(prev[:, :], NEG_BIG))
            then(dve.memset(mx[:, :], 0.0))
            dve.wait_ge(actd, 3)
            then(dve.scalar_tensor_tensor(out=lf[:, :], in0=m.gate_f[:, :], scalar=0.0, in1=tmp[:, :],
                                          op0=ALU.min, op1=ALU.subtract))
            then(dve.tensor_tensor_scan(mx[FW, :], lf[FW, :], m.gate_i[FW, :], NEG_BIG, ALU.add, ALU.max))
            then(dve.tensor_tensor_scan(mx[BW, CTX - 1::-1], lf[BW, CTX - 1::-1], m.gate_i[BW, CTX - 1::-1],
                                        NEG_BIG, ALU.add, ALU.max))
            then(dve.tensor_tensor_scan(mx[BW, T - 1:CTX - 1:-1], lf[BW, T - 1:CTX - 1:-1],
                                        m.gate_i[BW, T - 1:CTX - 1:-1], mx[BW, 0:1], ALU.add, ALU.max))
            then(dve.memset(b[:, :], 0.0))
            for half in (slice(0, T // 2), slice(T // 2, T)):
                bh, lh = b[:, half], lf[:, half]
                dve.tensor_tensor_scan(bh[FW], m.restart[FW, 0, :], lh[FW], 0.0, ALU.mult, ALU.add)\
                    .then_inc(moved, 1)
                dve.tensor_tensor_scan(bh[BW, ::-1], m.restart[BW, 1, ::-1], lh[BW, ::-1], 0.0,
                                       ALU.mult, ALU.add).then_inc(moved, 1)
            dve.wait_ge(moved, 4)
            mv = chunks(mx)
            then(dve.tensor_copy(prev[FW, 1:NT], mv[FW, 0:NT - 1, P - 1]))
            then(dve.tensor_copy(prev[BW, 0:NC - 1], mv[BW, 1:NC, 0]))
            then(dve.tensor_copy(prev[BW, NT - 1:NT], mv[BW, 0:1, 0]))
            then(dve.tensor_copy(prev[BW, NC:NT - 1], mv[BW, NC + 1:NT, 0]))
            then(dve.tensor_tensor(m.gate_g[:, :], m.gate_i[:, :], b[:, :], ALU.subtract))
            then(dve.tensor_tensor(m.neg_m[:, :], b[:, :], mx[:, :], ALU.subtract))
            then(dve.tensor_tensor(chunks(m.w_inter), chunks(m.neg_m), across(prev), ALU.add))
            then(dve.memset(end[:, :], 0.0))
            nv = chunks(m.neg_m)
            then(dve.tensor_copy(end[FW, :], nv[FW, :, P - 1]))
            dve.tensor_copy(end[BW, :], nv[BW, :, 0]).then_inc(moved, 1)
            dve.wait_ge(moved, 5)
            dve.tensor_tensor(chunks(wsrc), chunks(m.gate_g), across(end), ALU.add).then_inc(step, 1)
            dve.tensor_tensor(dec[:, :], end[:, :], prev[:, :], ALU.add).then_inc(step, 1)
            dve.wait_ge(turned, 1)
            dve.tensor_copy(m.g_col[:, :, :], cols[0][:, :, :]).then_inc(moved, 1)
            dve.tensor_copy(m.ws_col[:, :, :], cols[1][:, :, :]).then_inc(moved, 1)
            dve.tensor_copy(m.emt_col[:, :, :], cols[2][:, :, :]).then_inc(moved, 1)
            dve.tensor_copy(m.dec_all[:, :, :], decps[:, :, :]).then_inc(moved, 1)
            dve.wait_ge(moved, 9)

        @block.tensor
        def _(pe):
            pe.wait_ge(actd, 7)
            pe.wait_ge(step, 18)
            for q, src in enumerate((m.gate_g, wsrc, emt)):
                for c in range(NT):
                    pe.transpose(cols[q][:, c, :], src[:, c * P:(c + 1) * P], m.ident[0:R, 0:R])
            for r in range(2 * HEADS):
                last = pe.matmul(decps[:, r, :], m.row_of[:, r, :], dec[:, :], start=True, stop=True)
            last.then_inc(turned, 1)


def mlstm_scan(nc, m, sem, w):
    SC = float(DK) ** -0.5
    with ExitStack() as ctx:
        sb = lambda n, s: ctx.enter_context(nc.sbuf_tensor(n, s, F32))
        bank = lambda n, k=1: ctx.enter_context(nc.psum_tensor(n, [P, k * 512], F32))
        v = sb("ml_v", [P, 2, D])
        ks = sb("ml_k", [P, 2, HEADS, P])
        expo = sb("ml_expo", [P, 2, HEADS, P])
        wt = sb("ml_wt", [P, 2, HEADS, P])
        qi = sb("ml_qi", [P, 2, HEADS, P])
        kw = sb("ml_kw", [P, 2, HEADS, P])
        den = sb("ml_den", [P, 2, HEADS])
        cmat = sb("ml_c", [P, 2, D])
        nvec = sb("ml_n", [P, 2, HEADS])
        hm = sb("ml_h", [P, NL, D])
        s_ps, m_ps, t_ps = bank("ml_s_ps"), bank("ml_m_ps"), bank("ml_t_ps")
        num_ps, st_ps, small_ps = bank("ml_num_ps", 2), bank("ml_st_ps", 2), bank("ml_small_ps")
        v_loaded = [sem(f"ml_v_loaded{d}") for d in range(2)]
        (cleared, k_ready, scores, maxes, inters, keys_t, expo_ready, masked, exp_ready, w_ready, qi_ready,
         kw_ready, out_made, state_made, c_ready, h_added, den_step, n_step, stored) = (
            sem(f"ml_{n}") for n in (
                "cleared", "k_ready", "scores", "maxes", "inters", "keys_t", "expo_ready", "masked", "exp_ready",
                "w_ready", "qi_ready", "kw_ready", "out_made", "state_made", "c_ready", "h_added", "den_step",
                "n_step", "stored"))
        mask_begun = sem("ml_mask_begun")
        block = ctx.enter_context(nc.Block())
        heads = lambda ap: ap.rearrange("p (h n) -> p h n", h=HEADS)

        def steps(eng, body):
            for d in range(2):
                body(d, 0, (0, NC - 1)[d], d, False)
            for d in range(2):
                body(2 + d, 1, (1, NC - 2)[d], d, False)
            with eng.Fori(NC, NT) as i:
                back = i * -1 + (NT - 1 + NC)
                for d in range(2):
                    body(2 * i + d, i, back if d else i, d, True)

        assert NC == 2

        @block.sync
        def _(sp):
            def load(u, i, c, d, out):
                if not (isinstance(i, int) and i == 0):
                    sp.wait_ge(state_made, u - 1)
                sp.dma_start(v[:, d, :], m.vals[0, bass.ds(c * P, P), :]).then_inc(v_loaded[d], 16)
            steps(sp, load)
            sp.wait_ge(h_added, 2 * NL)
            sp.dma_start(m.hm.rearrange("(c p) n -> p c n", p=P), hm[:, :, :]).then_inc(stored, 16)
            sp.wait_ge(stored, 16)

        @block.gpsimd
        def _(pool):
            pool.memset(cmat[:, :, :], 0.0).then_inc(cleared, 1)
            pool.memset(nvec[:, :, :], 0.0).then_inc(cleared, 1)
            pool.memset(hm[:, :, :], 0.0).then_inc(cleared, 1)

            def mask(u, i, c, d, out):
                if out:
                    n = u - 2 * NC
                    pool.wait_ge(expo_ready, n + 1)
                    pool.sem_inc(mask_begun, 1)
                    sign = 1 - 2 * d
                    pool.affine_select(out=expo[:, d, :, :], in_=expo[:, d, :, :], compare_op=ALU.is_ge,
                                       fill=NEG_BIG, base=0, pattern=[[0, HEADS], [sign, P]],
                                       channel_multiplier=-sign).then_inc(masked, 1)
            steps(pool, mask)

        @block.scalar
        def _(act):
            def stage(u, i, c, d, out):
                if not (isinstance(i, int) and i == 0):
                    act.wait_ge(keys_t, u - 1)
                act.activation(ks[:, d, :, :], m.km[:, :, bass.ds(c * P, P)], ACT.Copy, scale=SC).then_inc(k_ready, 1)
                if out:
                    n = u - 2 * NC
                    act.wait_ge(masked, n + 1)
                    act.activation(expo[:, d, :, :], expo[:, d, :, :], ACT.Exp).then_inc(exp_ready, 1)
            steps(act, stage)

        @block.tensor
        def _(pe):
            def chunk(u, i, c, d, out):
                n = u - 2 * NC
                after_first = not (isinstance(u, int) and u == 0)
                tok = bass.ds(c * P, P)
                if out:
                    pe.wait_ge(k_ready, u + 1)
                    if d == 0:
                        pe.wait_ge(c_ready, u)
                    else:
                        pe.wait_ge(w_ready, n)
                    for h in range(HEADS):
                        last = pe.matmul(s_ps[:, h * P:(h + 1) * P], ks[:, d, h, :],
                                         m.qm[:, h, bass.ds(c * P - CTX, P)], start=True, stop=True)
                    last.then_inc(scores, 1)
                    if d == 1:
                        pe.wait_ge(expo_ready, n)
                    for h in range(HEADS):
                        last = pe.matmul(m_ps[:, h * P:(h + 1) * P], m.row_of[:, HEADS * d + h, :],
                                         m.neg_m[:, tok], start=True, stop=True)
                    last.then_inc(maxes, 1)
                    pe.wait_ge(kw_ready, u)
                    if d == 1:
                        pe.wait_ge(den_step, 3 * n - 1)
                    for h in range(HEADS):
                        last = pe.matmul(t_ps[:, h * P:(h + 1) * P], m.row_of[:, HEADS * d + h, :],
                                         m.w_inter[:, tok], start=True, stop=True)
                    last.then_inc(inters, 1)
                    pe.wait_ge(qi_ready, n + 1)
                else:
                    pe.wait_ge(k_ready, u + 1)
                    if after_first:
                        pe.wait_ge(kw_ready, u)
                for h in range(HEADS):
                    last = pe.transpose(t_ps[:, h * P:(h + 1) * P], ks[:, d, h, :], m.ident[:, :])
                last.then_inc(keys_t, 1)
                pe.wait_ge(v_loaded[d], 16 * i + 16)
                if after_first:
                    pe.wait_ge(c_ready, u)
                else:
                    pe.wait_ge(cleared, 3)
                if out:
                    pe.wait_ge(w_ready, n + 1)
                    pe.wait_ge(kw_ready, u + 1)
                    for h in range(HEADS):
                        o = num_ps[:, h * DV:(h + 1) * DV]
                        pe.matmul(o, wt[:, d, h, :], v[:, d, h * DV:(h + 1) * DV], start=True, stop=False)
                        pe.matmul(o, qi[:, d, h, :], cmat[:, d, h * DV:(h + 1) * DV], start=False, stop=True)
                    for h in range(HEADS):
                        o = t_ps[:, h:h + 1]
                        pe.matmul(o, wt[:, d, h, :], m.ones[:, 0:1], start=True, stop=False)
                        last = pe.matmul(o, qi[:, d, h, :], nvec[:, d, h:h + 1], start=False, stop=True)
                    last.then_inc(out_made, 1)
                pe.wait_ge(kw_ready, u + 1)
                for h in range(HEADS):
                    pe.matmul(st_ps[:, h * DV:(h + 1) * DV], kw[:, d, h, :], v[:, d, h * DV:(h + 1) * DV],
                              start=True, stop=True)
                for h in range(HEADS):
                    last = pe.matmul(small_ps[:, 8 + h:9 + h], kw[:, d, h, :], m.ones[:, 0:1], start=True, stop=True)
                last.then_inc(state_made, 1)
            steps(pe, chunk)

        @block.vector
        def _(dve):
            dve.wait_ge(cleared, 3)

            def chunk(u, i, c, d, out):
                n = u - 2 * NC
                gcol = slice(32 * d, 32 * d + HEADS)
                ci = bass.ds(c, 1)
                per_key = lambda a, width: a[:, ci, gcol].rearrange("p a (h n) -> p (a h) n", n=1)\
                    .to_broadcast([P, HEADS, width])
                if out:
                    dve.wait_ge(maxes, n + 1)
                    dve.tensor_tensor(expo[:, d, :, :], heads(m_ps[:, :]), per_key(m.g_col, P), ALU.add)\
                        .then_inc(expo_ready, 1)
                    dve.wait_ge(inters, n + 1)
                    dve.tensor_tensor(qi[:, d, :, :], m.qm[:, :, bass.ds(c * P - CTX, P)], heads(t_ps[:, :]),
                                      ALU.mult).then_inc(qi_ready, 1)
                dve.wait_ge(keys_t, u + 1)
                dve.tensor_tensor(kw[:, d, :, :], heads(t_ps[:, :]), per_key(m.ws_col, P), ALU.mult)\
                    .then_inc(kw_ready, 1)
                if out:
                    dve.wait_ge(exp_ready, n + 1)
                    dve.wait_ge(scores, n + 1)
                    dve.tensor_tensor(wt[:, d, :, :], heads(s_ps[:, :]), expo[:, d, :, :], ALU.mult)\
                        .then_inc(w_ready, 1)
                    dve.wait_ge(out_made, n + 1)
                    dn = den[:, d, :]
                    dve.scalar_tensor_tensor(out=dn, in0=t_ps[:, 0:HEADS], scalar=-1.0,
                                             in1=m.emt_col[:, ci, gcol].rearrange("p a h -> p (a h)"),
                                             op0=ALU.mult, op1=ALU.max).then_inc(den_step, 1)
                    dve.wait_ge(den_step, 3 * n + 1)
                    dve.tensor_tensor(dn, t_ps[:, 0:HEADS], dn, ALU.max).then_inc(den_step, 1)
                    dve.wait_ge(den_step, 3 * n + 2)
                    dve.reciprocal(dn, dn).then_inc(den_step, 1)
                    dve.wait_ge(den_step, 3 * n + 3)
                    tile = bass.ds(c - NC, 1)
                    for h in range(HEADS):
                        o = hm[:, tile, h * DV:(h + 1) * DV].rearrange("p a n -> p (a n)")
                        last = dve.scalar_tensor_tensor(out=o, in0=num_ps[:, h * DV:(h + 1) * DV],
                                                        scalar=dn[:, h:h + 1], in1=o, op0=ALU.mult, op1=ALU.add)
                    last.then_inc(h_added, 1)
                dve.wait_ge(state_made, u + 1)
                dec = lambda h0, h1: m.dec_all[:, HEADS * d + h0:HEADS * d + h1, ci].rearrange("p h a -> p (h a)")
                dve.tensor_tensor(nvec[:, d, :], nvec[:, d, :], dec(0, HEADS), ALU.mult).then_inc(n_step, 1)
                for h in range(HEADS):
                    o = cmat[:, d, h * DV:(h + 1) * DV]
                    last = dve.scalar_tensor_tensor(out=o, in0=o, scalar=dec(h, h + 1),
                                                    in1=st_ps[:, h * DV:(h + 1) * DV], op0=ALU.mult, op1=ALU.add)
                dve.wait_ge(n_step, u + 1)
                dve.tensor_tensor(nvec[:, d, :], nvec[:, d, :], small_ps[:, 8:8 + HEADS], ALU.add).then_inc(c_ready, 1)
            steps(dve, chunk)


def gla_scan(nc, m, sem, w):
    H = HEADS
    Q_IN, K_OUT = LEVELS, LEVELS + 1
    with ExitStack() as ctx:
        sb = lambda n, s: ctx.enter_context(nc.sbuf_tensor(n, s, F32))
        bank = lambda n, k=1: ctx.enter_context(nc.psum_tensor(n, [P, k * 512], F32))
        v = sb("gl_v", [P, 2, D])
        z = sb("gl_z", [P, 2, H * P])
        l1p = sb("gl_log1p", [P, 2, H * P])
        b = sb("gl_b", [P, 2, H * P])
        ex = sb("gl_exp", [P, LEVELS + 2, H * P])
        ks = sb("gl_k", [P, 2, H, P])
        kl = sb("gl_k_level", [P, 2, LEVELS, H * P])
        ql = sb("gl_q_level", [P, LEVELS, H * P // 2])
        qe = sb("gl_q_in", [P, H, P])
        ke = sb("gl_k_out", [P, H, P])
        ket = sb("gl_k_out_t", [P, H, P])
        at = sb("gl_scores", [P, H * P])
        smat = sb("gl_s", [P, 2, D])
        og = sb("gl_o", [P, NL, D])
        z_ps, dg_ps = bank("gl_z_ps"), bank("gl_dg_ps")
        lv_ps = [bank(f"gl_lv_ps{q}") for q in range(2)]
        o_ps, st_ps = bank("gl_o_ps", 2), bank("gl_st_ps", 2)
        v_loaded = [sem(f"gl_v_loaded{d}") for d in range(2)]
        (cleared, k_ready, z_made, z_ready, z_abs, log_ready, la_ready, b_ready, ex_in, ex_ready, qk_ready,
         qe_ready, ke_ready, dg_made, dg_left, lv_made, lv_left, turned, ket_ready, o_made, o_added, state_made,
         s_ready, stored) = (
            sem(f"gl_{n}") for n in (
                "cleared", "k_ready", "z_made", "z_ready", "z_abs", "log_ready", "la_ready", "b_ready", "ex_in",
                "ex_ready", "qk_ready", "qe_ready", "ke_ready", "dg_made", "dg_left", "lv_made", "lv_left",
                "turned", "ket_ready", "o_made", "o_added", "state_made", "s_ready", "stored"))
        lv_seen = sem("gl_lv_seen")
        block = ctx.enter_context(nc.Block())
        heads = lambda ap: ap.rearrange("p (h n) -> p h n", h=H)

        def steps(eng, body):
            for d in range(2):
                body(d, 0, (0, NC - 1)[d], d, False)
            for d in range(2):
                body(2 + d, 1, (1, NC - 2)[d], d, False)
            with eng.Fori(NC, NT) as i:
                back = i * -1 + (NT - 1 + NC)
                for d in range(2):
                    body(2 * i + d, i, back if d else i, d, True)

        @block.sync
        def _(sp):
            def load(u, i, c, d, out):
                if not (isinstance(i, int) and i == 0):
                    sp.wait_ge(state_made, u - 1)
                sp.dma_start(v[:, d, :], m.vals[1, bass.ds(c * P, P), :]).then_inc(v_loaded[d], 16)
            steps(sp, load)
            sp.wait_ge(o_added, 2 * NL)
            sp.dma_start(m.og.rearrange("(c p) n -> p c n", p=P), og[:, :, :]).then_inc(stored, 16)
            sp.wait_ge(stored, 16)

        @block.gpsimd
        def _(pool):
            pool.memset(smat[:, :, :], 0.0).then_inc(cleared, 1)
            pool.memset(og[:, :, :], 0.0).then_inc(cleared, 1)
            pool.memset(kl[:, :, :, :], 0.0).then_inc(cleared, 1)

        def halves(ap, l):
            v4 = ap.rearrange("p (j two i) -> p two j i", two=2, i=1 << l)
            return v4[:, 0], v4[:, 1]

        @block.scalar
        def _(act):
            def chunk(u, i, c, d, out):
                first = isinstance(u, int) and u == 0
                act.wait_ge(z_ready, u + 1)
                act.activation(l1p[:, d, :], z[:, d, :], ACT.Abs).then_inc(z_abs, 1)
                act.wait_ge(z_abs, 2 * u + 1)
                act.activation(l1p[:, d, :], l1p[:, d, :], ACT.Exp, scale=-1.0).then_inc(z_abs, 1)
                act.wait_ge(z_abs, 2 * u + 2)
                act.activation(l1p[:, d, :], l1p[:, d, :], ACT.Ln, bias=1.0).then_inc(log_ready, 1)
                if out:
                    if d == 1:
                        act.wait_ge(dg_made, u - 2 * NC)
                    act.activation(ks[:, d, :, :], m.kg[:, :, bass.ds(c * P, P)], ACT.Copy).then_inc(k_ready, 1)
                act.wait_ge(ex_in, u + 1)
                lo = 0 if out else Q_IN
                act.activation(ex[:, lo:, :], ex[:, lo:, :], ACT.Exp, scale=1.0 / TAU).then_inc(ex_ready, 1)
                act.wait_ge(turned, u + 1)
                if not first:
                    act.wait_ge(state_made, u)
                act.activation(ket[:, :, :], heads(z_ps[:, :]), ACT.Copy).then_inc(ket_ready, 1)
            steps(act, chunk)

        @block.tensor
        def _(pe):
            pe.wait_ge(cleared, 3)

            def chunk(u, i, c, d, out):
                n = u - 2 * NC
                first = isinstance(u, int) and u == 0
                tok = bass.ds(c * P, P)
                if not first:
                    pe.wait_ge(ket_ready, u)
                for h in range(H):
                    last = pe.matmul(z_ps[:, h * P:(h + 1) * P], m.w2[:, d, h * DK:(h + 1) * DK],
                                     m.lr[:, d, tok], start=True, stop=True)
                last.then_inc(z_made, 1)
                if out:
                    pe.wait_ge(k_ready, n + 1)
                    if d == 1:
                        pe.wait_ge(dg_left, n)
                    else:
                        pe.wait_ge(s_ready, u)
                    for h in range(H):
                        last = pe.matmul(dg_ps[:, h * P:(h + 1) * P], ks[:, d, h, :],
                                         m.qg[:, h, bass.ds(c * P - CTX, P)], start=True, stop=True)
                    last.then_inc(dg_made, 1)
                    for l in range(LEVELS):
                        pe.wait_ge(qk_ready, LEVELS * n + l + 1)
                        if l >= 2:
                            pe.wait_ge(lv_left, LEVELS * n + l - 1)
                        elif d == 1:
                            pe.wait_ge(lv_left, LEVELS * n)
                        for h in range(H):
                            last = pe.matmul(lv_ps[l % 2][:, h * P // 2:(h + 1) * P // 2],
                                             kl[:, d, l, h * P:(h + 1) * P],
                                             ql[:, l, h * P // 2:(h + 1) * P // 2], start=True, stop=True)
                        last.then_inc(lv_made, 1)
                pe.wait_ge(ke_ready, u + 1)
                pe.wait_ge(z_ready, u + 1)
                for h in range(H):
                    last = pe.transpose(z_ps[:, h * P:(h + 1) * P], ke[:, h, :], m.ident[:, :])
                last.then_inc(turned, 1)
                pe.wait_ge(v_loaded[d], 16 * i + 16)
                if out:
                    pe.wait_ge(qe_ready, n + 1)
                    pe.wait_ge(lv_left, LEVELS * n + LEVELS)
                    pe.wait_ge(s_ready, u)
                    for h in range(H):
                        o = o_ps[:, h * DV:(h + 1) * DV]
                        pe.matmul(o, at[:, h * P:(h + 1) * P], v[:, d, h * DV:(h + 1) * DV], start=True, stop=False)
                        last = pe.matmul(o, qe[:, h, :], smat[:, d, h * DV:(h + 1) * DV], start=False, stop=True)
                    last.then_inc(o_made, 1)
                elif not first:
                    pe.wait_ge(s_ready, u)
                pe.wait_ge(ket_ready, u + 1)
                for h in range(H):
                    last = pe.matmul(st_ps[:, h * DV:(h + 1) * DV], ket[:, h, :], v[:, d, h * DV:(h + 1) * DV],
                                     start=True, stop=True)
                last.then_inc(state_made, 1)
            steps(pe, chunk)

        @block.vector
        def _(dve):
            dve.wait_ge(cleared, 3)

            def chunk(u, i, c, d, out):
                n = u - 2 * NC
                first = isinstance(u, int) and u == 0
                end = P - 1 if d == 0 else 0
                dve.wait_ge(z_made, u + 1)
                dve.tensor_tensor(heads(z[:, d, :]), heads(z_ps[:, :]),
                                  m.vec[:, HEADS * d:HEADS * d + HEADS, B2:B2 + 1].to_broadcast([P, H, P]), ALU.add)\
                    .then_inc(z_ready, 1)
                dve.wait_ge(log_ready, u + 1)
                dve.scalar_tensor_tensor(out=z[:, d, :], in0=z[:, d, :], scalar=0.0, in1=l1p[:, d, :],
                                         op0=ALU.min, op1=ALU.subtract).then_inc(la_ready, 1)
                dve.wait_ge(la_ready, u + 1)
                back = slice(None, None, -1) if d else slice(None)
                dve.tensor_tensor_scan(b[:, d, back], m.restart[:, d, 0:H * P][:, back], z[:, d, back], 0.0,
                                       ALU.mult, ALU.add).then_inc(b_ready, 1)
                dve.wait_ge(b_ready, u + 1)
                bd = b[:, d, :]
                if out:
                    for l in range(LEVELS):
                        hl = 1 << l
                        early, late = halves(bd, l)
                        e_early, e_late = halves(ex[:, l, :], l)
                        shape = [P, H * P // 2 // hl, hl]
                        if d == 0:
                            mid = early[:, :, hl - 1:hl].to_broadcast(shape)
                            dve.tensor_tensor(e_late, late, mid, ALU.subtract)
                            dve.tensor_tensor(e_early, mid, early, ALU.subtract)
                        else:
                            mid = late[:, :, 0:1].to_broadcast(shape)
                            dve.tensor_tensor(e_early, early, mid, ALU.subtract)
                            dve.tensor_tensor(e_late, mid, late, ALU.subtract)
                dve.tensor_copy(ex[:, Q_IN, :], bd)
                dve.tensor_tensor(heads(ex[:, K_OUT, :]), heads(bd)[:, :, end:end + 1].to_broadcast([P, H, P]),
                                  heads(bd), ALU.subtract).then_inc(ex_in, 1)
                dve.wait_ge(ex_ready, u + 1)
                kc = m.kg[:, :, bass.ds(c * P, P)]
                if not first:
                    dve.wait_ge(turned, u)
                dve.tensor_tensor(ke[:, :, :], kc, heads(ex[:, K_OUT, :]), ALU.mult).then_inc(ke_ready, 1)
                if out:
                    qc = m.qg[:, :, bass.ds(c * P - CTX, P)]
                    for l in range(LEVELS):
                        hl = 1 << l
                        q_half, k_half = (1, 0) if d == 0 else (0, 1)
                        parts = lambda ap: ap.rearrange("p h (j two i) -> p two h j i", two=2, i=hl)
                        e = parts(heads(ex[:, l, :]))
                        dve.tensor_tensor(ql[:, l, :].rearrange("p (h j i) -> p h j i", h=H, i=hl),
                                          parts(qc)[:, q_half], e[:, q_half], ALU.mult)
                        dve.tensor_tensor(parts(heads(kl[:, d, l, :]))[:, k_half], parts(kc)[:, k_half],
                                          e[:, k_half], ALU.mult).then_inc(qk_ready, 1)
                    dve.tensor_tensor(qe[:, :, :], qc, heads(ex[:, Q_IN, :]), ALU.mult).then_inc(qe_ready, 1)
                    dve.wait_ge(dg_made, n + 1)
                    dve.tensor_tensor(heads(at[:, :]), heads(dg_ps[:, :]),
                                      m.ident[:, :].rearrange("p (a n) -> p a n", a=1).to_broadcast([P, H, P]),
                                      ALU.mult).then_inc(dg_left, 1)
                    dve.wait_ge(dg_left, n + 1)
                    for l in range(LEVELS):
                        hl = 1 << l
                        dve.wait_ge(lv_made, LEVELS * n + l + 1)
                        if l:
                            dve.wait_ge(lv_left, LEVELS * n + l)
                        dve.sem_inc(lv_seen, 1)
                        sel = halves(at[:, :], l)[1 - d]
                        mask = m.level_mask[:, d, l, :].rearrange("p (j i) -> p j i", i=hl)
                        data = lv_ps[l % 2][:, 0:H * P // 2].rearrange("p (j i) -> p j i", i=hl)
                        dve.copy_predicated(sel, mask, data).then_inc(lv_left, 1)
                    dve.wait_ge(o_made, n + 1)
                    o = og[:, bass.ds(c - NC, 1), :].rearrange("p a n -> p (a n)")
                    dve.tensor_tensor(o, o_ps[:, :], o, ALU.add).then_inc(o_added, 1)
                dve.wait_ge(state_made, u + 1)
                for h in range(H):
                    o = smat[:, d, h * DV:(h + 1) * DV]
                    last = dve.scalar_tensor_tensor(out=o, in0=o, scalar=ex[:, Q_IN, h * P + end:h * P + end + 1],
                                                    in1=st_ps[:, h * DV:(h + 1) * DV], op0=ALU.mult, op1=ALU.add)
                last.then_inc(s_ready, 1)
            steps(dve, chunk)


def mix_out(nc, m, sem, w):
    with ExitStack() as ctx:
        sb = lambda n, s: ctx.enter_context(nc.sbuf_tensor(n, s, F32))
        bank = lambda n, k=1: ctx.enter_context(nc.psum_tensor(n, [P, k * 512], F32))
        wp = sb("mo_w_proj", [P, 2, KD, D])
        wo = sb("mo_w_out", [P, KD, D])
        wr = sb("mo_w_router", [P, KD, GROUPS + EXPERTS])
        hin = sb("mo_in", [P, 2, 4, D])
        mg = sb("mo_merge", [P, 2, D])
        xt = sb("mo_x", [P, D])
        yt = sb("mo_y_t", [P, 2, KD, P])
        y = sb("mo_y", [P, 2, D])
        yg = sb("mo_yg", [P, D])
        x1 = sb("mo_x1", [P, 2, D])
        h2 = sb("mo_h2", [P, D])
        sq = sb("mo_sq", [P, D])
        sqh = sb("mo_sqh", [P, 2 * HEADS, DV])
        spread = sb("mo_spread", [P, 3, D])
        st = sb("mo_stat", [P, 2, 3, 2 * HEADS])
        st2 = sb("mo_stat2", [P, 3])
        tp_m, tp_g, p_m, p_g = (bank(f"mo_{n}", 2) for n in ("tp_m", "tp_g", "p_m", "p_g"))
        s = {name: sem(f"mo_{name}") for name in ("w_loaded", "mg_loaded", "x_loaded", "spread_loaded", "a2", "stat", "rstd", "y_ready", "t_m",
                     "t_g", "ym_t", "yg_t", "made_m", "made_g", "y_part", "yg_part", "y_done", "t_y", "y_t",
                     "made_out", "x1_part", "x1_done", "stat2", "xn", "h2_part", "h2_done", "t_h", "h_t", "made_r",
                     "logits", "x1_stored", "h2_stored", "h2_free")}
        in_loaded = [sem(f"mo_in_loaded{j}") for j in range(2)]
        block = ctx.enter_context(nc.Block())
        kmaj = lambda ap: ap.rearrange("p (k n) -> p k n", k=KD)

        def pipeline(eng, *stages):
            def step(n):
                for f, lag in stages:
                    t = n - lag
                    if 0 <= t < NL:
                        f(t, t % 2, t // 2, t == 0, t == NL - 1)
            for n in range(4):
                step(n)
            with eng.Fori(2, NL // 2 - 1) as i:
                for j in range(2):
                    for f, lag in stages:
                        f(2 * i + (j - lag), (j - lag) % 2, i + (j - lag) // 2, False, False)
            for n in range(NL - 2, NL + 2):
                step(n)

        def rows(ap, n):
            return ap[bass.ds(n * P, P), :]

        @block.sync
        def _(sp):
            def load_in(n, j):
                sp.dma_start(hin[:, j, 0, :], rows(m.hm, n)).then_inc(in_loaded[j], 16)
                sp.dma_start(hin[:, j, 1, :], rows(m.og, n)).then_inc(in_loaded[j], 16)
                sp.dma_start(hin[:, j, 2:4, :], m.gates[0:2, bass.ds(n * P, P), :].rearrange("g p n -> p g n"))\
                    .then_inc(in_loaded[j], 16)
            load_in(0, 0)
            for q, name in enumerate(("w_proj_m", "w_proj_g")):
                sp.dma_start(wp[:, q, :, :], w[name][0].rearrange("(k p) n -> p k n", p=P)).then_inc(s["w_loaded"], 16)
            sp.dma_start(wo[:, :, :], w["w_out"][0].rearrange("(k p) n -> p k n", p=P)).then_inc(s["w_loaded"], 16)
            sp.dma_start(wr[:, :, 0:GROUPS], w["w_grp"][0].rearrange("(k p) n -> p k n", p=P))\
                .then_inc(s["w_loaded"], 16)
            sp.dma_start(wr[:, :, GROUPS:], w["w_rexp"][0].rearrange("(k p) n -> p k n", p=P))\
                .then_inc(s["w_loaded"], 16)
            sp.dma_start(spread[:, :, :], m.mod_rows[:, 0:3 * D].rearrange("p (a n) -> p a n", a=3))\
                .then_inc(s["spread_loaded"], 16)
            sp.dma_start(sq[:, :], w["g_norm2"][0:1, :].partition_broadcast(P)).then_inc(s["spread_loaded"], 16)

            def a(n, j, half, first, final):
                if not first:
                    sp.wait_ge(s["yg_part"], n)
                sp.dma_start(mg[:, :, :], m.gates[2:4, bass.ds(n * P, P), :].rearrange("g p n -> p g n"))\
                    .then_inc(s["mg_loaded"], 16)
                if not final:
                    if not first:
                        sp.wait_ge(s["t_g"], n)
                    load_in(n + 1, 1 - j)

            def b(n, j, half, first, final):
                if not first:
                    sp.wait_ge(s["x1_done"], n)
                sp.dma_start(xt[:, :], rows(w["x"][0], n)).then_inc(s["x_loaded"], 16)

            def c(n, j, half, first, final):
                if first:
                    sp.sem_inc(s["h2_free"], 1)
                sp.wait_ge(s["x1_done"], n + 1)
                sp.dma_start(rows(m.x1, n), x1[:, j, :]).then_inc(s["x1_stored"], 16)
                sp.wait_ge(s["h2_done"], n + 1)
                sp.dma_start(rows(m.h2, n), h2[:, :]).then_inc(s["h2_stored"], 16)
                sp.wait_ge(s["h2_stored"], 16 * n + 16)
                sp.wait_ge(s["x1_stored"], 16 * n + 16)
                sp.sem_inc(s["h2_free"], 1)
            pipeline(sp, (a, 0), (c, 2), (b, 1))

        @block.scalar
        def _(act):
            def norms(n, j, half):
                act.wait_ge(in_loaded[j], 48 * half + 48)
                for q in range(2):
                    for h in range(HEADS):
                        last = act.activation(sqh[:, HEADS * q + h, :], hin[:, j, q, h * DV:(h + 1) * DV], ACT.Square,
                                              accum_out=st[:, j, 0, HEADS * q + h:HEADS * q + h + 1])
                last.then_inc(s["stat"], 1)
                act.wait_ge(s["stat"], 2 * n + 1)
                act.activation(st[:, j, 1, :], st[:, j, 0, :], ACT.Ln, bias=m.eps[:, 0:1], scale=1.0 / DV)\
                    .then_inc(s["stat"], 1)
                act.wait_ge(s["stat"], 2 * n + 2)
                act.activation(st[:, j, 2, :], st[:, j, 1, :], ACT.Exp, scale=-0.5).then_inc(s["rstd"], 1)

            def a(n, j, half, first, final):
                if not final:
                    norms(n + 1, 1 - j, half + j)

            def c(n, j, half, first, final):
                act.wait_ge(s["x1_done"], n + 1)
                act.activation(sq[:, :], x1[:, j, :], ACT.Square, accum_out=st2[:, 0:1]).then_inc(s["stat2"], 1)
                act.wait_ge(s["stat2"], 3 * n + 1)
                act.activation(st2[:, 1:2], st2[:, 0:1], ACT.Ln, bias=m.eps[:, 0:1], scale=1.0 / D)\
                    .then_inc(s["stat2"], 1)
                act.wait_ge(s["stat2"], 3 * n + 2)
                act.activation(st2[:, 2:3], st2[:, 1:2], ACT.Exp, scale=-0.5).then_inc(s["stat2"], 1)
                act.wait_ge(s["stat2"], 3 * n + 3)
                act.wait_ge(s["h2_free"], n + 1)
                if not first:
                    act.wait_ge(s["t_h"], n)
                act.activation(h2[:, :], x1[:, j, :], ACT.Copy, scale=st2[:, 2:3]).then_inc(s["xn"], 1)
            act.wait_ge(s["a2"], 1)
            norms(0, 0, 0)
            pipeline(act, (c, 2), (a, 0))

        @block.gpsimd
        def _(pool):
            def a(n, j, half, first, final):
                pool.wait_ge(s["yg_part"], n + 1)
                pool.tensor_tensor(y[:, j, :], y[:, j, :], yg[:, :], ALU.add).then_inc(s["y_done"], 1)

            def b(n, j, half, first, final):
                pool.wait_ge(s["x1_part"], n + 1)
                pool.wait_ge(s["x_loaded"], 16 * n + 16)
                pool.tensor_tensor(x1[:, j, :], x1[:, j, :], xt[:, :], ALU.add).then_inc(s["x1_done"], 1)

            def c(n, j, half, first, final):
                pool.wait_ge(s["xn"], n + 1)
                pool.tensor_tensor(h2[:, :], h2[:, :], spread[:, 2, :], ALU.mult).then_inc(s["h2_part"], 1)
                pool.wait_ge(s["h2_part"], n + 1)
                pool.tensor_tensor(h2[:, :], h2[:, :], spread[:, 1, :], ALU.add).then_inc(s["h2_done"], 1)
            pool.wait_ge(s["a2"], 1)
            pipeline(pool, (c, 2), (a, 0), (b, 1))

        @block.vector
        def _(dve):
            dve.wait_ge(s["spread_loaded"], 32)
            dve.scalar_tensor_tensor(out=spread[:, 2, :], in0=spread[:, 2, :], scalar=1.0, in1=sq[:, :],
                                     op0=ALU.add, op1=ALU.mult).then_inc(s["a2"], 1)

            def gated(n, j):
                dve.wait_ge(s["rstd"], n + 1)
                for q in range(2):
                    for h in range(HEADS):
                        o = hin[:, j, q, h * DV:(h + 1) * DV]
                        ins = dve.scalar_tensor_tensor(
                            out=o, in0=o, scalar=st[:, j, 2, HEADS * q + h:HEADS * q + h + 1],
                            in1=hin[:, j, 2 + q, h * DV:(h + 1) * DV], op0=ALU.mult, op1=ALU.mult)
                ins.then_inc(s["y_ready"], 1)

            def norm_col(row):
                return m.vec[:, :, row:row + 1].to_broadcast([P, KD, P])

            def turned(n, j, half, first, final):
                dve.wait_ge(s["t_m"], n + 1)
                dve.tensor_tensor(yt[:, 0, :, :], kmaj(tp_m[:, :]), norm_col(NORM_M), ALU.mult).then_inc(s["ym_t"], 1)
                dve.wait_ge(s["t_g"], n + 1)
                dve.tensor_tensor(yt[:, 1, :, :], kmaj(tp_g[:, :]), norm_col(NORM_G), ALU.mult).then_inc(s["yg_t"], 1)

            def part_m(n, j, half, first, final):
                dve.wait_ge(s["made_m"], n + 1)
                dve.wait_ge(s["mg_loaded"], 16 * n + 16)
                dve.tensor_tensor(y[:, j, :], p_m[:, :], mg[:, 0, :], ALU.mult).then_inc(s["y_part"], 1)

            def y_turned(n, j, half, first, final):
                dve.wait_ge(s["t_y"], n + 1)
                dve.tensor_copy(yt[:, 0, :, :], kmaj(tp_m[:, :])).then_inc(s["y_t"], 1)

            def part_g(n, j, half, first, final):
                if not final:
                    gated(n + 1, 1 - j)
                dve.wait_ge(s["made_g"], n + 1)
                if not first:
                    dve.wait_ge(s["y_done"], n)
                dve.tensor_tensor(yg[:, :], p_g[:, :], mg[:, 1, :], ALU.mult).then_inc(s["yg_part"], 1)

            def mixed(n, j, half, first, final):
                dve.wait_ge(s["made_out"], n + 1)
                if not isinstance(n, int) or n >= 2:
                    dve.wait_ge(s["h2_free"], n)
                dve.tensor_tensor(x1[:, j, :], p_m[:, :], spread[:, 0, :], ALU.mult).then_inc(s["x1_part"], 1)

            def router(n, j, half, first, final):
                dve.wait_ge(s["t_h"], n + 1)
                dve.tensor_copy(yt[:, 1, :, :], kmaj(tp_g[:, :])).then_inc(s["h_t"], 1)
                dve.wait_ge(s["made_r"], n + 1)
                dve.tensor_copy(m.logits[:, bass.ds(n, 1), :], tp_g[:, 0:GROUPS + EXPERTS]
                                .rearrange("p (a n) -> p a n", a=1)).then_inc(s["logits"], 1)
            gated(0, 0)
            pipeline(dve, (turned, 0), (part_m, 0), (y_turned, 1), (part_g, 0), (mixed, 1), (router, 2))
            dve.wait_ge(s["logits"], NL)

        @block.tensor
        def _(pe):
            pe.wait_ge(s["w_loaded"], 16 * 5)

            def turn(dst, src):
                for k in range(KD):
                    last = pe.transpose(dst[:, k * P:(k + 1) * P], src[:, k * P:(k + 1) * P], m.ident[:, :])
                return last

            def product(dst, lhs_t, weights):
                for q in range(2):
                    for k in range(KD):
                        last = pe.matmul(dst[:, q * 512:(q + 1) * 512], lhs_t[:, k, :],
                                         weights[:, k, q * 512:(q + 1) * 512], start=(k == 0), stop=(k == KD - 1))
                return last

            def branch_m(n, j, half, first, final):
                pe.wait_ge(s["y_ready"], n + 1)
                turn(tp_m, hin[:, j, 0, :]).then_inc(s["t_m"], 1)
                if not isinstance(n, int) or n >= 3:
                    pe.wait_ge(s["logits"], n - 2)
                turn(tp_g, hin[:, j, 1, :]).then_inc(s["t_g"], 1)
                pe.wait_ge(s["ym_t"], n + 1)
                if not isinstance(n, int) or n >= 2:
                    pe.wait_ge(s["x1_part"], n - 1)
                product(p_m, yt[:, 0, :, :], wp[:, 0, :, :]).then_inc(s["made_m"], 1)

            def turn_y(n, j, half, first, final):
                pe.wait_ge(s["y_done"], n + 1)
                turn(tp_m, y[:, j, :]).then_inc(s["t_y"], 1)

            def branch_g(n, j, half, first, final):
                pe.wait_ge(s["yg_t"], n + 1)
                if not first:
                    pe.wait_ge(s["yg_part"], n)
                product(p_g, yt[:, 1, :, :], wp[:, 1, :, :]).then_inc(s["made_g"], 1)

            def project_out(n, j, half, first, final):
                pe.wait_ge(s["y_t"], n + 1)
                if not final:
                    pe.wait_ge(s["y_part"], n + 2)
                product(p_m, yt[:, 0, :, :], wo).then_inc(s["made_out"], 1)

            def router(n, j, half, first, final):
                pe.wait_ge(s["h2_done"], n + 1)
                if not first:
                    pe.wait_ge(s["logits"], n)
                turn(tp_g, h2[:, :]).then_inc(s["t_h"], 1)
                pe.wait_ge(s["h_t"], n + 1)
                for k in range(KD):
                    last = pe.matmul(tp_g[:, 0:GROUPS + EXPERTS], yt[:, 1, k, :], wr[:, k, :],
                                     start=(k == 0), stop=(k == KD - 1))
                last.then_inc(s["made_r"], 1)
            pipeline(pe, (branch_m, 0), (turn_y, 1), (branch_g, 0), (project_out, 1), (router, 2))


def route(nc, m, sem, w):
    G, E, N = PER_GROUP, EXPERTS, NL
    BIG = 1e30
    with ExitStack() as ctx:
        sb = lambda n, s, dt=F32: ctx.enter_context(nc.sbuf_tensor(n, s, dt))
        bias = sb("rt_bias", [P, GROUPS + E])
        lg = sb("rt_lg", [P, N, GROUPS + E])
        rank4 = sb("rt_rank4", [P, 4])
        mx = sb("rt_max", [P, N])
        eg = sb("rt_eg", [P, N, 4])
        sg = sb("rt_sg", [P, N])
        hot = sb("rt_hot", [P, 3, N, 4])
        tmp = sb("rt_tmp", [P, N, 4])
        sel = sb("rt_sel", [P, N, GROUPS, 4])
        es = sb("rt_es", [P, N, 4])
        e12 = sb("rt_e12", [P, 2, N])
        x = sb("rt_x", [P, N])
        hots = sb("rt_hots", [P, 2, N, GROUPS, 4])
        both = sb("rt_both", [P, N * E])
        pre = sb("rt_pre", [P, N + 1, E])
        tot = sb("rt_tot", [P, N, E])
        base = sb("rt_base", [P, N, E])
        blocks = sb("rt_blocks", [P, E])
        ends = sb("rt_ends", [P, E])
        ones16 = sb("rt_ones16", [P, E])
        prod = sb("rt_prod", [P, 2, N, E])
        dest = sb("rt_dest", [P, 2, N])
        assert BLOCKS + 1 == 1 << 5 and P == 1 << 7
        hi = sb("rt_hi", [P, 2, N], I32)
        place = sb("rt_place", [P, 2, N], I32)
        token = sb("rt_token", [P, N], I32)
        zero = sb("rt_zero", [P, BLOCKS + 1], I32)
        which = sb("rt_which", [P, BLOCKS])
        le = sb("rt_le", [P, BLOCKS, E])
        blk = sb("rt_blk", [P, BLOCKS])
        cum_ps = ctx.enter_context(nc.psum_tensor("rt_cum_ps", [P, N * E], F32))
        tot_ps = ctx.enter_context(nc.psum_tensor("rt_tot_ps", [P, N * E], F32))
        step, loaded, built, exps, ranked, zeroed, scattered = (sem(f"rt_{n}") for n in (
            "step", "loaded", "built", "exps", "ranked", "zeroed", "scattered"))
        block = ctx.enter_context(nc.Block())
        table = m.row_tok.rearrange("(p b) a -> p (b a)", p=P)
        over = lambda ap, shape: ap.to_broadcast(shape)

        @block.sync
        def _(sp):
            sp.dma_start(bias[:, 0:GROUPS], w["b_grp"].partition_broadcast(P)).then_inc(loaded, 16)
            sp.dma_start(bias[:, GROUPS:], w["b_rexp"].partition_broadcast(P)).then_inc(loaded, 16)
            sp.wait_ge(built, 1)
            sp.dma_start(table, zero[:, :]).then_inc(zeroed, 16)

        @block.gpsimd
        def _(pool):
            pool.memset(zero[:, :], 0).then_inc(built, 1)
            pool.iota(token[:, :], pattern=[[P, N]], base=0, channel_multiplier=1).then_inc(built, 1)
            pool.iota(which[:, :], pattern=[[1, BLOCKS]], base=0, channel_multiplier=0,
                      allow_small_or_imprecise_dtypes=True).then_inc(built, 1)
            pool.iota(rank4[:, :], pattern=[[-1, 4]], base=4, channel_multiplier=0,
                      allow_small_or_imprecise_dtypes=True).then_inc(built, 1)
            pool.memset(ones16[:, :], 1.0).then_inc(built, 1)
            pool.wait_ge(built, 2)
            pool.wait_ge(zeroed, 16)
            pool.wait_ge(ranked, 2)
            for k in range(TOP_K):
                for n in range(N):
                    pool.indirect_dma_start(
                        out=m.row_tok, out_offset=bass.IndirectOffsetOnAxis(ap=place[:, k, n:n + 1], axis=0),
                        in_=token[:, n:n + 1], in_offset=None).then_inc(scattered, 16)
            pool.wait_ge(scattered, 16 * TOP_K * N)

        @block.scalar
        def _(act):
            act.wait_ge(step, 3)
            act.activation(eg[:, :, :], eg[:, :, :], ACT.Exp).then_inc(exps, 1)
            act.wait_ge(exps, 1)
            act.wait_ge(built, 6)
            act.activation(x[:, :], x[:, :], ACT.Exp).then_inc(exps, 1)

        @block.tensor
        def _(pe):
            pe.wait_ge(ranked, 1)
            pe.matmul(cum_ps[:, :], m.before[:, :], both[:, :], start=True, stop=True)
            pe.matmul(tot_ps[:, :], m.ones[:, :], both[:, :], start=True, stop=True).then_inc(built, 1)

        @block.vector
        def _(dve):
            count = [0]

            def then(ins):
                count[0] += 1
                ins.then_inc(step, 1)
                dve.wait_ge(step, count[0])

            tt, ts = dve.tensor_tensor, dve.tensor_scalar
            dve.wait_ge(loaded, 32)
            then(tt(lg[:, :, :], m.logits[:, :, :],
                    bias[:, :].rearrange("p (a n) -> p a n", a=1).to_broadcast([P, N, GROUPS + E]), ALU.add))
            grp = lg[:, :, 0:GROUPS]
            wide = lambda ap: ap.rearrange("p (n a) -> p n a", a=1).to_broadcast([P, N, 4])
            then(dve.tensor_reduce(mx[:, :], grp, AX.X, ALU.max))
            then(tt(eg[:, :, :], grp, wide(mx[:, :]), ALU.subtract))
            dve.wait_ge(exps, 1)
            then(dve.tensor_reduce(sg[:, :], eg[:, :, :], AX.X, ALU.add))
            dve.wait_ge(built, 5)
            prefer = rank4[:, :].rearrange("p (a n) -> p a n", a=1).to_broadcast([P, N, 4])

            def first_max(values, largest, out):
                then(tt(tmp[:, :, :], values, wide(largest), ALU.is_equal))
                then(tt(tmp[:, :, :], tmp[:, :, :], prefer, ALU.mult))
                then(dve.tensor_reduce(mx[:, :], tmp[:, :, :], AX.X, ALU.max))
                then(tt(out, tmp[:, :, :], wide(mx[:, :]), ALU.is_equal))

            first_max(grp, mx[:, :], hot[:, 0])
            then(tt(sel[:, :, :, :], lg[:, :, GROUPS:].rearrange("p n (g e) -> p n g e", g=GROUPS),
                    hot[:, 0].rearrange("p n (g a) -> p n g a", a=1).to_broadcast([P, N, GROUPS, 4]), ALU.mult))
            then(dve.tensor_reduce(es[:, :, :], sel[:, :, :, :].rearrange("p n g e -> p n e g"), AX.X, ALU.add))
            then(dve.tensor_reduce(e12[:, 0, :], es[:, :, :], AX.X, ALU.max))
            first_max(es[:, :, :], e12[:, 0, :], hot[:, 1])
            then(dve.scalar_tensor_tensor(out=es[:, :, :], in0=hot[:, 1], scalar=-BIG, in1=es[:, :, :],
                                          op0=ALU.mult, op1=ALU.add))
            then(dve.tensor_reduce(e12[:, 1, :], es[:, :, :], AX.X, ALU.max))
            first_max(es[:, :, :], e12[:, 1, :], hot[:, 2])
            then(tt(x[:, :], e12[:, 1, :], e12[:, 0, :], ALU.subtract))
            dve.sem_inc(built, 1)
            for k in range(TOP_K):
                for g in range(GROUPS):
                    then(tt(hots[:, k, :, g, :], hot[:, 1 + k], hot[:, 0, :, g:g + 1].to_broadcast([P, N, 4]),
                            ALU.mult))
            hv = hots[:, :, :, :, :].rearrange("p k n g e -> p k (n g e)")
            tt(both[:, :], hv[:, 0], hv[:, 1], ALU.add).then_inc(ranked, 1)
            dve.wait_ge(exps, 2)
            then(dve.scalar_tensor_tensor(out=sg[:, :], in0=x[:, :], scalar=1.0, in1=sg[:, :],
                                          op0=ALU.add, op1=ALU.mult))
            then(dve.reciprocal(m.weight[:, 0, :], sg[:, :]))
            then(tt(m.weight[:, 1, :], m.weight[:, 0, :], x[:, :], ALU.mult))
            dve.wait_ge(built, 7)
            then(dve.tensor_copy(tot[:, :, :], tot_ps[:, :].rearrange("p (n e) -> p n e", e=E)))
            then(dve.memset(pre[:, 0, :], 0.0))
            for n in range(N):
                then(tt(pre[:, n + 1, :], pre[:, n, :], tot[:, n, :], ALU.add))
            then(ts(blocks[:, :], pre[:, N, :], 0.0, None, ALU.is_gt))
            for q in range(1, SEQ // P):
                then(dve.scalar_tensor_tensor(out=blocks[:, :], in0=pre[:, N, :], scalar=float(P * q),
                                              in1=blocks[:, :], op0=ALU.is_gt, op1=ALU.add))
            then(dve.tensor_tensor_scan(ends[:, :], ones16[:, :], blocks[:, :], 0.0, ALU.mult, ALU.add))
            then(tt(le[:, :, :], ends[:, :].rearrange("p (a e) -> p a e", a=1).to_broadcast([P, BLOCKS, E]),
                    which[:, :].rearrange("p (b a) -> p b a", a=1).to_broadcast([P, BLOCKS, E]), ALU.is_le))
            then(dve.tensor_reduce(blk[:, :], le[:, :, :], AX.X, ALU.add))
            then(ts(m.block_e[:, 0:BLOCKS], blk[:, :], float(E - 1), None, ALU.min))
            then(tt(ends[:, :], ends[:, :], blocks[:, :], ALU.subtract))
            then(tt(base[:, :, :], cum_ps[:, :].rearrange("p (n e) -> p n e", e=E), pre[:, 0:N, :], ALU.add))
            then(dve.scalar_tensor_tensor(out=base[:, :, :],
                                          in0=ends[:, :].rearrange("p (a e) -> p a e", a=1).to_broadcast([P, N, E]),
                                          scalar=float(P), in1=base[:, :, :], op0=ALU.mult, op1=ALU.add))
            for k in range(TOP_K):
                then(tt(prod[:, k].rearrange("p n e -> p (n e)"), hv[:, k],
                        base[:, :, :].rearrange("p n e -> p (n e)"), ALU.mult))
            then(dve.tensor_reduce(dest[:, :, :], prod[:, :, :, :], AX.X, ALU.add))
            then(dve.tensor_copy(m.dest_i[:, :, :], dest[:, :, :]))
            then(ts(hi[:, :, :], m.dest_i[:, :, :], 7, None, ALU.logical_shift_right))
            then(ts(place[:, :, :], m.dest_i[:, :, :], P - 1, 5, ALU.bitwise_and, ALU.logical_shift_left))
            tt(place[:, :, :], place[:, :, :], hi[:, :, :], ALU.add).then_inc(ranked, 1)
            dve.wait_ge(ranked, 2)


def experts(nc, m, sem, w):
    with ExitStack() as ctx:
        sb = lambda n, s, dt=F32: ctx.enter_context(nc.sbuf_tensor(n, s, dt))
        bank = lambda n, k=1: ctx.enter_context(nc.psum_tensor(n, [P, k * 512], F32))
        HK = FF // P
        PIECE = KD * FF
        assert PIECE == HK * D
        HALF = PIECE // 2
        raw = sb("ex_raw", [P, 3, PIECE])
        hi = sb("ex_w_hi", [P, 3, PIECE], F32R)
        lo = sb("ex_w_lo", [P, 3, PIECE], F32R)
        table = sb("ex_rows", [P, BLOCKS + 1], I32)
        idx = sb("ex_idx", [P, 2], I32)
        xg = sb("ex_x", [P, 2, D])
        xt_hi = sb("ex_x_hi", [P, D], F32R)
        xt_lo = sb("ex_x_lo", [P, D], F32R)
        gate = sb("ex_gate", [P, FF])
        hid = sb("ex_hidden", [P, FF])
        ht_hi = sb("ex_hidden_hi", [P, FF], F32R)
        ht_lo = sb("ex_hidden_lo", [P, FF], F32R)
        yo = sb("ex_y", [P, 2, D])
        x_ps, g_ps, u_ps, h_ps, y_ps = bank("ex_x_ps", 2), bank("ex_g_ps"), bank("ex_u_ps"), bank("ex_h_ps"), bank("ex_y_ps", 2)
        s = {name: sem(f"ex_{name}") for name in (
            "table", "idx", "t_x", "x_hi", "x_lo", "gate", "hidden", "t_h", "h_hi", "h_lo", "y_left",
            "gather_begun")}
        loaded, hi_done, lo_done, made = ([sem(f"ex_{n}{q}") for q in range(3)] for n in (
            "loaded", "hi_done", "lo_done", "made"))
        gathered, stored = ([sem(f"ex_{n}{j}") for j in range(2)] for n in ("gathered", "stored"))
        block = ctx.enter_context(nc.Block())

        def each(eng, body):
            for b in range(2):
                body(b, b, 0)
            with eng.Fori(1, BLOCKS // 2) as i:
                for j in range(2):
                    body(2 * i + j, j, i)
            if BLOCKS % 2:
                body(BLOCKS - 1, (BLOCKS - 1) % 2, BLOCKS // 2)
        late = lambda b, n: not isinstance(b, int) or b >= n
        more = lambda b: not isinstance(b, int) or b < BLOCKS - 1

        @block.sync
        def _(sp):
            def load(b, q):
                e = sp.value_load(m.block_e[0:1, bass.ds(b, 1)], min_val=0, max_val=EXPERTS - 1)
                if late(b, 1):
                    sp.wait_ge(lo_done[q], 2 * b)
                if q < 2:
                    src = w["w_up"][0][bass.ds(e, 1)].rearrange("a (k p) n -> p (a k) n", p=P)
                    src = src[:, :, q * FF:(q + 1) * FF]
                else:
                    src = w["w_down"][0][bass.ds(e, 1)].rearrange("a (k p) n -> p (a k) n", p=P)
                sp.dma_start(raw[:, q, :].rearrange("p (k n) -> p k n", n=FF if q < 2 else D), src)\
                    .then_inc(loaded[q], 16)

            def step(b, j, half):
                if more(b):
                    load(b + 1, 0)
                    load(b + 1, 1)
                load(b, 2)
            load(0, 0)
            load(0, 1)
            each(sp, step)

        @block.gpsimd
        def _(pool):
            pool.dma_start(table[:, :], m.row_tok.rearrange("(p b) a -> p (b a)", p=P)).then_inc(s["table"], 16)
            pool.wait_ge(s["table"], 16)

            def gather(b, j, half):
                if late(b, 2):
                    pool.wait_ge(s["t_x"], b - 1)
                pool.tensor_copy(idx[:, j:j + 1], table[:, bass.ds(b, 1)]).then_inc(s["idx"], 1)
                pool.wait_ge(s["idx"], b + 1)
                pool.sem_inc(s["gather_begun"], 1)
                pool.indirect_dma_start(out=xg[:, j, :], out_offset=None, in_=m.h2,
                                        in_offset=bass.IndirectOffsetOnAxis(ap=idx[:, j:j + 1], axis=0))\
                    .then_inc(gathered[j], 16)
            each(pool, gather)

        @block.tensor
        def _(pe):
            def product(dst, a_hi, a_lo, q, at, k, first, last):
                ka = slice(k * P, (k + 1) * P)
                pe.matmul(dst, a_hi[:, ka], hi[:, q, at:at + 512], start=first, stop=False)
                pe.matmul(dst, a_hi[:, ka], lo[:, q, at:at + 512], start=False, stop=False)
                return pe.matmul(dst, a_lo[:, ka], hi[:, q, at:at + 512], start=False, stop=last)

            def turn_x(b, j, half):
                pe.wait_ge(gathered[j], 16 * half + 16)
                if late(b, 1):
                    pe.wait_ge(s["x_lo"], b)
                for k in range(KD):
                    last = pe.transpose(x_ps[:, k * P:(k + 1) * P], xg[:, j, k * P:(k + 1) * P], m.ident[:, :])
                last.then_inc(s["t_x"], 1)

            def down(b, j, half):
                pe.wait_ge(lo_done[2], 2 * b + 2)
                pe.wait_ge(s["h_lo"], b + 1)
                if late(b, 1):
                    pe.wait_ge(s["y_left"], b)
                for n in range(D // 512):
                    for k in range(HK):
                        last = product(y_ps[:, n * 512:(n + 1) * 512], ht_hi, ht_lo, 2, k * D + n * 512, k,
                                       k == 0, k == HK - 1)
                last.then_inc(made[2], 1)

            def step(b, j, half):
                pe.wait_ge(s["x_lo"], b + 1)
                if late(b, 1):
                    pe.wait_ge(s["hidden"], b)
                for q, dst in enumerate((g_ps, u_ps)):
                    pe.wait_ge(lo_done[q], 2 * b + 2)
                    for k in range(KD):
                        last = product(dst[:, :], xt_hi, xt_lo, q, k * FF, k, k == 0, k == KD - 1)
                    last.then_inc(made[q], 1)
                if more(b):
                    turn_x(b + 1, 1 - j, half + j)
                if late(b, 1):
                    down(b - 1, 1 - j, half - 1 + j)
                pe.wait_ge(s["hidden"], b + 1)
                if late(b, 1):
                    pe.wait_ge(s["h_lo"], b)
                for k in range(HK):
                    last = pe.transpose(h_ps[:, k * P:(k + 1) * P], hid[:, k * P:(k + 1) * P], m.ident[:, :])
                last.then_inc(s["t_h"], 1)
            turn_x(0, 0, 0)
            each(pe, step)
            down(BLOCKS - 1, (BLOCKS - 1) % 2, (BLOCKS - 1) // 2)

        @block.scalar
        def _(act):
            def split_hi(b, q):
                act.wait_ge(loaded[q], 16 * b + 16)
                if late(b, 1):
                    act.wait_ge(made[q], b)
                for h in (slice(0, HALF), slice(HALF, PIECE)):
                    act.activation(hi[:, q, h], raw[:, q, h], ACT.Copy).then_inc(hi_done[q], 1)

            def x_hi(b):
                act.wait_ge(s["t_x"], b + 1)
                act.activation(xt_hi[:, :], x_ps[:, :], ACT.Copy).then_inc(s["x_hi"], 1)

            def out(b, j, half):
                act.wait_ge(made[2], b + 1)
                if late(b, 2):
                    act.wait_ge(stored[j], 16 * half)
                act.activation(yo[:, j, :], y_ps[:, :], ACT.Copy).then_inc(s["y_left"], 1)
                act.wait_ge(s["y_left"], b + 1)
                act.dma_start(m.y_rows[bass.ds(b * P, P), :], yo[:, j, :]).then_inc(stored[j], 16)

            def step(b, j, half):
                act.wait_ge(made[0], b + 1)
                if late(b, 1):
                    act.wait_ge(s["hidden"], b)
                act.activation(gate[:, :], g_ps[:, :], ACT.Silu).then_inc(s["gate"], 1)
                if more(b):
                    split_hi(b + 1, 0)
                    split_hi(b + 1, 1)
                    x_hi(b + 1)
                if late(b, 1):
                    out(b - 1, 1 - j, half - 1 + j)
                split_hi(b, 2)
            split_hi(0, 0)
            x_hi(0)
            split_hi(0, 1)
            each(act, step)
            out(BLOCKS - 1, (BLOCKS - 1) % 2, (BLOCKS - 1) // 2)
            act.wait_ge(stored[0], 16 * ((BLOCKS + 1) // 2))
            act.wait_ge(stored[1], 16 * (BLOCKS // 2))

        @block.vector
        def _(dve):
            def split_lo(b, q):
                for h in range(2):
                    at = slice(h * HALF, (h + 1) * HALF)
                    dve.wait_ge(hi_done[q], 2 * b + 1 + h)
                    dve.tensor_tensor(lo[:, q, at], raw[:, q, at], hi[:, q, at].bitcast(F32), ALU.subtract)\
                        .then_inc(lo_done[q], 1)

            def x_lo(b):
                dve.wait_ge(s["x_hi"], b + 1)
                dve.tensor_tensor(xt_lo[:, :], x_ps[:, :], xt_hi[:, :].bitcast(F32), ALU.subtract)\
                    .then_inc(s["x_lo"], 1)

            def step(b, j, half):
                if more(b):
                    split_lo(b + 1, 0)
                dve.wait_ge(s["gate"], b + 1)
                dve.wait_ge(made[1], b + 1)
                if late(b, 1):
                    dve.wait_ge(s["t_h"], b)
                dve.tensor_tensor(hid[:, :], u_ps[:, :], gate[:, :], ALU.mult).then_inc(s["hidden"], 1)
                if more(b):
                    split_lo(b + 1, 1)
                    x_lo(b + 1)
                dve.wait_ge(s["t_h"], b + 1)
                if late(b, 1):
                    dve.wait_ge(made[2], b)
                dve.tensor_copy(ht_hi[:, :], h_ps[:, :]).then_inc(s["h_hi"], 1)
                dve.wait_ge(s["h_hi"], b + 1)
                dve.tensor_tensor(ht_lo[:, :], h_ps[:, :], ht_hi[:, :].bitcast(F32), ALU.subtract)\
                    .then_inc(s["h_lo"], 1)
                split_lo(b, 2)
            split_lo(0, 0)
            x_lo(0)
            split_lo(0, 1)
            each(dve, step)


def combine(nc, m, sem, w):
    with ExitStack() as ctx:
        sb = lambda n, s: ctx.enter_context(nc.sbuf_tensor(n, s, F32))
        yr = sb("co_rows", [P, NL, TOP_K, D])
        x1 = sb("co_x1", [P, NL, D])
        sq = sb("co_sq", [P, 2, D])
        gate2 = sb("co_gate2", [P, D])
        gf = sb("co_g_final", [P, D])
        st = sb("co_stat", [P, NL, 3])
        loaded, x_loaded, mixed, stat, normed, stored = (sem(f"co_{n}") for n in (
            "loaded", "x_loaded", "mixed", "stat", "normed", "stored"))
        gathered = [sem(f"co_gathered{n}") for n in range(NL)]
        block = ctx.enter_context(nc.Block())

        @block.sync
        def _(sp):
            sp.dma_start(gate2[:, :], m.mod_rows[:, 3 * D:4 * D]).then_inc(loaded, 16)
            sp.dma_start(gf[:, :], w["g_final"].rearrange("(a n) -> a n", a=1).partition_broadcast(P))\
                .then_inc(loaded, 16)
            sp.dma_start(x1[:, :, :], m.x1.rearrange("(n p) d -> p n d", p=P)).then_inc(x_loaded, 16)
            for n in range(NL):
                sp.wait_ge(normed, n + 1)
                sp.dma_start(m.out[0, n * P:(n + 1) * P, :], yr[:, n, 0, :]).then_inc(stored, 16)
            sp.wait_ge(stored, 16 * NL)

        @block.gpsimd
        def _(pool):
            for n in range(NL):
                for k in range(TOP_K):
                    pool.indirect_dma_start(
                        out=yr[:, n, k, :], out_offset=None, in_=m.y_rows,
                        in_offset=bass.IndirectOffsetOnAxis(ap=m.dest_i[:, k, n:n + 1], axis=0))\
                        .then_inc(gathered[n], 16)

        @block.scalar
        def _(act):
            for n in range(NL):
                act.wait_ge(mixed, 4 * n + 4)
                act.activation(sq[:, n % 2, :], x1[:, n, :], ACT.Square, accum_out=st[:, n, 0:1]).then_inc(stat, 1)
                act.wait_ge(stat, 3 * n + 1)
                act.activation(st[:, n, 1:2], st[:, n, 0:1], ACT.Ln, bias=m.eps[:, 0:1], scale=1.0 / D)\
                    .then_inc(stat, 1)
                act.wait_ge(stat, 3 * n + 2)
                act.activation(st[:, n, 2:3], st[:, n, 1:2], ACT.Exp, scale=-0.5).then_inc(stat, 1)

        @block.vector
        def _(dve):
            dve.wait_ge(loaded, 32)
            dve.wait_ge(x_loaded, 16)

            def finish(n):
                dve.wait_ge(stat, 3 * n + 3)
                dve.scalar_tensor_tensor(out=yr[:, n, 0, :], in0=x1[:, n, :], scalar=st[:, n, 2:3], in1=gf[:, :],
                                         op0=ALU.mult, op1=ALU.mult).then_inc(normed, 1)
            for n in range(NL):
                y0, y1 = yr[:, n, 0, :], yr[:, n, 1, :]
                dve.wait_ge(gathered[n], 32)
                dve.tensor_scalar(y0, y0, m.weight[:, 0, n:n + 1], None, ALU.mult).then_inc(mixed, 1)
                dve.wait_ge(mixed, 4 * n + 1)
                dve.scalar_tensor_tensor(out=y0, in0=y1, scalar=m.weight[:, 1, n:n + 1], in1=y0,
                                         op0=ALU.mult, op1=ALU.add).then_inc(mixed, 1)
                dve.wait_ge(mixed, 4 * n + 2)
                dve.tensor_tensor(y0, y0, gate2[:, :], ALU.mult).then_inc(mixed, 1)
                dve.wait_ge(mixed, 4 * n + 3)
                dve.tensor_tensor(x1[:, n, :], x1[:, n, :], y0, ALU.add).then_inc(mixed, 1)
                if n:
                    finish(n - 1)
            finish(NL - 1)


def build(nc, w, out, upto=99):
    m = Shared()
    top = ExitStack()
    with top:
        used = []

        def sem(name):
            used.append(nc.alloc_semaphore(name))
            return used[-1]

        def fresh_semaphores():
            nc.all_engine_barrier()
            nc.clear_and_free_semaphores(used)
            used.clear()
            nc.all_engine_barrier()

        def place(stack, name, shape, dt=F32):
            return stack.enter_context(nc.sbuf_tensor(name, shape, dt))

        def dram(name, shape, dt=F32):
            return nc.dram_tensor(name, shape, dt, kind="Internal").ap()

        def run(*stages):
            for stage in stages:
                stage(nc, m, sem, w)

        m.out = out
        m.vals = dram("vals", [2, T, D])
        m.gates = dram("out_gates", [4, SEQ, D])
        m.mod_rows = dram("mod_spread", [P, 4 * D])
        m.h_kept = dram("h_kept", [P, KD, T])
        m.hm = dram("mlstm_out", [SEQ, D])
        m.og = dram("gla_out", [SEQ, D])
        m.x1 = dram("x_mixed", [SEQ, D])
        m.h2 = dram("moe_in", [SEQ, D])
        m.row_tok = dram("row_token", [(BLOCKS + 1) * P, 1], I32)
        m.y_rows = dram("expert_rows", [BLOCKS * P, D])
        m.ident = place(top, "ident", [P, P])
        m.ones = place(top, "ones", [P, P])
        m.before = place(top, "before", [P, P])
        m.logits = place(top, "logits", [P, NL, GROUPS + EXPERTS])
        m.vec = place(top, "vec", [P, KD, NVEC])
        m.mod_col = place(top, "mod_col", [P, 2 * KD, 2])
        m.a1 = place(top, "a1", [P, KD, 2])
        m.eps = place(top, "eps", [P, 1])
        m.weight = place(top, "weight", [P, TOP_K, NL])
        m.dest_i = place(top, "dest_i", [P, TOP_K, NL], I32)
        m.block_e = place(top, "block_e", [P, BLOCKS + 1], I32)
        with ExitStack() as gla:
            m.row_of = place(gla, "row_of", [GATE_ROWS, 2 * HEADS, P])
            m.level_mask = place(gla, "level_mask", [P, 2, LEVELS, HEADS * P // 2], mybir.dt.int8)
            m.restart = place(gla, "restart", [P, 2, 5 * P])
            run(constants, modulation)
            with ExitStack() as split:
                m.h_hi = place(split, "h_hi", [P, KD, T], F32R)
                m.h_lo = place(split, "h_lo", [P, KD, T], F32R)
                with ExitStack() as whole:
                    m.h_t = place(whole, "h_first", [P, KD, T])
                    run(norm_in, split_h)
                run(project_values, project_gates)
            fresh_semaphores()
            m.qg = place(gla, "qg", [P, HEADS, SEQ])
            m.kg = place(gla, "kg", [P, HEADS, T])
            m.lr = place(gla, "lr", [32, 2, T])
            m.w2 = place(gla, "w2", [32, 2, HEADS * DK])
            with ExitStack() as mls:
                m.qm = place(mls, "qm", [P, HEADS, SEQ])
                m.km = place(mls, "km", [P, HEADS, T])
                m.gate_i = place(mls, "gate_i", [GATE_ROWS, T])
                m.gate_f = place(mls, "gate_f", [GATE_ROWS, T])
                with ExitStack() as proj:
                    m.h_t = place(proj, "h_t", [P, KD, T])
                    run(reload_h, project_qk, project_small)
                fresh_semaphores()
                m.gate_g = place(mls, "gate_g", [GATE_ROWS, T])
                m.neg_m = place(mls, "neg_m", [GATE_ROWS, T])
                m.w_inter = place(mls, "w_inter", [GATE_ROWS, T])
                m.g_col = place(mls, "g_col", [P, NT, GATE_ROWS])
                m.ws_col = place(mls, "ws_col", [P, NT, GATE_ROWS])
                m.emt_col = place(mls, "emt_col", [P, NT, GATE_ROWS])
                m.dec_all = place(mls, "dec_all", [P, 2 * HEADS, NT])
                run(gate_rows)
                if upto >= 1:
                    run(mlstm_scan)
            if upto >= 2:
                run(gla_scan)
        fresh_semaphores()
        if upto >= 3:
            run(mix_out)
        if upto >= 4:
            run(route, experts, combine)


_INS = ["x", "c", "ctx", "c_ctx", "w_mod", "b_mod", "g_norm1", "w_in", "ml_conv", "ml_conv_b", "b_mgate", "ml_norm",
        "gla_w2", "gla_b2", "gla_norm", "w_proj_m", "w_proj_g", "w_out", "g_norm2", "w_grp", "b_grp", "w_rexp",
        "b_rexp", "w_up", "w_down", "g_final"]


def kernel(**inputs):
    import numpy as _np
    import concourse.bacc as _bacc
    from concourse import mybir as _mybir
    from concourse.bass_utils import run_bass_kernel_spmd as _run

    nc = _bacc.Bacc("TRN2", target_bir_lowering=False, num_devices=1)
    arrays, w = {}, {}
    for name in _INS:
        a = _np.ascontiguousarray(inputs[name])
        arrays[f"in_{name}_dram"] = a
        w[name] = nc.dram_tensor(f"in_{name}_dram", a.shape, _mybir.dt.from_np(a.dtype), kind="ExternalInput").ap()
    out = nc.dram_tensor("out_0_dram", (1, SEQ, D), F32, kind="ExternalOutput").ap()
    build(nc, w, out)
    r = _run(nc, [arrays], core_ids=[0])
    return r.results[0]["out_0_dram"]
```

```python
from contextlib import ExitStack

import concourse.bass as bass
from concourse import mybir

F32 = mybir.dt.float32
F32R = mybir.dt.float32r
I32 = mybir.dt.int32
ALU = mybir.AluOpType
ACT = mybir.ActivationFunctionType
AX = mybir.AxisListType

P = 128
D = 1024
KD = D // P
SEQ = 1024
CTX = 256
T = CTX + SEQ
NT = T // P
NC = CTX // P
NL = SEQ // P
GRID_W = 64
GRID_H = SEQ // GRID_W
HEADS = 4
DK = 128
DV = 256
RANK = 16
TAU = 16.0
EPS = 1e-6
NEG_BIG = -1e30
LEVELS = 7
GROUPS = 4
PER_GROUP = 4
EXPERTS = GROUPS * PER_GROUP
FF = 512
TOP_K = 2
BLOCKS = (SEQ * TOP_K + EXPERTS * (P - 1)) // P

QM, KM, VM, OM = 0, 512, 1024, 2048
GATE = 3072
QG, KG, VG, RG = 3088, 3600, 4112, 5136
LR = 6160
MGM, MGG = 6192, 7216
COLS = 512

GATE_ROWS = 36
SMALL = 100
CONV_B, GN1, B2, NORM_M, NORM_G, NVEC = 9, 10, 11, 12, 13, 14


class Shared:
    pass


def constants(nc, m, sem, w):
    with ExitStack() as ctx:
        rows = ctx.enter_context(nc.sbuf_tensor("vec_rows", [NVEC, D], F32))
        ps = ctx.enter_context(nc.psum_tensor("vec_ps", [P, KD * NVEC], F32))
        built = sem("const_built")
        ident_ready = sem("ident_ready")
        rows_loaded = sem("vec_rows_loaded")
        turned = sem("vec_turned")
        moved = sem("vec_moved")
        block = ctx.enter_context(nc.Block())

        @block.sync
        def _(sp):
            loads = [
                (rows[0:9, :], w["ml_conv"][0].rearrange("a b n -> (a b) n")),
                (rows[CONV_B:CONV_B + 1, :], w["ml_conv_b"]),
                (rows[GN1:GN1 + 1, :], w["g_norm1"]),
                (rows[B2:B2 + 1, :], w["gla_b2"].rearrange("a d e -> a (d e)")),
                (rows[NORM_M:NORM_M + 1, :], w["ml_norm"]),
                (rows[NORM_G:NORM_G + 1, :], w["gla_norm"]),
            ]
            for dst, src in loads:
                sp.dma_start(dst, src).then_inc(rows_loaded, 16)

        @block.gpsimd
        def _(pool):
            n = [0]

            def step(ins):
                n[0] += 1
                ins.then_inc(built, 1)
                pool.wait_ge(built, n[0])

            step(pool.memset(m.ident[:, :], 0.0))
            pool.affine_select(out=m.ident[:, :], in_=m.ident[:, :], compare_op=ALU.not_equal, fill=1.0,
                               base=0, pattern=[[-1, P]], channel_multiplier=1).then_inc(ident_ready, 1)
            step(pool.memset(m.ones[:, :], 1.0))
            step(pool.memset(m.eps[:, :], EPS))

        @block.tensor
        def _(pe):
            pe.wait_ge(ident_ready, 1)
            pe.wait_ge(rows_loaded, 16 * 6)
            for k in range(KD):
                last = pe.transpose(ps[:, k * NVEC:(k + 1) * NVEC], rows[:, k * P:(k + 1) * P],
                                    m.ident[0:NVEC, 0:NVEC])
            last.then_inc(turned, 1)

        @block.vector
        def _(dve):
            dve.wait_ge(turned, 1)
            dve.tensor_copy(m.vec[:, :, :], ps[:, :].rearrange("p (k n) -> p k n", k=KD)).then_inc(moved, 1)
            dve.wait_ge(moved, 1)


def build_masks(m, pool, built):
    n = [0]

    def step(ins):
        n[0] += 1
        ins.then_inc(built, 1)
        pool.wait_ge(built, n[0])

    step(pool.affine_select(out=m.before[:, :], in_=m.ones[:, :], compare_op=ALU.is_gt, fill=0.0,
                            base=0, pattern=[[1, P]], channel_multiplier=-1))
    step(pool.memset(m.row_of[:, :, :], 0.0))
    v = m.row_of[:, :, :].rearrange("p (d h) t -> p d h t", d=2)
    step(pool.affine_select(out=v, in_=v, compare_op=ALU.not_equal, fill=1.0, base=0,
                            pattern=[[-32, 2], [-1, HEADS], [0, P]], channel_multiplier=1))
    step(pool.memset(m.level_mask[:, :, :, :], 1))
    for d in range(2):
        for l in range(LEVELS):
            h = 1 << l
            nj = P // 2 // h
            v = m.level_mask[:, d, l, :].rearrange("p (n j i) -> p n j i", n=HEADS, i=h)
            step(pool.affine_select(out=v, in_=v, compare_op=ALU.is_ge, fill=0.0, base=-h * d,
                                    pattern=[[0, HEADS], [-2 * h, nj], [0, h]], channel_multiplier=1))
            step(pool.affine_select(out=v, in_=v, compare_op=ALU.is_ge, fill=0.0, base=h - 1 + h * d,
                                    pattern=[[0, HEADS], [2 * h, nj], [0, h]], channel_multiplier=-1))
    step(pool.memset(m.restart[:, :, :], 1.0))
    v = m.restart[:, :, :].rearrange("p d (c t) -> p d c t", t=P)
    step(pool.memset(v[:, 0, :, 0:1], 0.0))
    step(pool.memset(v[:, 1, :, P - 1:P], 0.0))


def modulation(nc, m, sem, w):
    GM = 6 * D // COLS
    with ExitStack() as ctx:
        sb = lambda n, s: ctx.enter_context(nc.sbuf_tensor(n, s, F32))
        wt = sb("mod_w", [P, 4, KD, COLS])
        c_raw = sb("mod_c_raw", [P, 2, KD])
        c_act = sb("mod_c", [P, 2, KD])
        bias = sb("mod_bias", [2, 6 * D])
        row = sb("mod_row", [2, 2, COLS])
        first = sb("mod_first", [2, P])
        mod_all = sb("mod_all", [P, 4 * D])
        rows_ps = [ctx.enter_context(nc.psum_tensor(f"mod_rows_ps{j}", [2, COLS], F32)) for j in range(2)]
        out_ps = [ctx.enter_context(nc.psum_tensor(f"mod_out_ps{j}", [P, COLS], F32)) for j in range(2)]
        c_loaded, bias_loaded = sem("mod_c_loaded"), sem("mod_bias_loaded")
        c_ready = sem("mod_c_ready")
        first_ready = sem("mod_first_ready")
        masks_built = sem("masks_built")
        w_loaded = [sem(f"mod_w_loaded{j}") for j in range(4)]
        rows_done = sem("mod_rows_done")
        row_ready = sem("mod_row_ready")
        out_done = sem("mod_out_done")
        out_moved = sem("mod_out_moved")
        block = ctx.enter_context(nc.Block())
        wsrc = w["w_mod"][0].rearrange("(p k) n -> p k n", k=KD)

        @block.sync
        def _(sp):
            for j in range(4):
                sp.dma_start(wt[:, j, :, :], wsrc[:, :, j * COLS:(j + 1) * COLS]).then_inc(w_loaded[j], 16)
            with sp.Fori(1, GM // 4) as i:
                for j in range(4):
                    sp.wait_ge(rows_done, 4 * i + j - 3)
                    sp.dma_start(wt[:, j, :, :], wsrc[:, :, bass.ds((4 * i + j) * COLS, COLS)])\
                        .then_inc(w_loaded[j], 16)

        @block.scalar
        def _(act):
            act.dma_start(c_raw[:, 0, :], w["c"][0].rearrange("(p k) -> p k", k=KD)).then_inc(c_loaded, 16)
            act.dma_start(c_raw[:, 1, :], w["c_ctx"].rearrange("(p k) -> p k", k=KD)).then_inc(c_loaded, 16)
            act.dma_start(bias[0:1, :], w["b_mod"]).then_inc(bias_loaded, 16)
            act.dma_start(bias[1:2, :], w["b_mod"]).then_inc(bias_loaded, 16)
            act.wait_ge(c_loaded, 32)
            act.activation(c_act[:, :, :], c_raw[:, :, :], ACT.Silu).then_inc(c_ready, 1)
            for g in range(4):
                act.wait_ge(out_done, g + 1)
                act.activation(m.mod_col[:, 4 * g:4 * g + 4, :],
                               out_ps[g % 2][:, 0:8].rearrange("p (c s) -> p c s", s=2), ACT.Copy)\
                    .then_inc(out_moved, 1)
            with act.Fori(0, (GM - 4) // 2) as i:
                for j in range(2):
                    act.wait_ge(out_done, 2 * i + j + 5)
                    act.activation(mod_all[:, bass.ds((2 * i + j) * COLS, COLS)], out_ps[j][:, :], ACT.Copy)\
                        .then_inc(out_moved, 1)
            act.wait_ge(out_moved, GM)
            act.dma_start(m.mod_rows, mod_all[:, :]).then_inc(bias_loaded, 16)
            act.wait_ge(bias_loaded, 48)

        @block.gpsimd
        def _(pool):
            pool.affine_select(out=first[:, :], in_=m.ones[0:2, :], compare_op=ALU.is_equal, fill=0.0,
                               base=0, pattern=[[0, P]], channel_multiplier=1).then_inc(first_ready, 1)
            pool.wait_ge(first_ready, 1)
            build_masks(m, pool, masks_built)

        @block.tensor
        def _(pe):
            pe.wait_ge(c_ready, 1)
            pe.wait_ge(first_ready, 1)

            def rows(slot, round_, j, n):
                pe.wait_ge(w_loaded[slot], 16 * round_ + 16)
                for k in range(KD):
                    last = pe.matmul(rows_ps[j][:, :], c_act[:, :, k], wt[:, slot, k, :],
                                     start=(k == 0), stop=(k == KD - 1))
                last.then_inc(rows_done, 1)

            def columns(j, n):
                pe.wait_ge(row_ready, n + 1)
                if n >= 2:
                    pe.wait_ge(out_moved, n - 1)
                for q in range(4):
                    last = pe.transpose(out_ps[j][:, 2 * q:2 * q + 2], row[:, j, q * P:(q + 1) * P],
                                        m.ident[0:2, 0:2])
                last.then_inc(out_done, 1)

            def spread(j, n):
                pe.wait_ge(row_ready, n + 1)
                pe.wait_ge(out_moved, n - 1)
                pe.matmul(out_ps[j][:, :], first[:, :], row[:, j, :], start=True, stop=True)\
                    .then_inc(out_done, 1)

            for n in range(4):
                rows(n, 0, n % 2, n)
                columns(n % 2, n)
            with pe.Fori(1, GM // 4) as i:
                for j in range(4):
                    rows(j, i, j % 2, 4 * i + j)
                    spread(j % 2, 4 * i + j)

        @block.vector
        def _(dve):
            dve.wait_ge(bias_loaded, 32)
            with dve.Fori(0, GM // 2) as i:
                for j in range(2):
                    dve.wait_ge(rows_done, 2 * i + j + 1)
                    dve.tensor_tensor(row[:, j, :], rows_ps[j][:, :],
                                      bias[:, bass.ds((2 * i + j) * COLS, COLS)], ALU.add).then_inc(row_ready, 1)
            dve.wait_ge(out_moved, 4)
            dve.scalar_tensor_tensor(out=m.a1[:, :, :], in0=m.mod_col[:, KD:2 * KD, :], scalar=1.0,
                                     in1=m.vec[:, :, GN1:GN1 + 1].to_broadcast([P, KD, 2]),
                                     op0=ALU.add, op1=ALU.mult).then_inc(row_ready, 1)
            dve.wait_ge(row_ready, GM + 1)


def norm_in(nc, m, sem, w):
    with ExitStack() as ctx:
        sb = lambda n, s: ctx.enter_context(nc.sbuf_tensor(n, s, F32))
        xt = sb("nin_x", [P, 2, D])
        sq = sb("nin_sq", [P, 2, D])
        xn = sb("nin_xn", [P, 2, D])
        st = sb("nin_stat", [P, 3, 2])
        ps = [ctx.enter_context(nc.psum_tensor(f"nin_ps{j}", [P, D], F32)) for j in range(2)]
        x_loaded = [sem(f"nin_x_loaded{j}") for j in range(2)]
        stat, xn_ready, turned, moved, split_hi, split_lo, kept = (sem(f"nin_{n}") for n in (
            "stat", "xn_ready", "turned", "moved", "split_hi", "split_lo", "kept"))
        block = ctx.enter_context(nc.Block())

        @block.sync
        def _(sp):
            def load(src, pair, tile):
                for j in range(2):
                    if not isinstance(pair, int):
                        sp.wait_ge(xn_ready, 2 * pair + j - 1)
                    sp.dma_start(xt[:, j, :], src[bass.ds((tile + j) * P, P), :]).then_inc(x_loaded[j], 16)

            def keep(pair):
                sp.wait_ge(moved, 2 * pair + 2)
                cols = bass.ds(pair * (2 * P), 2 * P)
                sp.dma_start(m.h_kept[:, :, cols], m.h_t[:, :, cols]).then_inc(kept, 16)
            load(w["ctx"][0], 0, 0)
            with sp.Fori(1, NT // 2) as i:
                load(w["x"][0], i, 2 * i - 2)
                keep(i - 1)
            keep(NT // 2 - 1)
            sp.wait_ge(kept, 16 * (NT // 2))

        @block.scalar
        def _(act):
            def normalise(i):
                for j in range(2):
                    act.wait_ge(x_loaded[j], 16 * i + 16)
                    act.activation(sq[:, j, :], xt[:, j, :], ACT.Square, accum_out=st[:, 0, j:j + 1]).then_inc(stat, 1)
                act.wait_ge(stat, 4 * i + 2)
                act.activation(st[:, 1, :], st[:, 0, :], ACT.Ln, bias=m.eps[:, 0:1], scale=1.0 / D).then_inc(stat, 1)
                act.wait_ge(stat, 4 * i + 3)
                act.activation(st[:, 2, :], st[:, 1, :], ACT.Exp, scale=-0.5).then_inc(stat, 1)
                act.wait_ge(stat, 4 * i + 4)
                for j in range(2):
                    if not isinstance(i, int):
                        act.wait_ge(turned, 2 * i + j - 1)
                    act.activation(xn[:, j, :], xt[:, j, :], ACT.Copy, scale=st[:, 2, j:j + 1]).then_inc(xn_ready, 1)
            normalise(0)
            with act.Fori(1, NT // 2) as i:
                normalise(i)

        @block.tensor
        def _(pe):
            def turn(i):
                for j in range(2):
                    pe.wait_ge(xn_ready, 2 * i + j + 1)
                    if not isinstance(i, int):
                        pe.wait_ge(moved, 2 * i + j - 1)
                    for k in range(KD):
                        last = pe.transpose(ps[j][:, k * P:(k + 1) * P], xn[:, j, k * P:(k + 1) * P], m.ident[:, :])
                    last.then_inc(turned, 1)
            turn(0)
            with pe.Fori(1, NT // 2) as i:
                turn(i)

        @block.vector
        def _(dve):

            def leave(i, stream):
                for j in range(2):
                    dve.wait_ge(turned, 2 * i + j + 1)
                    for k in range(KD):
                        last = dve.tensor_scalar(m.h_t[:, k, bass.ds((2 * i + j) * P, P)], ps[j][:, k * P:(k + 1) * P],
                                                 m.a1[:, k, stream:stream + 1], m.mod_col[:, k, stream:stream + 1],
                                                 ALU.mult, ALU.add)
                    last.then_inc(moved, 1)
                    n = 2 * i + j
                    here = bass.ds(n * P, P)
                    dve.wait_ge(moved, n + 1)
                    dve.tensor_copy(m.h_hi[:, :, here], m.h_t[:, :, here]).then_inc(split_hi, 1)
            leave(0, 1)
            with dve.Fori(1, NT // 2) as i:
                leave(i, 0)
            dve.wait_ge(split_hi, NT)

        @block.gpsimd
        def _(pool):
            with pool.Fori(0, NT) as n:
                here = bass.ds(n * P, P)
                pool.wait_ge(split_hi, n + 1)
                pool.tensor_tensor(m.h_lo[:, :, here], m.h_t[:, :, here], m.h_hi[:, :, here].bitcast(F32),
                                   ALU.subtract).then_inc(split_lo, 1)
            pool.wait_ge(split_lo, NT)


def project_qk(nc, m, sem, w):
    LAT, C0 = SEQ, SEQ
    IW = GRID_W + 2
    with ExitStack() as ctx:
        sb = lambda n, s: ctx.enter_context(nc.sbuf_tensor(n, s, F32))
        wt = sb("qk_w", [P, 2, KD, P])
        img = sb("qk_img", [P, 2, (GRID_H + 2) * IW])
        line = sb("qk_line", [P, 2, CTX + 2])
        acc = sb("qk_acc", [P, 2, T])
        ps = [ctx.enter_context(nc.psum_tensor(f"qk_ps{j}", [P, 3 * 512], F32)) for j in range(2)]
        w_loaded = [sem(f"qk_w_loaded{j}") for j in range(2)]
        made, left_m, left_g, tap, conv, done = (sem(f"qk_{n}") for n in
                                                 ("made", "left_m", "left_g", "tap", "conv", "done"))
        cleared = sem("qk_cleared")
        PARTS = [(0, CTX, 512), (512, CTX + 512, 512), (C0, 0, CTX)]
        h_loaded = [sem(f"qk_h_loaded{part}") for part in range(3)]
        block = ctx.enter_context(nc.Block())
        wsrc = w["w_in"][0].rearrange("(k p) n -> p k n", p=P)
        PLAN = [(0, 0, 0), (0, 0, 1), (0, 1, (2, 4)), (1, 0, 4), (1, 0, 5), (1, 1, (6, 8))]

        def each(eng, body):
            for mixer, is_k, pairs in PLAN:
                if isinstance(pairs, int):
                    body(pairs, mixer, is_k, pairs)
                else:
                    with eng.Fori(*pairs) as i:
                        body(i, mixer, is_k, pairs[0])

        @block.sync
        def _(sp):
            def load(i, mixer, is_k, first):
                for j in range(2):
                    if first > 0:
                        sp.wait_ge(made, 2 * i + j - 1)
                    col = (2 * i + j) * P + (QG - 2 * COLS if mixer else QM)
                    sp.dma_start(wt[:, j, :, :], wsrc[:, :, bass.ds(col, P)]).then_inc(w_loaded[j], 16)
                    if isinstance(i, int) and i == 0 and j == 0:
                        for part, (_, t0, n) in enumerate(PARTS):
                            sp.dma_start(m.h_t[:, :, t0:t0 + n], m.h_kept[:, :, t0:t0 + n])\
                                .then_inc(h_loaded[part], 16)
            each(sp, load)

        @block.gpsimd
        def _(pool):
            pool.memset(img[:, :, :], 0.0).then_inc(cleared, 1)
            pool.memset(line[:, :, :], 0.0).then_inc(cleared, 1)

        @block.tensor
        def _(pe):
            def multiply(i, mixer, is_k, first):
                for j in range(2):
                    pe.wait_ge(w_loaded[j], 16 * i + 16)
                    if first == 4:
                        pe.wait_ge(left_m, 8)
                    elif mixer:
                        pe.wait_ge(left_g, 2 * i + j - 9)
                    elif first > 0:
                        pe.wait_ge(left_m, 2 * i + j - 1)
                    for part, (at, t0, n) in enumerate(PARTS if is_k else PARTS[:2]):
                        if (isinstance(i, int) and i == 0 and j == 0) or part == 2:
                            pe.wait_ge(h_loaded[part], 16)
                        for k in range(KD):
                            last = pe.matmul(ps[j][:, at:at + n], wt[:, j, k, :], m.h_t[:, k, t0:t0 + n],
                                             start=(k == 0), stop=(k == KD - 1))
                    last.then_inc(made, 1)
            each(pe, multiply)

        @block.vector
        def _(dve):
            dve.wait_ge(cleared, 2)

            def convolve(i, mixer, is_k, first):
                if mixer:
                    return
                for j in range(2):
                    n = 2 * i + j
                    dve.wait_ge(made, n + 1)
                    v = img[:, j, :].rearrange("p (y x) -> p y x", x=IW)
                    dve.tensor_copy(v[:, 1:GRID_H + 1, 1:GRID_W + 1],
                                    ps[j][:, 0:LAT].rearrange("p (y x) -> p y x", x=GRID_W)).then_inc(tap, 1)
                    if is_k:
                        dve.tensor_copy(line[:, j, 1:CTX + 1], ps[j][:, C0:C0 + CTX]).then_inc(tap, 1)
                    before = 10 * n if not is_k else 40 + 14 * (n - 4)
                    dve.wait_ge(tap, before + 1 + is_k)
                    dve.sem_inc(left_m, 1)
                    if first > 0:
                        dve.wait_ge(done, n - 1)
                    out = acc[:, j, CTX:T].rearrange("p (y x) -> p y x", x=GRID_W)
                    taps = [(out, v[:, dy:dy + GRID_H, dx:dx + GRID_W], 3 * dy + dx, dy == 0 and dx == 0)
                            for dy in range(3) for dx in range(3)]
                    if is_k:
                        taps += [(acc[:, j, 0:CTX], line[:, j, dx:dx + CTX], 3 + dx, dx == 0) for dx in range(3)]
                    count = before + 1 + is_k
                    for o, src, tp, start in taps:
                        wcol = m.vec[:, bass.ds(n, 1), tp:tp + 1].rearrange("p a b -> p (a b)")
                        if start:
                            ins = dve.tensor_scalar(o, src, wcol, None, ALU.mult)
                        else:
                            dve.wait_ge(tap, count)
                            ins = dve.scalar_tensor_tensor(out=o, in0=src, scalar=wcol, in1=o,
                                                           op0=ALU.mult, op1=ALU.add)
                        ins.then_inc(tap, 1)
                        count = count + 1
                    dve.wait_ge(tap, count)
                    dve.sem_inc(conv, 1)
            each(dve, convolve)

        @block.scalar
        def _(act):
            def finish(i, mixer, is_k, first):
                for j in range(2):
                    n = 2 * i + j
                    ch = n - (4 if is_k else 0) - (8 if mixer else 0)
                    dst = [[m.qm, m.km], [m.qg, m.kg]][mixer][is_k]
                    if not mixer:
                        act.wait_ge(conv, n + 1)
                        t0, t1 = (0, T) if is_k else (CTX, T)
                        act.activation(dst[:, bass.ds(ch, 1), :].rearrange("p a t -> p (a t)"), acc[:, j, t0:t1],
                                       ACT.Silu, bias=m.vec[:, bass.ds(n, 1), CONV_B:CONV_B + 1]
                                       .rearrange("p a b -> p (a b)")).then_inc(done, 1)
                    else:
                        act.wait_ge(made, n + 1)
                        scale = 1.0 if is_k else float(DK) ** -0.5
                        off = CTX if is_k else 0
                        ins = act.activation(dst[:, bass.ds(ch, 1), off:off + SEQ].rearrange("p a t -> p (a t)"),
                                             ps[j][:, 0:LAT], ACT.Copy, scale=scale)
                        if is_k:
                            ins = act.activation(dst[:, bass.ds(ch, 1), 0:CTX].rearrange("p a t -> p (a t)"),
                                                 ps[j][:, C0:C0 + CTX], ACT.Copy)
                        ins.then_inc(left_g, 1)
            each(act, finish)
            act.wait_ge(done, 8)
            act.wait_ge(left_g, 8)


def project_small(nc, m, sem, w):
    with ExitStack() as ctx:
        sb = lambda n, s: ctx.enter_context(nc.sbuf_tensor(n, s, F32))
        wt = sb("small_w", [P, KD, SMALL])
        bias = sb("small_bias", [GATE_ROWS, 2])
        ps = ctx.enter_context(nc.psum_tensor("small_ps", [P, 3 * 512], F32))
        cleared, loaded, bias_loaded, made, done = (sem(f"small_{n}") for n in
                                                    ("cleared", "loaded", "bias_loaded", "made", "done"))
        block = ctx.enter_context(nc.Block())
        wsrc = w["w_in"][0].rearrange("(k p) n -> p k n", p=P)

        @block.gpsimd
        def _(pool):
            pool.memset(wt[:, :, :], 0.0).then_inc(cleared, 1)
            pool.memset(bias[:, :], 0.0).then_inc(cleared, 1)
            pool.memset(m.w2[:, :, :], 0.0).then_inc(cleared, 1)

        @block.sync
        def _(sp):
            sp.wait_ge(cleared, 3)
            for at, col, n in [(0, GATE, 4), (16, LR, RANK), (32, GATE + 8, 4), (48, LR + RANK, RANK),
                               (64, GATE + 4, 4), (96, GATE + 12, 4)]:
                sp.dma_start(wt[:, :, at:at + n], wsrc[:, :, col:col + n]).then_inc(loaded, 16)
            for row, c, at in [(0, 0, 0), (32, 0, 8), (0, 1, 4), (32, 1, 12)]:
                sp.dma_start(bias[row:row + 4, c:c + 1],
                             w["b_mgate"][0, at:at + 4].rearrange("(p a) -> p a", a=1)).then_inc(bias_loaded, 16)
            for d in range(2):
                sp.dma_start(m.w2[16:32, d, :], w["gla_w2"][0, d]).then_inc(bias_loaded, 16)

        @block.tensor
        def _(pe):
            pe.wait_ge(loaded, 16 * 6)
            for t0, n in [(0, 512), (512, 512), (1024, 256)]:
                for k in range(KD):
                    last = pe.matmul(ps[0:SMALL, t0:t0 + n], wt[:, k, :], m.h_t[:, k, t0:t0 + n],
                                     start=(k == 0), stop=(k == KD - 1))
            last.then_inc(made, 1)

        @block.scalar
        def _(act):
            act.wait_ge(made, 1)
            act.wait_ge(bias_loaded, 16 * 6)
            act.activation(m.gate_i[:, :], ps[0:GATE_ROWS, 0:T], ACT.Identity, bias=bias[:, 0:1]).then_inc(done, 1)
            act.activation(m.gate_f[:, :], ps[64:64 + GATE_ROWS, 0:T], ACT.Identity, bias=bias[:, 1:2]).then_inc(done, 1)
            act.wait_ge(done, 4)

        @block.vector
        def _(dve):
            dve.wait_ge(done, 2)
            for d in range(2):
                dve.tensor_copy(m.lr[:, d, :], ps[32 * d:32 * d + 32, 0:T]).then_inc(done, 1)


def project_rows(nc, m, sem, w):
    PS = 4
    PLAN = [(0, VM, 0, 1, ACT.Copy, m.vals[0:1]), (0, VG, 0, 1, ACT.Copy, m.vals[1:2]),
            (NC, OM, 0, 1, ACT.Sigmoid, m.gates[0:1]), (NC, RG, 0, 1, ACT.Silu, m.gates[1:2]),
            (NC, MGM, MGG - MGM, 2, ACT.Sigmoid, m.gates[2:4])]
    with ExitStack() as ctx:
        sb = lambda n, s, dt=F32: ctx.enter_context(nc.sbuf_tensor(n, s, dt))
        raw = sb("rows_w", [P, KD, COLS])
        w_hi = sb("rows_w_hi", [P, 2, KD, COLS], F32R)
        w_lo = sb("rows_w_lo", [P, 2, KD, COLS], F32R)
        stage = sb("rows_stage", [P, PS, COLS])
        ps = [ctx.enter_context(nc.psum_tensor(f"rows_ps{j}", [P, COLS], F32)) for j in range(PS)]
        PART = (slice(0, KD // 2), slice(KD // 2, KD))
        w_loaded, hi_done, lo_done = ([sem(f"rows_{n}{x}") for x in range(2)] for n in (
            "w_loaded", "hi_done", "lo_done"))
        stored = [sem(f"rows_stored{j}") for j in range(PS)]
        made, moved = sem("rows_made"), sem("rows_moved")
        block = ctx.enter_context(nc.Block())
        wsrc = w["w_in"][0].rearrange("(k p) n -> p k n", p=P)

        def each(eng, body):
            at = base = prev = 0
            for first, col, step, n, func, dst in PLAN:
                chunks = range(first, NT)
                per = 2 * len(chunks)
                assert per % PS == 0
                if n == 1:
                    body(at, base, prev, 0, chunks, col, func, dst)
                else:
                    assert prev == len(chunks)
                    with eng.Fori(0, n) as i:
                        body(at + i, i * per + base, prev, i, chunks, col + step * i, func, dst)
                at, base, prev = at + n, base + n * per, len(chunks)
            return base

        @block.sync
        def _(sp):
            def load(r, base, prev, i, chunks, col, func, dst):
                for j in range(2):
                    for x in range(2):
                        if j or not (isinstance(r, int) and r == 0):
                            sp.wait_ge(lo_done[x], 2 * r + j)
                        sp.dma_start(raw[:, PART[x], :], wsrc[:, PART[x], bass.ds(col + COLS * j, COLS)])\
                            .then_inc(w_loaded[x], 16)
            each(sp, load)

        @block.tensor
        def _(pe):
            def multiply(r, base, prev, i, chunks, col, func, dst):
                for j in range(2):
                    for q, t in enumerate(chunks):
                        n = base + (len(chunks) * j + q)
                        s = (len(chunks) * j + q) % PS
                        if not (isinstance(n, int) and n < PS):
                            pe.wait_ge(moved, n - PS + 1)
                        for k in range(KD):
                            if q == 0 and k % (KD // 2) == 0:
                                pe.wait_ge(lo_done[k // (KD // 2)], 2 * r + j + 1)
                            h_hi, h_lo = (h[:, k, t * P:(t + 1) * P] for h in (m.h_hi, m.h_lo))
                            pe.matmul(ps[s][:, :], h_hi, w_hi[:, j, k, :], start=(k == 0), stop=False)
                            pe.matmul(ps[s][:, :], h_hi, w_lo[:, j, k, :], start=False, stop=False)
                            last = pe.matmul(ps[s][:, :], h_lo, w_hi[:, j, k, :], start=False, stop=(k == KD - 1))
                        last.then_inc(made, 1)
            each(pe, multiply)

        @block.vector
        def _(dve):
            def split(r, base, prev, i, chunks, col, func, dst):
                for j in range(2):
                    if not (isinstance(r, int) and r == 0):
                        dve.wait_ge(made, base - (1 - j) * prev)
                    for x in range(2):
                        dve.wait_ge(w_loaded[x], 32 * r + 16 * j + 16)
                        dve.tensor_copy(w_hi[:, j, PART[x], :], raw[:, PART[x], :]).then_inc(hi_done[x], 1)
                        dve.wait_ge(hi_done[x], 2 * r + j + 1)
                        dve.tensor_tensor(w_lo[:, j, PART[x], :], raw[:, PART[x], :],
                                          w_hi[:, j, PART[x], :].bitcast(F32), ALU.subtract).then_inc(lo_done[x], 1)
            each(dve, split)

        @block.scalar
        def _(act):
            def move(r, base, prev, i, chunks, col, func, dst):
                for j in range(2):
                    for q in range(len(chunks)):
                        n = base + (len(chunks) * j + q)
                        s = (len(chunks) * j + q) % PS
                        act.wait_ge(made, n + 1)
                        if not (isinstance(n, int) and n < PS):
                            act.wait_ge(stored[s], base * (16 // PS) + 16 * ((len(chunks) * j + q) // PS))
                        act.activation(stage[:, s, :], ps[s][:, :], func).then_inc(moved, 1)
            each(act, move)

        @block.gpsimd
        def _(pool):
            def store(r, base, prev, i, chunks, col, func, dst):
                for j in range(2):
                    for q in range(len(chunks)):
                        n = base + (len(chunks) * j + q)
                        s = (len(chunks) * j + q) % PS
                        pool.wait_ge(moved, n + 1)
                        rows = dst[bass.ds(i, 1), q * P:(q + 1) * P, j * COLS:(j + 1) * COLS]
                        pool.dma_start(rows.rearrange("a p n -> p (a n)"), stage[:, s, :]).then_inc(stored[s], 16)
            tiles = each(pool, store)
            for s in range(PS):
                pool.wait_ge(stored[s], 16 * (tiles // PS))


def gate_rows(nc, m, sem, w):
    R = GATE_ROWS
    with ExitStack() as ctx:
        sb = lambda n, s: ctx.enter_context(nc.sbuf_tensor(n, s, F32))
        lf = sb("gr_logf", [R, T])
        tmp = sb("gr_tmp", [R, T])
        b = sb("gr_b", [R, T])
        mx = sb("gr_max", [R, T])
        wsrc = sb("gr_wstate", [R, T])
        emt = sb("gr_emt", [R, T])
        prev = sb("gr_prev", [R, NT])
        end = sb("gr_end", [R, NT])
        dec = sb("gr_dec", [R, NT])
        cols = [ctx.enter_context(nc.psum_tensor(f"gr_cols{q}", [P, NT, GATE_ROWS], F32)) for q in range(3)]
        decps = ctx.enter_context(nc.psum_tensor("gr_decps", [P, 2 * HEADS, NT], F32))
        step, actd, turned, moved = (sem(f"gr_{n}") for n in ("step", "act_step", "turned", "moved"))
        block = ctx.enter_context(nc.Block())
        FW, BW = slice(0, HEADS), slice(32, 32 + HEADS)
        chunks = lambda a: a[:, :].rearrange("p (c t) -> p c t", t=P)
        across = lambda a: a[:, :].rearrange("p (c a) -> p c a", a=1).to_broadcast([R, NT, P])

        @block.scalar
        def _(act):
            n = [0]

            def then(ins):
                n[0] += 1
                ins.then_inc(actd, 1)
                act.wait_ge(actd, n[0])
            then(act.activation(tmp[:, :], m.gate_f[:, :], ACT.Abs))
            then(act.activation(tmp[:, :], tmp[:, :], ACT.Exp, scale=-1.0))
            then(act.activation(tmp[:, :], tmp[:, :], ACT.Ln, bias=1.0))
            act.wait_ge(step, 13)
            then(act.activation(emt[:, :], mx[:, :], ACT.Exp, scale=-1.0))
            act.wait_ge(step, 18)
            then(act.activation(m.w_inter[:, :], m.w_inter[:, :], ACT.Exp))
            then(act.activation(wsrc[:, :], wsrc[:, :], ACT.Exp))
            then(act.activation(dec[:, :], dec[:, :], ACT.Exp))

        @block.vector
        def _(dve):
            n = [0]

            def then(ins):
                n[0] += 1
                ins.then_inc(step, 1)
                dve.wait_ge(step, n[0])
            then(dve.memset(prev[:, :], NEG_BIG))
            then(dve.memset(mx[:, :], 0.0))
            dve.wait_ge(actd, 3)
            then(dve.scalar_tensor_tensor(out=lf[:, :], in0=m.gate_f[:, :], scalar=0.0, in1=tmp[:, :],
                                          op0=ALU.min, op1=ALU.subtract))
            then(dve.tensor_tensor_scan(mx[FW, :], lf[FW, :], m.gate_i[FW, :], NEG_BIG, ALU.add, ALU.max))
            then(dve.tensor_tensor_scan(mx[BW, CTX - 1::-1], lf[BW, CTX - 1::-1], m.gate_i[BW, CTX - 1::-1],
                                        NEG_BIG, ALU.add, ALU.max))
            then(dve.tensor_tensor_scan(mx[BW, T - 1:CTX - 1:-1], lf[BW, T - 1:CTX - 1:-1],
                                        m.gate_i[BW, T - 1:CTX - 1:-1], mx[BW, 0:1], ALU.add, ALU.max))
            then(dve.memset(b[:, :], 0.0))
            for half in (slice(0, T // 2), slice(T // 2, T)):
                bh, lh = b[:, half], lf[:, half]
                dve.tensor_tensor_scan(bh[FW], m.restart[FW, 0, :], lh[FW], 0.0, ALU.mult, ALU.add)\
                    .then_inc(moved, 1)
                dve.tensor_tensor_scan(bh[BW, ::-1], m.restart[BW, 1, ::-1], lh[BW, ::-1], 0.0,
                                       ALU.mult, ALU.add).then_inc(moved, 1)
            dve.wait_ge(moved, 4)
            mv = chunks(mx)
            then(dve.tensor_copy(prev[FW, 1:NT], mv[FW, 0:NT - 1, P - 1]))
            then(dve.tensor_copy(prev[BW, 0:NC - 1], mv[BW, 1:NC, 0]))
            then(dve.tensor_copy(prev[BW, NT - 1:NT], mv[BW, 0:1, 0]))
            then(dve.tensor_copy(prev[BW, NC:NT - 1], mv[BW, NC + 1:NT, 0]))
            then(dve.tensor_tensor(m.gate_g[:, :], m.gate_i[:, :], b[:, :], ALU.subtract))
            then(dve.tensor_tensor(m.neg_m[:, :], b[:, :], mx[:, :], ALU.subtract))
            then(dve.tensor_tensor(chunks(m.w_inter), chunks(m.neg_m), across(prev), ALU.add))
            then(dve.memset(end[:, :], 0.0))
            nv = chunks(m.neg_m)
            then(dve.tensor_copy(end[FW, :], nv[FW, :, P - 1]))
            dve.tensor_copy(end[BW, :], nv[BW, :, 0]).then_inc(moved, 1)
            dve.wait_ge(moved, 5)
            dve.tensor_tensor(chunks(wsrc), chunks(m.gate_g), across(end), ALU.add).then_inc(step, 1)
            dve.tensor_tensor(dec[:, :], end[:, :], prev[:, :], ALU.add).then_inc(step, 1)
            dve.wait_ge(turned, 1)
            dve.tensor_copy(m.g_col[:, :, :], cols[0][:, :, :]).then_inc(moved, 1)
            dve.tensor_copy(m.ws_col[:, :, :], cols[1][:, :, :]).then_inc(moved, 1)
            dve.tensor_copy(m.emt_col[:, :, :], cols[2][:, :, :]).then_inc(moved, 1)
            dve.tensor_copy(m.dec_all[:, :, :], decps[:, :, :]).then_inc(moved, 1)
            dve.wait_ge(moved, 9)

        @block.tensor
        def _(pe):
            pe.wait_ge(actd, 7)
            pe.wait_ge(step, 18)
            for q, src in enumerate((m.gate_g, wsrc, emt)):
                for c in range(NT):
                    pe.transpose(cols[q][:, c, :], src[:, c * P:(c + 1) * P], m.ident[0:R, 0:R])
            for r in range(2 * HEADS):
                last = pe.matmul(decps[:, r, :], m.row_of[:, r, :], dec[:, :], start=True, stop=True)
            last.then_inc(turned, 1)


def scan_rows(sp, load, rows, dst, added, stored):
    middle = NC + NL // 2
    other = lambda i: i * -1 + (NT - 1 + NC)

    def both(i):
        load(2 * i, i, i, 0, True, None)
        load(2 * i + 1, i, other(i), 1, True, None)

    def store(i):
        sp.wait_ge(added, 2 * i - 2 * NC + 2)
        for c in (i, other(i)):
            tile = bass.ds(c - NC, 1)
            sp.dma_start(dst[bass.ds(c * P - CTX, P), :], rows[:, tile, :].rearrange("p a n -> p (a n)"))\
                .then_inc(stored, 16)
    for i in range(NC):
        load(2 * i, i, i, 0, False, None)
        load(2 * i + 1, i, NC - 1 - i, 1, False, None)
    with sp.Fori(NC, middle + 1) as i:
        both(i)
    with sp.Fori(middle + 1, NT) as i:
        both(i)
        store(i - 1)
    store(NT - 1)
    sp.wait_ge(stored, 16 * NL)


def mlstm_scan(nc, m, sem, w):
    SC = float(DK) ** -0.5
    with ExitStack() as ctx:
        sb = lambda n, s: ctx.enter_context(nc.sbuf_tensor(n, s, F32))
        bank = lambda n, k=1: ctx.enter_context(nc.psum_tensor(n, [P, k * 512], F32))
        v = sb("ml_v", [P, 2, D])
        ks = sb("ml_k", [P, 2, HEADS, P])
        expo = sb("ml_expo", [P, 2, HEADS, P])
        wt = sb("ml_wt", [P, 2, HEADS, P])
        qi = sb("ml_qi", [P, 2, HEADS, P])
        kw = sb("ml_kw", [P, 2, HEADS, P])
        den = sb("ml_den", [P, 2, HEADS])
        cmat = sb("ml_c", [P, 2, D])
        nvec = sb("ml_n", [P, 2, HEADS])
        hm = sb("ml_h", [P, NL, D])
        s_ps, m_ps, t_ps = bank("ml_s_ps"), bank("ml_m_ps"), bank("ml_t_ps")
        num_ps, st_ps, small_ps = bank("ml_num_ps", 2), bank("ml_st_ps", 2), bank("ml_small_ps")
        v_loaded = [sem(f"ml_v_loaded{d}") for d in range(2)]
        (cleared, k_ready, scores, maxes, inters, keys_t, expo_ready, masked, exp_ready, w_ready, qi_ready,
         kw_ready, out_made, state_made, c_ready, h_added, den_step, n_step, stored) = (
            sem(f"ml_{n}") for n in (
                "cleared", "k_ready", "scores", "maxes", "inters", "keys_t", "expo_ready", "masked", "exp_ready",
                "w_ready", "qi_ready", "kw_ready", "out_made", "state_made", "c_ready", "h_added", "den_step",
                "n_step", "stored"))
        mask_begun = sem("ml_mask_begun")
        block = ctx.enter_context(nc.Block())
        heads = lambda ap: ap.rearrange("p (h n) -> p h n", h=HEADS)

        def steps(eng, body):
            body(0, 0, 0, 0, False, None)
            body(1, 0, NC - 1, 1, False, None)
            body(2, 1, 1, 0, False, None)
            body(3, 1, NC - 2, 1, False, NC)
            with eng.Fori(NC, NT - 1) as i:
                back = i * -1 + (NT - 1 + NC)
                body(2 * i, i, i, 0, True, back)
                body(2 * i + 1, i, back, 1, True, i + 1)
            body(2 * NT - 2, NT - 1, NT - 1, 0, True, NC)
            body(2 * NT - 1, NT - 1, NC, 1, True, None)

        assert NC == 2

        @block.sync
        def _(sp):
            def load(u, i, c, d, out, following):
                if not (isinstance(i, int) and i == 0):
                    sp.wait_ge(state_made, u - 1)
                sp.dma_start(v[:, d, :], m.vals[0, bass.ds(c * P, P), :]).then_inc(v_loaded[d], 16)
            scan_rows(sp, load, hm, m.hm, h_added, stored)

        @block.gpsimd
        def _(pool):
            pool.memset(cmat[:, :, :], 0.0).then_inc(cleared, 1)
            pool.memset(nvec[:, :, :], 0.0).then_inc(cleared, 1)
            pool.memset(hm[:, :, :], 0.0).then_inc(cleared, 1)

            def mask(u, i, c, d, out, following):
                if out:
                    n = u - 2 * NC
                    pool.wait_ge(expo_ready, n + 1)
                    pool.sem_inc(mask_begun, 1)
                    sign = 1 - 2 * d
                    pool.affine_select(out=expo[:, d, :, :], in_=expo[:, d, :, :], compare_op=ALU.is_ge,
                                       fill=NEG_BIG, base=0, pattern=[[0, HEADS], [sign, P]],
                                       channel_multiplier=-sign).then_inc(masked, 1)
            steps(pool, mask)

        @block.scalar
        def _(act):
            def stage(u, i, c, d, out, following):
                if not (isinstance(i, int) and i == 0):
                    act.wait_ge(keys_t, u - 1)
                act.activation(ks[:, d, :, :], m.km[:, :, bass.ds(c * P, P)], ACT.Copy, scale=SC).then_inc(k_ready, 1)
                if out:
                    n = u - 2 * NC
                    act.wait_ge(masked, n + 1)
                    act.activation(expo[:, d, :, :], expo[:, d, :, :], ACT.Exp).then_inc(exp_ready, 1)
            steps(act, stage)

        @block.tensor
        def _(pe):
            def chunk(u, i, c, d, out, following):
                n = u - 2 * NC
                after_first = not (isinstance(u, int) and u == 0)
                if out:
                    pe.wait_ge(qi_ready, n + 1)
                else:
                    pe.wait_ge(k_ready, u + 1)
                    if after_first:
                        pe.wait_ge(kw_ready, u)
                for h in range(HEADS):
                    last = pe.transpose(t_ps[:, h * P:(h + 1) * P], ks[:, d, h, :], m.ident[:, :])
                last.then_inc(keys_t, 1)
                if following is not None:
                    tok = bass.ds(following * P, P)
                    if out:
                        pe.wait_ge(expo_ready, n + 1)
                    for h in range(HEADS):
                        last = pe.matmul(m_ps[:, h * P:(h + 1) * P], m.row_of[:, HEADS * (1 - d) + h, :],
                                         m.neg_m[:, tok], start=True, stop=True)
                    last.then_inc(maxes, 1)
                    pe.wait_ge(kw_ready, u + 1)
                    for h in range(HEADS):
                        last = pe.matmul(t_ps[:, h * P:(h + 1) * P], m.row_of[:, HEADS * (1 - d) + h, :],
                                         m.w_inter[:, tok], start=True, stop=True)
                    last.then_inc(inters, 1)
                pe.wait_ge(v_loaded[d], 16 * i + 16)
                if after_first:
                    pe.wait_ge(c_ready, u)
                else:
                    pe.wait_ge(cleared, 3)
                pe.wait_ge(kw_ready, u + 1)
                for h in range(HEADS):
                    pe.matmul(small_ps[:, 8 + h:9 + h], kw[:, d, h, :], m.ones[:, 0:1], start=True, stop=True)
                if out:
                    pe.wait_ge(w_ready, n + 1)
                    for h in range(HEADS):
                        o = small_ps[:, h:h + 1]
                        pe.matmul(o, wt[:, d, h, :], m.ones[:, 0:1], start=True, stop=False)
                        pe.matmul(o, qi[:, d, h, :], nvec[:, d, h:h + 1], start=False, stop=True)
                    for h in range(HEADS):
                        o = num_ps[:, h * DV:(h + 1) * DV]
                        pe.matmul(o, wt[:, d, h, :], v[:, d, h * DV:(h + 1) * DV], start=True, stop=False)
                        last = pe.matmul(o, qi[:, d, h, :], cmat[:, d, h * DV:(h + 1) * DV], start=False, stop=True)
                    last.then_inc(out_made, 1)
                for h in range(HEADS):
                    last = pe.matmul(st_ps[:, h * DV:(h + 1) * DV], kw[:, d, h, :], v[:, d, h * DV:(h + 1) * DV],
                                     start=True, stop=True)
                last.then_inc(state_made, 1)
                if following is not None:
                    pe.wait_ge(k_ready, u + 2)
                    for h in range(HEADS):
                        last = pe.matmul(s_ps[:, h * P:(h + 1) * P], ks[:, 1 - d, h, :],
                                         m.qm[:, h, bass.ds(following * P - CTX, P)], start=True, stop=True)
                    last.then_inc(scores, 1)
            steps(pe, chunk)

        @block.vector
        def _(dve):
            def chunk(u, i, c, d, out, following):
                n = u - 2 * NC
                ci = bass.ds(c, 1)

                def per_key(a, at, direction, width):
                    gcol = slice(32 * direction, 32 * direction + HEADS)
                    return a[:, at, gcol].rearrange("p a (h n) -> p (a h) n", n=1).to_broadcast([P, HEADS, width])
                dve.wait_ge(keys_t, u + 1)
                dve.tensor_tensor(kw[:, d, :, :], heads(t_ps[:, :]), per_key(m.ws_col, ci, d, P), ALU.mult)\
                    .then_inc(kw_ready, 1)
                if out:
                    dve.wait_ge(exp_ready, n + 1)
                    dve.wait_ge(scores, n + 1)
                    dve.tensor_tensor(wt[:, d, :, :], heads(s_ps[:, :]), expo[:, d, :, :], ALU.mult)\
                        .then_inc(w_ready, 1)
                if following is not None:
                    dve.wait_ge(maxes, n + 2)
                    dve.tensor_tensor(expo[:, 1 - d, :, :], heads(m_ps[:, :]),
                                      per_key(m.g_col, bass.ds(following, 1), 1 - d, P), ALU.add)\
                        .then_inc(expo_ready, 1)
                    dve.wait_ge(inters, n + 2)
                    dve.tensor_tensor(qi[:, 1 - d, :, :], m.qm[:, :, bass.ds(following * P - CTX, P)],
                                      heads(t_ps[:, :]), ALU.mult).then_inc(qi_ready, 1)
                if out:
                    dve.wait_ge(out_made, n + 1)
                    dn = den[:, d, :]
                    dve.scalar_tensor_tensor(out=dn, in0=small_ps[:, 0:HEADS], scalar=-1.0,
                                             in1=m.emt_col[:, ci, 32 * d:32 * d + HEADS].rearrange("p a h -> p (a h)"),
                                             op0=ALU.mult, op1=ALU.max).then_inc(den_step, 1)
                    dve.wait_ge(den_step, 3 * n + 1)
                    dve.tensor_tensor(dn, small_ps[:, 0:HEADS], dn, ALU.max).then_inc(den_step, 1)
                    dve.wait_ge(den_step, 3 * n + 2)
                    dve.reciprocal(dn, dn).then_inc(den_step, 1)
                    dve.wait_ge(den_step, 3 * n + 3)
                    tile = bass.ds(c - NC, 1)
                    for h in range(HEADS):
                        o = hm[:, tile, h * DV:(h + 1) * DV].rearrange("p a n -> p (a n)")
                        last = dve.scalar_tensor_tensor(out=o, in0=num_ps[:, h * DV:(h + 1) * DV],
                                                        scalar=dn[:, h:h + 1], in1=o, op0=ALU.mult, op1=ALU.add)
                    last.then_inc(h_added, 1)
                dve.wait_ge(state_made, u + 1)
                dec = lambda h0, h1: m.dec_all[:, HEADS * d + h0:HEADS * d + h1, ci].rearrange("p h a -> p (h a)")
                dve.tensor_tensor(nvec[:, d, :], nvec[:, d, :], dec(0, HEADS), ALU.mult).then_inc(n_step, 1)
                for h in range(HEADS):
                    o = cmat[:, d, h * DV:(h + 1) * DV]
                    last = dve.scalar_tensor_tensor(out=o, in0=o, scalar=dec(h, h + 1),
                                                    in1=st_ps[:, h * DV:(h + 1) * DV], op0=ALU.mult, op1=ALU.add)
                dve.wait_ge(n_step, u + 1)
                dve.tensor_tensor(nvec[:, d, :], nvec[:, d, :], small_ps[:, 8:8 + HEADS], ALU.add).then_inc(c_ready, 1)
            steps(dve, chunk)


def gla_scan(nc, m, sem, w):
    H = HEADS
    Q_IN, K_OUT = LEVELS, LEVELS + 1
    FIRST = 4
    ORDER = list(range(FIRST, LEVELS)) + list(range(FIRST))
    with ExitStack() as ctx:
        sb = lambda n, s: ctx.enter_context(nc.sbuf_tensor(n, s, F32))
        bank = lambda n, k=1: ctx.enter_context(nc.psum_tensor(n, [P, k * 512], F32))
        v = sb("gl_v", [P, 2, D])
        z = sb("gl_z", [P, 2, H * P])
        l1p = sb("gl_log1p", [P, 2, H * P])
        b = sb("gl_b", [P, 2, H * P])
        ex = sb("gl_exp", [P, LEVELS + 2, H * P])
        ks = sb("gl_k", [P, 2, H, P])
        kl = sb("gl_k_level", [P, 2, LEVELS, H * P])
        ql = sb("gl_q_level", [P, LEVELS, H * P // 2])
        qe = sb("gl_q_in", [P, H, P])
        ke = sb("gl_k_out", [P, H, P])
        ket = sb("gl_k_out_t", [P, H, P])
        at = sb("gl_scores", [P, H * P])
        smat = sb("gl_s", [P, 2, D])
        decay = sb("gl_decay", [P, 2, H])
        og = sb("gl_o", [P, NL, D])
        z_ps, dg_ps = bank("gl_z_ps"), bank("gl_dg_ps")
        lv_ps = [bank(f"gl_lv_ps{q}") for q in range(2)]
        o_ps, st_ps = bank("gl_o_ps", 2), bank("gl_st_ps", 2)
        v_loaded = [sem(f"gl_v_loaded{d}") for d in range(2)]
        (cleared, k_ready, z_made, z_ready, z_abs, log_ready, la_ready, b_ready, ex_in, ex_ready, qk_ready,
         qe_ready, ke_ready, dg_made, dg_left, lv_made, lv_left, turned, ket_ready, o_made, o_added, state_made,
         s_ready, stored) = (
            sem(f"gl_{n}") for n in (
                "cleared", "k_ready", "z_made", "z_ready", "z_abs", "log_ready", "la_ready", "b_ready", "ex_in",
                "ex_ready", "qk_ready", "qe_ready", "ke_ready", "dg_made", "dg_left", "lv_made", "lv_left",
                "turned", "ket_ready", "o_made", "o_added", "state_made", "s_ready", "stored"))
        lv_in, lv_exp = sem("gl_lv_in"), sem("gl_lv_exp")
        lv_seen, decay_kept = sem("gl_lv_seen"), sem("gl_decay_kept")
        block = ctx.enter_context(nc.Block())
        heads = lambda ap: ap.rearrange("p (h n) -> p h n", h=H)

        def lv_cols(at_l, h=None):
            start = at_l % 2 * (H * P // 2)
            return slice(start, start + H * P // 2) if h is None else \
                slice(start + h * P // 2, start + (h + 1) * P // 2)

        def steps(eng, body):
            body(0, 0, 0, 0, False, NC - 1)
            body(1, 0, NC - 1, 1, False, 1)
            body(2, 1, 1, 0, False, NC - 2)
            body(3, 1, NC - 2, 1, False, NC)
            with eng.Fori(NC, NT - 1) as i:
                back = i * -1 + (NT - 1 + NC)
                body(2 * i, i, i, 0, True, back)
                body(2 * i + 1, i, back, 1, True, i + 1)
            body(2 * NT - 2, NT - 1, NT - 1, 0, True, NC)
            body(2 * NT - 1, NT - 1, NC, 1, True, None)

        @block.sync
        def _(sp):
            def load(u, i, c, d, out, following):
                if not (isinstance(i, int) and i == 0):
                    sp.wait_ge(s_ready, u - 1)
                sp.dma_start(v[:, d, :], m.vals[1, bass.ds(c * P, P), :]).then_inc(v_loaded[d], 16)
            scan_rows(sp, load, og, m.og, o_added, stored)

        def halves(ap, l):
            v4 = ap.rearrange("p (j two i) -> p two j i", two=2, i=1 << l)
            return v4[:, 0], v4[:, 1]

        def level_exponents(eng, l, d):
            hl = 1 << l
            early, late = halves(b[:, d, :], l)
            e_early, e_late = halves(ex[:, l, :], l)
            shape = [P, H * P // 2 // hl, hl]
            if d == 0:
                mid = early[:, :, hl - 1:hl].to_broadcast(shape)
                eng.tensor_tensor(e_late, late, mid, ALU.subtract)
                return eng.tensor_tensor(e_early, mid, early, ALU.subtract)
            mid = late[:, :, 0:1].to_broadcast(shape)
            eng.tensor_tensor(e_early, early, mid, ALU.subtract)
            return eng.tensor_tensor(e_late, mid, late, ALU.subtract)

        @block.gpsimd
        def _(pool):
            pool.memset(smat[:, :, :], 0.0).then_inc(cleared, 1)
            pool.memset(og[:, :, :], 0.0).then_inc(cleared, 1)
            pool.memset(kl[:, :, :, :], 0.0).then_inc(cleared, 1)

            def lower_levels(u, d):
                pool.wait_ge(b_ready, u + 1)
                for l in ORDER[LEVELS - FIRST:]:
                    last = level_exponents(pool, l, d)
                last.then_inc(lv_in, 1)

            def chunk(u, i, c, d, out, following):
                n = u - 2 * NC
                if out:
                    pool.wait_ge(ex_ready, u + 1)
                    pool.wait_ge(s_ready, u)
                    pool.tensor_tensor(qe[:, :, :], m.qg[:, :, bass.ds(c * P - CTX, P)], heads(ex[:, Q_IN, :]),
                                       ALU.mult).then_inc(qe_ready, 1)
                if following is not None and (not isinstance(u, int) or u + 1 >= 2 * NC):
                    if out:
                        pool.wait_ge(qk_ready, LEVELS * n + LEVELS)
                    lower_levels(u + 1, 1 - d)
            steps(pool, chunk)

        @block.scalar
        def _(act):
            def logs(u, d):
                act.wait_ge(z_ready, u + 1)
                act.activation(l1p[:, d, :], z[:, d, :], ACT.Abs).then_inc(z_abs, 1)
                act.wait_ge(z_abs, 2 * u + 1)
                act.activation(l1p[:, d, :], l1p[:, d, :], ACT.Exp, scale=-1.0).then_inc(z_abs, 1)
                act.wait_ge(z_abs, 2 * u + 2)
                act.activation(l1p[:, d, :], l1p[:, d, :], ACT.Ln, bias=1.0).then_inc(log_ready, 1)

            def chunk(u, i, c, d, out, following):
                first = isinstance(u, int) and u == 0
                n = u - 2 * NC
                if out:
                    if d == 1:
                        act.wait_ge(dg_made, n)
                    act.activation(ks[:, d, :, :], m.kg[:, :, bass.ds(c * P, P)], ACT.Copy).then_inc(k_ready, 1)
                act.wait_ge(ex_in, u + 1)
                lo = FIRST if out else Q_IN
                act.activation(ex[:, lo:, :], ex[:, lo:, :], ACT.Exp, scale=1.0 / TAU).then_inc(ex_ready, 1)
                if out:
                    act.wait_ge(lv_in, n + 1)
                    act.activation(ex[:, 0:FIRST, :], ex[:, 0:FIRST, :], ACT.Exp, scale=1.0 / TAU)\
                        .then_inc(lv_exp, 1)
                act.wait_ge(turned, u + 1)
                if not first:
                    act.wait_ge(state_made, u)
                act.activation(ket[:, :, :], heads(z_ps[:, :]), ACT.Copy).then_inc(ket_ready, 1)
                if following is not None:
                    logs(u + 1, 1 - d)
            logs(0, 0)
            steps(act, chunk)

        @block.tensor
        def _(pe):
            def decays(c, d):
                for h in range(H):
                    last = pe.matmul(z_ps[:, h * P:(h + 1) * P], m.w2[:, d, h * DK:(h + 1) * DK],
                                     m.lr[:, d, bass.ds(c * P, P)], start=True, stop=True)
                last.then_inc(z_made, 1)

            def chunk(u, i, c, d, out, following):
                n = u - 2 * NC
                first = isinstance(u, int) and u == 0

                def next_decays():
                    if following is not None:
                        pe.wait_ge(ket_ready, u + 1)
                        decays(following, 1 - d)

                def state_sum():
                    pe.wait_ge(v_loaded[d], 16 * i + 16)
                    pe.wait_ge(ket_ready, u + 1)
                    if not first:
                        pe.wait_ge(s_ready, u)
                    for h in range(H):
                        last = pe.matmul(st_ps[:, h * DV:(h + 1) * DV], ket[:, h, :], v[:, d, h * DV:(h + 1) * DV],
                                         start=True, stop=True)
                    last.then_inc(state_made, 1)
                pe.wait_ge(ke_ready, u + 1)
                pe.wait_ge(z_ready, u + 1)
                for h in range(H):
                    last = pe.transpose(z_ps[:, h * P:(h + 1) * P], ke[:, h, :], m.ident[:, :])
                last.then_inc(turned, 1)
                if not out:
                    next_decays()
                if out:
                    pe.wait_ge(k_ready, n + 1)
                    if d == 1:
                        pe.wait_ge(dg_left, n)
                    else:
                        pe.wait_ge(s_ready, u)
                    for h in range(H):
                        last = pe.matmul(dg_ps[:, h * P:(h + 1) * P], ks[:, d, h, :],
                                         m.qg[:, h, bass.ds(c * P - CTX, P)], start=True, stop=True)
                    last.then_inc(dg_made, 1)
                    for at_l, l in enumerate(ORDER):
                        if at_l == 2:
                            next_decays()
                        if at_l == 4:
                            state_sum()
                        pe.wait_ge(qk_ready, LEVELS * n + at_l + 1)
                        if at_l >= 4:
                            pe.wait_ge(lv_left, LEVELS * n + at_l // 2 * 2 - 2)
                        elif d == 1:
                            pe.wait_ge(lv_left, LEVELS * n)
                        for h in range(H):
                            last = pe.matmul(lv_ps[at_l // 2 % 2][:, lv_cols(at_l, h)],
                                             kl[:, d, l, h * P:(h + 1) * P],
                                             ql[:, l, h * P // 2:(h + 1) * P // 2], start=True, stop=True)
                        last.then_inc(lv_made, 1)
                    pe.wait_ge(qe_ready, n + 1)
                    pe.wait_ge(lv_left, LEVELS * n + LEVELS)
                    for h in range(H):
                        o = o_ps[:, h * DV:(h + 1) * DV]
                        pe.matmul(o, at[:, h * P:(h + 1) * P], v[:, d, h * DV:(h + 1) * DV], start=True, stop=False)
                        last = pe.matmul(o, qe[:, h, :], smat[:, d, h * DV:(h + 1) * DV], start=False, stop=True)
                    last.then_inc(o_made, 1)
                else:
                    state_sum()
            decays(0, 0)
            pe.wait_ge(cleared, 3)
            steps(pe, chunk)

        @block.vector
        def _(dve):
            def take_z(u, d):
                dve.wait_ge(z_made, u + 1)
                dve.tensor_tensor(heads(z[:, d, :]), heads(z_ps[:, :]),
                                  m.vec[:, HEADS * d:HEADS * d + HEADS, B2:B2 + 1].to_broadcast([P, H, P]), ALU.add)\
                    .then_inc(z_ready, 1)

            def sums(u, d):
                dve.wait_ge(log_ready, u + 1)
                dve.scalar_tensor_tensor(out=z[:, d, :], in0=z[:, d, :], scalar=0.0, in1=l1p[:, d, :],
                                         op0=ALU.min, op1=ALU.subtract).then_inc(la_ready, 1)
                dve.wait_ge(la_ready, u + 1)
                back = slice(None, None, -1) if d else slice(None)
                dve.tensor_tensor_scan(b[:, d, back], m.restart[:, d, 0:H * P][:, back], z[:, d, back], 0.0,
                                       ALU.mult, ALU.add).then_inc(b_ready, 1)

            def exponents(u, d, out):
                end = P - 1 if d == 0 else 0
                dve.wait_ge(b_ready, u + 1)
                bd = b[:, d, :]
                if out:
                    for l in ORDER[:LEVELS - FIRST]:
                        level_exponents(dve, l, d)
                dve.tensor_copy(ex[:, Q_IN, :], bd)
                dve.tensor_tensor(heads(ex[:, K_OUT, :]), heads(bd)[:, :, end:end + 1].to_broadcast([P, H, P]),
                                  heads(bd), ALU.subtract).then_inc(ex_in, 1)

            def chunk(u, i, c, d, out, following):
                n = u - 2 * NC
                first = isinstance(u, int) and u == 0
                end = P - 1 if d == 0 else 0
                dve.wait_ge(ex_ready, u + 1)
                kc = m.kg[:, :, bass.ds(c * P, P)]
                if not first:
                    dve.wait_ge(turned, u)
                dve.tensor_tensor(ke[:, :, :], kc, heads(ex[:, K_OUT, :]), ALU.mult).then_inc(ke_ready, 1)
                dve.tensor_copy(decay[:, d, :], heads(ex[:, Q_IN, :])[:, :, end:end + 1].rearrange("p h a -> p (h a)"))\
                    .then_inc(decay_kept, 1)
                if out:
                    qc = m.qg[:, :, bass.ds(c * P - CTX, P)]
                    for at_l, l in enumerate(ORDER):
                        if at_l == LEVELS - FIRST:
                            dve.wait_ge(lv_exp, n + 1)
                        hl = 1 << l
                        q_half, k_half = (1, 0) if d == 0 else (0, 1)
                        parts = lambda ap: ap.rearrange("p h (j two i) -> p two h j i", two=2, i=hl)
                        e = parts(heads(ex[:, l, :]))
                        dve.tensor_tensor(ql[:, l, :].rearrange("p (h j i) -> p h j i", h=H, i=hl),
                                          parts(qc)[:, q_half], e[:, q_half], ALU.mult)
                        dve.tensor_tensor(parts(heads(kl[:, d, l, :]))[:, k_half], parts(kc)[:, k_half],
                                          e[:, k_half], ALU.mult).then_inc(qk_ready, 1)
                if following is not None:
                    take_z(u + 1, 1 - d)
                if out:
                    dve.wait_ge(dg_made, n + 1)
                    dve.tensor_tensor(heads(at[:, :]), heads(dg_ps[:, :]),
                                      m.ident[:, :].rearrange("p (a n) -> p a n", a=1).to_broadcast([P, H, P]),
                                      ALU.mult).then_inc(dg_left, 1)
                    dve.wait_ge(dg_left, n + 1)
                    for at_l, l in enumerate(ORDER):
                        hl = 1 << l
                        dve.wait_ge(lv_made, LEVELS * n + min(LEVELS, at_l // 2 * 2 + 2))
                        if at_l:
                            dve.wait_ge(lv_left, LEVELS * n + at_l)
                        dve.sem_inc(lv_seen, 1)
                        sel = halves(at[:, :], l)[1 - d]
                        mask = m.level_mask[:, d, l, :].rearrange("p (j i) -> p j i", i=hl)
                        data = lv_ps[at_l // 2 % 2][:, lv_cols(at_l)].rearrange("p (j i) -> p j i", i=hl)
                        dve.copy_predicated(sel, mask, data).then_inc(lv_left, 1)
                if following is not None:
                    sums(u + 1, 1 - d)
                    dve.wait_ge(decay_kept, u + 1)
                    if out:
                        dve.wait_ge(qe_ready, n + 1)
                    exponents(u + 1, 1 - d, not isinstance(u, int) or u + 1 >= 2 * NC)
                if out:
                    dve.wait_ge(o_made, n + 1)
                    o = og[:, bass.ds(c - NC, 1), :].rearrange("p a n -> p (a n)")
                    dve.tensor_tensor(o, o_ps[:, :], o, ALU.add).then_inc(o_added, 1)
                dve.wait_ge(state_made, u + 1)
                dve.wait_ge(decay_kept, u + 1)
                for h in range(H):
                    o = smat[:, d, h * DV:(h + 1) * DV]
                    last = dve.scalar_tensor_tensor(out=o, in0=o, scalar=decay[:, d, h:h + 1],
                                                    in1=st_ps[:, h * DV:(h + 1) * DV], op0=ALU.mult, op1=ALU.add)
                last.then_inc(s_ready, 1)
            take_z(0, 0)
            sums(0, 0)
            exponents(0, 0, False)
            dve.wait_ge(cleared, 3)
            steps(dve, chunk)


def mix_out(nc, m, sem, w):
    with ExitStack() as ctx:
        sb = lambda n, s: ctx.enter_context(nc.sbuf_tensor(n, s, F32))
        bank = lambda n, k=1: ctx.enter_context(nc.psum_tensor(n, [P, k * 512], F32))
        wp = sb("mo_w_proj", [P, 2, KD, D])
        wo = sb("mo_w_out", [P, KD, D])
        wr = sb("mo_w_router", [P, KD, GROUPS + EXPERTS])
        hin = sb("mo_in", [P, 2, 4, D])
        mg = sb("mo_merge", [P, 2, D])
        xt = sb("mo_x", [P, D])
        yt = sb("mo_y_t", [P, 2, KD, P])
        y = sb("mo_y", [P, 2, D])
        yg = sb("mo_yg", [P, D])
        x1 = sb("mo_x1", [P, 2, D])
        h2 = sb("mo_h2", [P, D])
        sq = sb("mo_sq", [P, D])
        sqh = sb("mo_sqh", [P, 2 * HEADS, DV])
        spread = sb("mo_spread", [P, 3, D])
        st = sb("mo_stat", [P, 2, 3, 2 * HEADS])
        st2 = sb("mo_stat2", [P, 3])
        tp_m, tp_g, p_m, p_g = (bank(f"mo_{n}", 2) for n in ("tp_m", "tp_g", "p_m", "p_g"))
        s = {name: sem(f"mo_{name}") for name in ("wm_loaded", "wg_loaded", "wo_loaded", "wr_loaded", "mg_loaded", "x_loaded", "spread_loaded", "a2", "stat", "rstd", "y_ready", "t_m",
                     "t_g", "ym_t", "yg_t", "made_m", "made_g", "y_part", "yg_part", "y_done", "t_y", "y_t",
                     "made_out", "x1_part", "x1_done", "stat2", "xn", "h2_part", "h2_done", "t_h", "h_t", "made_r",
                     "logits", "x1_stored", "h2_stored", "h2_free")}
        in_loaded = [sem(f"mo_in_loaded{j}") for j in range(2)]
        block = ctx.enter_context(nc.Block())
        kmaj = lambda ap: ap.rearrange("p (k n) -> p k n", k=KD)

        def pipeline(eng, *stages):
            def step(n):
                for f, lag in stages:
                    t = n - lag
                    if 0 <= t < NL:
                        f(t, t % 2, t // 2, t == 0, t == NL - 1)
            for n in range(4):
                step(n)
            with eng.Fori(2, NL // 2 - 1) as i:
                for j in range(2):
                    for f, lag in stages:
                        f(2 * i + (j - lag), (j - lag) % 2, i + (j - lag) // 2, False, False)
            for n in range(NL - 2, NL + 2):
                step(n)

        def rows(ap, n):
            return ap[bass.ds(n * P, P), :]

        @block.sync
        def _(sp):
            def load_in(n, j):
                sp.dma_start(hin[:, j, 0, :], rows(m.hm, n)).then_inc(in_loaded[j], 16)
                sp.dma_start(hin[:, j, 1, :], rows(m.og, n)).then_inc(in_loaded[j], 16)
                sp.dma_start(hin[:, j, 2:4, :], m.gates[0:2, bass.ds(n * P, P), :].rearrange("g p n -> p g n"))\
                    .then_inc(in_loaded[j], 16)
            sp.dma_start(spread[:, :, :], m.mod_rows[:, 0:3 * D].rearrange("p (a n) -> p a n", a=3))\
                .then_inc(s["spread_loaded"], 16)
            sp.dma_start(sq[:, :], w["g_norm2"][0:1, :].partition_broadcast(P)).then_inc(s["spread_loaded"], 16)
            load_in(0, 0)
            sp.dma_start(wp[:, 0, :, :], w["w_proj_m"][0].rearrange("(k p) n -> p k n", p=P))\
                .then_inc(s["wm_loaded"], 16)

            def a(n, j, half, first, final):
                if not first:
                    sp.wait_ge(s["yg_part"], n)
                sp.dma_start(mg[:, :, :], m.gates[2:4, bass.ds(n * P, P), :].rearrange("g p n -> p g n"))\
                    .then_inc(s["mg_loaded"], 16)
                if not final:
                    if not first:
                        sp.wait_ge(s["t_g"], n)
                    load_in(n + 1, 1 - j)

            def b(n, j, half, first, final):
                if not first:
                    sp.wait_ge(s["x1_done"], n)
                sp.dma_start(xt[:, :], rows(w["x"][0], n)).then_inc(s["x_loaded"], 16)

            def c(n, j, half, first, final):
                if first:
                    sp.sem_inc(s["h2_free"], 1)
                sp.wait_ge(s["x1_done"], n + 1)
                sp.dma_start(rows(m.x1, n), x1[:, j, :]).then_inc(s["x1_stored"], 16)
                sp.wait_ge(s["h2_done"], n + 1)
                sp.dma_start(rows(m.h2, n), h2[:, :]).then_inc(s["h2_stored"], 16)
                sp.wait_ge(s["h2_stored"], 16 * n + 16)
                sp.wait_ge(s["x1_stored"], 16 * n + 16)
                sp.sem_inc(s["h2_free"], 1)
            pipeline(sp, (a, 0), (c, 2), (b, 1))

        @block.scalar
        def _(act):
            def norms(n, j, half):
                act.wait_ge(in_loaded[j], 48 * half + 48)
                for q in range(2):
                    for h in range(HEADS):
                        last = act.activation(sqh[:, HEADS * q + h, :], hin[:, j, q, h * DV:(h + 1) * DV], ACT.Square,
                                              accum_out=st[:, j, 0, HEADS * q + h:HEADS * q + h + 1])
                last.then_inc(s["stat"], 1)
                act.wait_ge(s["stat"], 2 * n + 1)
                act.activation(st[:, j, 1, :], st[:, j, 0, :], ACT.Ln, bias=m.eps[:, 0:1], scale=1.0 / DV)\
                    .then_inc(s["stat"], 1)
                act.wait_ge(s["stat"], 2 * n + 2)
                act.activation(st[:, j, 2, :], st[:, j, 1, :], ACT.Exp, scale=-0.5).then_inc(s["rstd"], 1)

            def a(n, j, half, first, final):
                if not final:
                    norms(n + 1, 1 - j, half + j)

            def c(n, j, half, first, final):
                act.wait_ge(s["x1_done"], n + 1)
                act.activation(sq[:, :], x1[:, j, :], ACT.Square, accum_out=st2[:, 0:1]).then_inc(s["stat2"], 1)
                act.wait_ge(s["stat2"], 3 * n + 1)
                act.activation(st2[:, 1:2], st2[:, 0:1], ACT.Ln, bias=m.eps[:, 0:1], scale=1.0 / D)\
                    .then_inc(s["stat2"], 1)
                act.wait_ge(s["stat2"], 3 * n + 2)
                act.activation(st2[:, 2:3], st2[:, 1:2], ACT.Exp, scale=-0.5).then_inc(s["stat2"], 1)
                act.wait_ge(s["stat2"], 3 * n + 3)
                act.wait_ge(s["h2_free"], n + 1)
                if not first:
                    act.wait_ge(s["t_h"], n)
                act.activation(h2[:, :], x1[:, j, :], ACT.Copy, scale=st2[:, 2:3]).then_inc(s["xn"], 1)
            act.wait_ge(s["a2"], 1)
            norms(0, 0, 0)
            act.dma_start(wp[:, 1, :, :], w["w_proj_g"][0].rearrange("(k p) n -> p k n", p=P))\
                .then_inc(s["wg_loaded"], 16)
            act.dma_start(wo[:, :, :], w["w_out"][0].rearrange("(k p) n -> p k n", p=P)).then_inc(s["wo_loaded"], 16)
            act.dma_start(wr[:, :, 0:GROUPS], w["w_grp"][0].rearrange("(k p) n -> p k n", p=P))\
                .then_inc(s["wr_loaded"], 16)
            act.dma_start(wr[:, :, GROUPS:], w["w_rexp"][0].rearrange("(k p) n -> p k n", p=P))\
                .then_inc(s["wr_loaded"], 16)
            pipeline(act, (c, 2), (a, 0))

        @block.gpsimd
        def _(pool):
            def a(n, j, half, first, final):
                pool.wait_ge(s["yg_part"], n + 1)
                pool.tensor_tensor(y[:, j, :], y[:, j, :], yg[:, :], ALU.add).then_inc(s["y_done"], 1)

            def b(n, j, half, first, final):
                pool.wait_ge(s["x1_part"], n + 1)
                pool.wait_ge(s["x_loaded"], 16 * n + 16)
                pool.tensor_tensor(x1[:, j, :], x1[:, j, :], xt[:, :], ALU.add).then_inc(s["x1_done"], 1)

            def c(n, j, half, first, final):
                pool.wait_ge(s["xn"], n + 1)
                pool.tensor_tensor(h2[:, :], h2[:, :], spread[:, 2, :], ALU.mult).then_inc(s["h2_part"], 1)
                pool.wait_ge(s["h2_part"], n + 1)
                pool.tensor_tensor(h2[:, :], h2[:, :], spread[:, 1, :], ALU.add).then_inc(s["h2_done"], 1)
            pool.wait_ge(s["a2"], 1)
            pipeline(pool, (c, 2), (a, 0), (b, 1))

        @block.vector
        def _(dve):
            dve.wait_ge(s["spread_loaded"], 32)
            dve.scalar_tensor_tensor(out=spread[:, 2, :], in0=spread[:, 2, :], scalar=1.0, in1=sq[:, :],
                                     op0=ALU.add, op1=ALU.mult).then_inc(s["a2"], 1)

            def gated(n, j):
                dve.wait_ge(s["rstd"], n + 1)
                for q in range(2):
                    for h in range(HEADS):
                        o = hin[:, j, q, h * DV:(h + 1) * DV]
                        ins = dve.scalar_tensor_tensor(
                            out=o, in0=o, scalar=st[:, j, 2, HEADS * q + h:HEADS * q + h + 1],
                            in1=hin[:, j, 2 + q, h * DV:(h + 1) * DV], op0=ALU.mult, op1=ALU.mult)
                ins.then_inc(s["y_ready"], 1)

            def norm_col(row):
                return m.vec[:, :, row:row + 1].to_broadcast([P, KD, P])

            def turned(n, j, half, first, final):
                dve.wait_ge(s["t_m"], n + 1)
                dve.tensor_tensor(yt[:, 0, :, :], kmaj(tp_m[:, :]), norm_col(NORM_M), ALU.mult).then_inc(s["ym_t"], 1)
                dve.wait_ge(s["t_g"], n + 1)
                dve.tensor_tensor(yt[:, 1, :, :], kmaj(tp_g[:, :]), norm_col(NORM_G), ALU.mult).then_inc(s["yg_t"], 1)

            def part_m(n, j, half, first, final):
                dve.wait_ge(s["made_m"], n + 1)
                dve.wait_ge(s["mg_loaded"], 16 * n + 16)
                dve.tensor_tensor(y[:, j, :], p_m[:, :], mg[:, 0, :], ALU.mult).then_inc(s["y_part"], 1)

            def y_turned(n, j, half, first, final):
                dve.wait_ge(s["t_y"], n + 1)
                dve.tensor_copy(yt[:, 0, :, :], kmaj(tp_m[:, :])).then_inc(s["y_t"], 1)

            def part_g(n, j, half, first, final):
                if not final:
                    gated(n + 1, 1 - j)
                dve.wait_ge(s["made_g"], n + 1)
                if not first:
                    dve.wait_ge(s["y_done"], n)
                dve.tensor_tensor(yg[:, :], p_g[:, :], mg[:, 1, :], ALU.mult).then_inc(s["yg_part"], 1)

            def mixed(n, j, half, first, final):
                dve.wait_ge(s["made_out"], n + 1)
                if not isinstance(n, int) or n >= 2:
                    dve.wait_ge(s["h2_free"], n)
                dve.tensor_tensor(x1[:, j, :], p_m[:, :], spread[:, 0, :], ALU.mult).then_inc(s["x1_part"], 1)

            def router(n, j, half, first, final):
                dve.wait_ge(s["t_h"], n + 1)
                dve.tensor_copy(yt[:, 1, :, :], kmaj(tp_g[:, :])).then_inc(s["h_t"], 1)
                dve.wait_ge(s["made_r"], n + 1)
                dve.tensor_copy(m.logits[:, bass.ds(n, 1), :], tp_g[:, 0:GROUPS + EXPERTS]
                                .rearrange("p (a n) -> p a n", a=1)).then_inc(s["logits"], 1)
            gated(0, 0)
            pipeline(dve, (turned, 0), (part_m, 0), (y_turned, 1), (part_g, 0), (mixed, 1), (router, 2))
            dve.wait_ge(s["logits"], NL)

        @block.tensor
        def _(pe):

            def turn(dst, src):
                for k in range(KD):
                    last = pe.transpose(dst[:, k * P:(k + 1) * P], src[:, k * P:(k + 1) * P], m.ident[:, :])
                return last

            def product(dst, lhs_t, weights):
                for q in range(2):
                    for k in range(KD):
                        last = pe.matmul(dst[:, q * 512:(q + 1) * 512], lhs_t[:, k, :],
                                         weights[:, k, q * 512:(q + 1) * 512], start=(k == 0), stop=(k == KD - 1))
                return last

            def branch_m(n, j, half, first, final):
                pe.wait_ge(s["y_ready"], n + 1)
                turn(tp_m, hin[:, j, 0, :]).then_inc(s["t_m"], 1)
                if not isinstance(n, int) or n >= 3:
                    pe.wait_ge(s["logits"], n - 2)
                turn(tp_g, hin[:, j, 1, :]).then_inc(s["t_g"], 1)
                pe.wait_ge(s["ym_t"], n + 1)
                if not isinstance(n, int) or n >= 2:
                    pe.wait_ge(s["x1_part"], n - 1)
                if first:
                    pe.wait_ge(s["wm_loaded"], 16)
                product(p_m, yt[:, 0, :, :], wp[:, 0, :, :]).then_inc(s["made_m"], 1)

            def turn_y(n, j, half, first, final):
                pe.wait_ge(s["y_done"], n + 1)
                turn(tp_m, y[:, j, :]).then_inc(s["t_y"], 1)

            def branch_g(n, j, half, first, final):
                pe.wait_ge(s["yg_t"], n + 1)
                if not first:
                    pe.wait_ge(s["yg_part"], n)
                if first:
                    pe.wait_ge(s["wg_loaded"], 16)
                product(p_g, yt[:, 1, :, :], wp[:, 1, :, :]).then_inc(s["made_g"], 1)

            def project_out(n, j, half, first, final):
                pe.wait_ge(s["y_t"], n + 1)
                if not final:
                    pe.wait_ge(s["y_part"], n + 2)
                if first:
                    pe.wait_ge(s["wo_loaded"], 16)
                product(p_m, yt[:, 0, :, :], wo).then_inc(s["made_out"], 1)

            def router(n, j, half, first, final):
                pe.wait_ge(s["h2_done"], n + 1)
                if not first:
                    pe.wait_ge(s["logits"], n)
                turn(tp_g, h2[:, :]).then_inc(s["t_h"], 1)
                pe.wait_ge(s["h_t"], n + 1)
                if first:
                    pe.wait_ge(s["wr_loaded"], 32)
                for k in range(KD):
                    last = pe.matmul(tp_g[:, 0:GROUPS + EXPERTS], yt[:, 1, k, :], wr[:, k, :],
                                     start=(k == 0), stop=(k == KD - 1))
                last.then_inc(s["made_r"], 1)
            pipeline(pe, (branch_m, 0), (turn_y, 1), (branch_g, 0), (project_out, 1), (router, 2))


def route(nc, m, sem, w):
    G, E, N = PER_GROUP, EXPERTS, NL
    BIG = 1e30
    with ExitStack() as ctx:
        sb = lambda n, s, dt=F32: ctx.enter_context(nc.sbuf_tensor(n, s, dt))
        bias = sb("rt_bias", [P, GROUPS + E])
        lg = sb("rt_lg", [P, N, GROUPS + E])
        rank4 = sb("rt_rank4", [P, 4])
        mx = sb("rt_max", [P, N])
        eg = sb("rt_eg", [P, N, 4])
        sg = sb("rt_sg", [P, N])
        hot = sb("rt_hot", [P, 3, N, 4])
        tmp = sb("rt_tmp", [P, N, 4])
        sel = sb("rt_sel", [P, N, GROUPS, 4])
        es = sb("rt_es", [P, N, 4])
        e12 = sb("rt_e12", [P, 2, N])
        x = sb("rt_x", [P, N])
        hots = sb("rt_hots", [P, 2, N, GROUPS, 4])
        both = sb("rt_both", [P, N * E])
        pre = sb("rt_pre", [P, N + 1, E])
        tot = sb("rt_tot", [P, N, E])
        base = sb("rt_base", [P, N, E])
        blocks = sb("rt_blocks", [P, E])
        ends = sb("rt_ends", [P, E])
        ones16 = sb("rt_ones16", [P, E])
        prod = sb("rt_prod", [P, 2, N, E])
        dest = sb("rt_dest", [P, 2, N])
        assert BLOCKS + 1 == 1 << 5 and P == 1 << 7
        hi = sb("rt_hi", [P, 2, N], I32)
        place, token = m.place_i, m.token
        zero = sb("rt_zero", [P, BLOCKS + 1], I32)
        which = sb("rt_which", [P, BLOCKS])
        le = sb("rt_le", [P, BLOCKS, E])
        blk = sb("rt_blk", [P, BLOCKS])
        cum_ps = ctx.enter_context(nc.psum_tensor("rt_cum_ps", [P, N * E], F32))
        tot_ps = ctx.enter_context(nc.psum_tensor("rt_tot_ps", [P, N * E], F32))
        step, loaded, built, exps, ranked, zeroed = (sem(f"rt_{n}") for n in (
            "step", "loaded", "built", "exps", "ranked", "zeroed"))
        block = ctx.enter_context(nc.Block())
        table = m.row_tok.rearrange("(p b) a -> p (b a)", p=P)
        over = lambda ap, shape: ap.to_broadcast(shape)

        @block.sync
        def _(sp):
            sp.dma_start(bias[:, 0:GROUPS], w["b_grp"].partition_broadcast(P)).then_inc(loaded, 16)
            sp.dma_start(bias[:, GROUPS:], w["b_rexp"].partition_broadcast(P)).then_inc(loaded, 16)
            sp.wait_ge(built, 1)
            sp.dma_start(table, zero[:, :]).then_inc(zeroed, 16)
            sp.wait_ge(zeroed, 16)

        @block.gpsimd
        def _(pool):
            pool.memset(zero[:, :], 0).then_inc(built, 1)
            pool.iota(token[:, :], pattern=[[P, N]], base=0, channel_multiplier=1).then_inc(built, 1)
            pool.iota(which[:, :], pattern=[[1, BLOCKS]], base=0, channel_multiplier=0,
                      allow_small_or_imprecise_dtypes=True).then_inc(built, 1)
            pool.iota(rank4[:, :], pattern=[[-1, 4]], base=4, channel_multiplier=0,
                      allow_small_or_imprecise_dtypes=True).then_inc(built, 1)
            pool.memset(ones16[:, :], 1.0).then_inc(built, 1)

        @block.scalar
        def _(act):
            act.wait_ge(step, 3)
            act.activation(eg[:, :, :], eg[:, :, :], ACT.Exp).then_inc(exps, 1)
            act.wait_ge(exps, 1)
            act.wait_ge(built, 6)
            act.activation(x[:, :], x[:, :], ACT.Exp).then_inc(exps, 1)

        @block.tensor
        def _(pe):
            pe.wait_ge(ranked, 1)
            pe.matmul(cum_ps[:, :], m.before[:, :], both[:, :], start=True, stop=True)
            pe.matmul(tot_ps[:, :], m.ones[:, :], both[:, :], start=True, stop=True).then_inc(built, 1)

        @block.vector
        def _(dve):
            count = [0]

            def then(ins):
                count[0] += 1
                ins.then_inc(step, 1)
                dve.wait_ge(step, count[0])

            tt, ts = dve.tensor_tensor, dve.tensor_scalar
            dve.wait_ge(loaded, 32)
            then(tt(lg[:, :, :], m.logits[:, :, :],
                    bias[:, :].rearrange("p (a n) -> p a n", a=1).to_broadcast([P, N, GROUPS + E]), ALU.add))
            grp = lg[:, :, 0:GROUPS]
            wide = lambda ap: ap.rearrange("p (n a) -> p n a", a=1).to_broadcast([P, N, 4])
            then(dve.tensor_reduce(mx[:, :], grp, AX.X, ALU.max))
            then(tt(eg[:, :, :], grp, wide(mx[:, :]), ALU.subtract))
            dve.wait_ge(exps, 1)
            then(dve.tensor_reduce(sg[:, :], eg[:, :, :], AX.X, ALU.add))
            dve.wait_ge(built, 5)
            prefer = rank4[:, :].rearrange("p (a n) -> p a n", a=1).to_broadcast([P, N, 4])

            def first_max(values, largest, out):
                then(tt(tmp[:, :, :], values, wide(largest), ALU.is_equal))
                then(tt(tmp[:, :, :], tmp[:, :, :], prefer, ALU.mult))
                then(dve.tensor_reduce(mx[:, :], tmp[:, :, :], AX.X, ALU.max))
                then(tt(out, tmp[:, :, :], wide(mx[:, :]), ALU.is_equal))

            first_max(grp, mx[:, :], hot[:, 0])
            then(tt(sel[:, :, :, :], lg[:, :, GROUPS:].rearrange("p n (g e) -> p n g e", g=GROUPS),
                    hot[:, 0].rearrange("p n (g a) -> p n g a", a=1).to_broadcast([P, N, GROUPS, 4]), ALU.mult))
            then(dve.tensor_reduce(es[:, :, :], sel[:, :, :, :].rearrange("p n g e -> p n e g"), AX.X, ALU.add))
            then(dve.tensor_reduce(e12[:, 0, :], es[:, :, :], AX.X, ALU.max))
            first_max(es[:, :, :], e12[:, 0, :], hot[:, 1])
            then(dve.scalar_tensor_tensor(out=es[:, :, :], in0=hot[:, 1], scalar=-BIG, in1=es[:, :, :],
                                          op0=ALU.mult, op1=ALU.add))
            then(dve.tensor_reduce(e12[:, 1, :], es[:, :, :], AX.X, ALU.max))
            first_max(es[:, :, :], e12[:, 1, :], hot[:, 2])
            then(tt(x[:, :], e12[:, 1, :], e12[:, 0, :], ALU.subtract))
            dve.sem_inc(built, 1)
            for k in range(TOP_K):
                for g in range(GROUPS):
                    then(tt(hots[:, k, :, g, :], hot[:, 1 + k], hot[:, 0, :, g:g + 1].to_broadcast([P, N, 4]),
                            ALU.mult))
            hv = hots[:, :, :, :, :].rearrange("p k n g e -> p k (n g e)")
            tt(both[:, :], hv[:, 0], hv[:, 1], ALU.add).then_inc(ranked, 1)
            dve.wait_ge(exps, 2)
            then(dve.scalar_tensor_tensor(out=sg[:, :], in0=x[:, :], scalar=1.0, in1=sg[:, :],
                                          op0=ALU.add, op1=ALU.mult))
            then(dve.reciprocal(m.weight[:, 0, :], sg[:, :]))
            then(tt(m.weight[:, 1, :], m.weight[:, 0, :], x[:, :], ALU.mult))
            dve.wait_ge(built, 7)
            then(dve.tensor_copy(tot[:, :, :], tot_ps[:, :].rearrange("p (n e) -> p n e", e=E)))
            then(dve.memset(pre[:, 0, :], 0.0))
            for n in range(N):
                then(tt(pre[:, n + 1, :], pre[:, n, :], tot[:, n, :], ALU.add))
            then(ts(blocks[:, :], pre[:, N, :], 0.0, None, ALU.is_gt))
            for q in range(1, SEQ // P):
                then(dve.scalar_tensor_tensor(out=blocks[:, :], in0=pre[:, N, :], scalar=float(P * q),
                                              in1=blocks[:, :], op0=ALU.is_gt, op1=ALU.add))
            then(dve.tensor_tensor_scan(ends[:, :], ones16[:, :], blocks[:, :], 0.0, ALU.mult, ALU.add))
            then(tt(le[:, :, :], ends[:, :].rearrange("p (a e) -> p a e", a=1).to_broadcast([P, BLOCKS, E]),
                    which[:, :].rearrange("p (b a) -> p b a", a=1).to_broadcast([P, BLOCKS, E]), ALU.is_le))
            then(dve.tensor_reduce(blk[:, :], le[:, :, :], AX.X, ALU.add))
            then(ts(m.block_e[:, 0:BLOCKS], blk[:, :], float(E - 1), None, ALU.min))
            then(tt(ends[:, :], ends[:, :], blocks[:, :], ALU.subtract))
            then(tt(base[:, :, :], cum_ps[:, :].rearrange("p (n e) -> p n e", e=E), pre[:, 0:N, :], ALU.add))
            then(dve.scalar_tensor_tensor(out=base[:, :, :],
                                          in0=ends[:, :].rearrange("p (a e) -> p a e", a=1).to_broadcast([P, N, E]),
                                          scalar=float(P), in1=base[:, :, :], op0=ALU.mult, op1=ALU.add))
            for k in range(TOP_K):
                then(tt(prod[:, k].rearrange("p n e -> p (n e)"), hv[:, k],
                        base[:, :, :].rearrange("p n e -> p (n e)"), ALU.mult))
            then(dve.tensor_reduce(dest[:, :, :], prod[:, :, :, :], AX.X, ALU.add))
            then(dve.tensor_copy(m.dest_i[:, :, :], dest[:, :, :]))
            then(ts(hi[:, :, :], m.dest_i[:, :, :], 7, None, ALU.logical_shift_right))
            then(ts(place[:, :, :], m.dest_i[:, :, :], P - 1, 5, ALU.bitwise_and, ALU.logical_shift_left))
            tt(place[:, :, :], place[:, :, :], hi[:, :, :], ALU.add).then_inc(ranked, 1)
            dve.wait_ge(ranked, 2)


def experts(nc, m, sem, w):
    with ExitStack() as ctx:
        sb = lambda n, s, dt=F32: ctx.enter_context(nc.sbuf_tensor(n, s, dt))
        bank = lambda n, k=1: ctx.enter_context(nc.psum_tensor(n, [P, k * 512], F32))
        HK = FF // P
        PIECE = KD * FF
        assert PIECE == HK * D
        HALF = PIECE // 2
        raw = sb("ex_raw", [P, 3, PIECE])
        hi = sb("ex_w_hi", [P, 3, PIECE], F32R)
        lo = sb("ex_w_lo", [P, 3, PIECE], F32R)
        table = sb("ex_rows", [P, BLOCKS + 1], I32)
        idx = sb("ex_idx", [P, 2], I32)
        xg = sb("ex_x", [P, 2, D])
        xt_hi = sb("ex_x_hi", [P, D], F32R)
        xt_lo = sb("ex_x_lo", [P, D], F32R)
        gate = sb("ex_gate", [P, FF])
        hid = sb("ex_hidden", [P, FF])
        ht_hi = sb("ex_hidden_hi", [P, FF], F32R)
        ht_lo = sb("ex_hidden_lo", [P, FF], F32R)
        yo = sb("ex_y", [P, 2, D])
        x_ps, g_ps, u_ps, h_ps, y_ps = bank("ex_x_ps", 2), bank("ex_g_ps"), bank("ex_u_ps"), bank("ex_h_ps"), bank("ex_y_ps", 2)
        s = {name: sem(f"ex_{name}") for name in (
            "table", "idx", "t_x", "x_hi", "x_lo", "gate", "hidden", "t_h", "h_hi", "h_lo", "y_left",
            "gather_begun")}
        loaded, hi_done, lo_done, made = ([sem(f"ex_{n}{q}") for q in range(3)] for n in (
            "loaded", "hi_done", "lo_done", "made"))
        scattered = sem("ex_scattered")
        gathered, stored = ([sem(f"ex_{n}{j}") for j in range(2)] for n in ("gathered", "stored"))
        block = ctx.enter_context(nc.Block())

        def each(eng, body):
            for b in range(2):
                body(b, b, 0)
            with eng.Fori(1, BLOCKS // 2) as i:
                for j in range(2):
                    body(2 * i + j, j, i)
            if BLOCKS % 2:
                body(BLOCKS - 1, (BLOCKS - 1) % 2, BLOCKS // 2)
        late = lambda b, n: not isinstance(b, int) or b >= n
        more = lambda b: not isinstance(b, int) or b < BLOCKS - 1

        @block.sync
        def _(sp):
            def load(b, q):
                e = sp.value_load(m.block_e[0:1, bass.ds(b, 1)], min_val=0, max_val=EXPERTS - 1)
                if late(b, 1):
                    sp.wait_ge(lo_done[q], 2 * b)
                if q < 2:
                    src = w["w_up"][0][bass.ds(e, 1)].rearrange("a (k p) n -> p (a k) n", p=P)
                    src = src[:, :, q * FF:(q + 1) * FF]
                else:
                    src = w["w_down"][0][bass.ds(e, 1)].rearrange("a (k p) n -> p (a k) n", p=P)
                sp.dma_start(raw[:, q, :].rearrange("p (k n) -> p k n", n=FF if q < 2 else D), src)\
                    .then_inc(loaded[q], 16)

            def step(b, j, half):
                if more(b):
                    load(b + 1, 0)
                    load(b + 1, 1)
                load(b, 2)
            load(0, 0)
            load(0, 1)
            each(sp, step)

        @block.gpsimd
        def _(pool):
            for k in range(TOP_K):
                for n in range(NL):
                    pool.indirect_dma_start(
                        out=m.row_tok, out_offset=bass.IndirectOffsetOnAxis(ap=m.place_i[:, k, n:n + 1], axis=0),
                        in_=m.token[:, n:n + 1], in_offset=None).then_inc(scattered, 16)
            pool.wait_ge(scattered, 16 * TOP_K * NL)
            pool.dma_start(table[:, :], m.row_tok.rearrange("(p b) a -> p (b a)", p=P)).then_inc(s["table"], 16)
            pool.wait_ge(s["table"], 16)

            def gather(b, j, half):
                if late(b, 2):
                    pool.wait_ge(s["t_x"], b - 1)
                pool.tensor_copy(idx[:, j:j + 1], table[:, bass.ds(b, 1)]).then_inc(s["idx"], 1)
                pool.wait_ge(s["idx"], b + 1)
                pool.sem_inc(s["gather_begun"], 1)
                pool.indirect_dma_start(out=xg[:, j, :], out_offset=None, in_=m.h2,
                                        in_offset=bass.IndirectOffsetOnAxis(ap=idx[:, j:j + 1], axis=0))\
                    .then_inc(gathered[j], 16)
            each(pool, gather)

        @block.tensor
        def _(pe):
            def product(dst, a_hi, a_lo, q, at, k, first, last):
                ka = slice(k * P, (k + 1) * P)
                pe.matmul(dst, a_hi[:, ka], hi[:, q, at:at + 512], start=first, stop=False)
                pe.matmul(dst, a_hi[:, ka], lo[:, q, at:at + 512], start=False, stop=False)
                return pe.matmul(dst, a_lo[:, ka], hi[:, q, at:at + 512], start=False, stop=last)

            def turn_x(b, j, half):
                pe.wait_ge(gathered[j], 16 * half + 16)
                if late(b, 1):
                    pe.wait_ge(s["x_lo"], b)
                for k in range(KD):
                    last = pe.transpose(x_ps[:, k * P:(k + 1) * P], xg[:, j, k * P:(k + 1) * P], m.ident[:, :])
                last.then_inc(s["t_x"], 1)

            def down(b, j, half):
                pe.wait_ge(lo_done[2], 2 * b + 2)
                pe.wait_ge(s["h_lo"], b + 1)
                if late(b, 1):
                    pe.wait_ge(s["y_left"], b)
                for n in range(D // 512):
                    for k in range(HK):
                        last = product(y_ps[:, n * 512:(n + 1) * 512], ht_hi, ht_lo, 2, k * D + n * 512, k,
                                       k == 0, k == HK - 1)
                last.then_inc(made[2], 1)

            def step(b, j, half):
                pe.wait_ge(s["x_lo"], b + 1)
                if late(b, 1):
                    pe.wait_ge(s["hidden"], b)
                for q, dst in enumerate((g_ps, u_ps)):
                    pe.wait_ge(lo_done[q], 2 * b + 2)
                    for k in range(KD):
                        last = product(dst[:, :], xt_hi, xt_lo, q, k * FF, k, k == 0, k == KD - 1)
                    last.then_inc(made[q], 1)
                if more(b):
                    turn_x(b + 1, 1 - j, half + j)
                if late(b, 1):
                    down(b - 1, 1 - j, half - 1 + j)
                pe.wait_ge(s["hidden"], b + 1)
                if late(b, 1):
                    pe.wait_ge(s["h_lo"], b)
                for k in range(HK):
                    last = pe.transpose(h_ps[:, k * P:(k + 1) * P], hid[:, k * P:(k + 1) * P], m.ident[:, :])
                last.then_inc(s["t_h"], 1)
            turn_x(0, 0, 0)
            each(pe, step)
            down(BLOCKS - 1, (BLOCKS - 1) % 2, (BLOCKS - 1) // 2)

        @block.scalar
        def _(act):
            def split_hi(b, q):
                act.wait_ge(loaded[q], 16 * b + 16)
                if late(b, 1):
                    act.wait_ge(made[q], b)
                for h in (slice(0, HALF), slice(HALF, PIECE)):
                    act.activation(hi[:, q, h], raw[:, q, h], ACT.Copy).then_inc(hi_done[q], 1)

            def x_hi(b):
                act.wait_ge(s["t_x"], b + 1)
                act.activation(xt_hi[:, :], x_ps[:, :], ACT.Copy).then_inc(s["x_hi"], 1)

            def out(b, j, half):
                act.wait_ge(made[2], b + 1)
                if late(b, 2):
                    act.wait_ge(stored[j], 16 * half)
                act.activation(yo[:, j, :], y_ps[:, :], ACT.Copy).then_inc(s["y_left"], 1)
                act.wait_ge(s["y_left"], b + 1)
                act.dma_start(m.y_rows[bass.ds(b * P, P), :], yo[:, j, :]).then_inc(stored[j], 16)

            def step(b, j, half):
                act.wait_ge(made[0], b + 1)
                if late(b, 1):
                    act.wait_ge(s["hidden"], b)
                act.activation(gate[:, :], g_ps[:, :], ACT.Silu).then_inc(s["gate"], 1)
                if more(b):
                    split_hi(b + 1, 0)
                    split_hi(b + 1, 1)
                    x_hi(b + 1)
                if late(b, 1):
                    out(b - 1, 1 - j, half - 1 + j)
                split_hi(b, 2)
            split_hi(0, 0)
            x_hi(0)
            split_hi(0, 1)
            each(act, step)
            out(BLOCKS - 1, (BLOCKS - 1) % 2, (BLOCKS - 1) // 2)
            act.wait_ge(stored[0], 16 * ((BLOCKS + 1) // 2))
            act.wait_ge(stored[1], 16 * (BLOCKS // 2))

        @block.vector
        def _(dve):
            def split_lo(b, q):
                for h in range(2):
                    at = slice(h * HALF, (h + 1) * HALF)
                    dve.wait_ge(hi_done[q], 2 * b + 1 + h)
                    dve.tensor_tensor(lo[:, q, at], raw[:, q, at], hi[:, q, at].bitcast(F32), ALU.subtract)\
                        .then_inc(lo_done[q], 1)

            def x_lo(b):
                dve.wait_ge(s["x_hi"], b + 1)
                dve.tensor_tensor(xt_lo[:, :], x_ps[:, :], xt_hi[:, :].bitcast(F32), ALU.subtract)\
                    .then_inc(s["x_lo"], 1)

            def step(b, j, half):
                if more(b):
                    split_lo(b + 1, 0)
                dve.wait_ge(s["gate"], b + 1)
                dve.wait_ge(made[1], b + 1)
                if late(b, 1):
                    dve.wait_ge(s["t_h"], b)
                dve.tensor_tensor(hid[:, :], u_ps[:, :], gate[:, :], ALU.mult).then_inc(s["hidden"], 1)
                if more(b):
                    split_lo(b + 1, 1)
                    x_lo(b + 1)
                dve.wait_ge(s["t_h"], b + 1)
                if late(b, 1):
                    dve.wait_ge(made[2], b)
                dve.tensor_copy(ht_hi[:, :], h_ps[:, :]).then_inc(s["h_hi"], 1)
                dve.wait_ge(s["h_hi"], b + 1)
                dve.tensor_tensor(ht_lo[:, :], h_ps[:, :], ht_hi[:, :].bitcast(F32), ALU.subtract)\
                    .then_inc(s["h_lo"], 1)
                split_lo(b, 2)
            split_lo(0, 0)
            x_lo(0)
            split_lo(0, 1)
            each(dve, step)


def combine(nc, m, sem, w):
    with ExitStack() as ctx:
        sb = lambda n, s: ctx.enter_context(nc.sbuf_tensor(n, s, F32))
        yr = sb("co_rows", [P, NL, TOP_K, D])
        x1 = sb("co_x1", [P, NL, D])
        sq = sb("co_sq", [P, 2, D])
        gate2 = sb("co_gate2", [P, D])
        gf = sb("co_g_final", [P, D])
        st = sb("co_stat", [P, NL, 3])
        loaded, scaled, summed, gated, x2_ready, stat, normed, stored = (sem(f"co_{n}") for n in (
            "loaded", "scaled", "summed", "gated", "x2_ready", "stat", "normed", "stored"))
        gathered, x_loaded = ([sem(f"co_{name}{n}") for n in range(NL)] for name in ("gathered", "x_loaded"))
        block = ctx.enter_context(nc.Block())

        @block.sync
        def _(sp):
            sp.dma_start(gate2[:, :], m.mod_rows[:, 3 * D:4 * D]).then_inc(loaded, 16)
            sp.dma_start(gf[:, :], w["g_final"].rearrange("(a n) -> a n", a=1).partition_broadcast(P))\
                .then_inc(loaded, 16)
            for n in range(NL):
                sp.dma_start(x1[:, n, :], m.x1[n * P:(n + 1) * P, :]).then_inc(x_loaded[n], 16)
            for n in range(NL):
                sp.wait_ge(normed, n + 1)
                sp.dma_start(m.out[0, n * P:(n + 1) * P, :], yr[:, n, 0, :]).then_inc(stored, 16)
            sp.wait_ge(stored, 16 * NL)

        @block.gpsimd
        def _(pool):
            for n in range(NL):
                for k in range(TOP_K):
                    pool.indirect_dma_start(
                        out=yr[:, n, k, :], out_offset=None, in_=m.y_rows,
                        in_offset=bass.IndirectOffsetOnAxis(ap=m.dest_i[:, k, n:n + 1], axis=0))\
                        .then_inc(gathered[n], 16)
            pool.wait_ge(loaded, 32)
            for n in range(NL):
                pool.wait_ge(summed, n + 1)
                pool.tensor_tensor(yr[:, n, 0, :], yr[:, n, 0, :], gate2[:, :], ALU.mult).then_inc(gated, 1)

        @block.scalar
        def _(act):
            def scale(n):
                act.wait_ge(gathered[n], 32)
                act.activation(yr[:, n, 0, :], yr[:, n, 0, :], ACT.Copy, scale=m.weight[:, 0, n:n + 1])\
                    .then_inc(scaled, 1)

            def norm(n):
                act.wait_ge(x2_ready, n + 1)
                act.activation(sq[:, n % 2, :], x1[:, n, :], ACT.Square, accum_out=st[:, n, 0:1]).then_inc(stat, 1)
                act.wait_ge(stat, 3 * n + 1)
                act.activation(st[:, n, 1:2], st[:, n, 0:1], ACT.Ln, bias=m.eps[:, 0:1], scale=1.0 / D)\
                    .then_inc(stat, 1)
                act.wait_ge(stat, 3 * n + 2)
                act.activation(st[:, n, 2:3], st[:, n, 1:2], ACT.Exp, scale=-0.5).then_inc(stat, 1)
            for n in range(NL + 2):
                if n < NL:
                    scale(n)
                if n >= 2:
                    norm(n - 2)

        @block.vector
        def _(dve):
            def second(n):
                dve.wait_ge(scaled, n + 1)
                dve.scalar_tensor_tensor(out=yr[:, n, 0, :], in0=yr[:, n, 1, :], scalar=m.weight[:, 1, n:n + 1],
                                         in1=yr[:, n, 0, :], op0=ALU.mult, op1=ALU.add).then_inc(summed, 1)

            def residual(n):
                dve.wait_ge(gated, n + 1)
                dve.wait_ge(x_loaded[n], 16)
                dve.tensor_tensor(x1[:, n, :], x1[:, n, :], yr[:, n, 0, :], ALU.add).then_inc(x2_ready, 1)

            def finish(n):
                dve.wait_ge(stat, 3 * n + 3)
                dve.scalar_tensor_tensor(out=yr[:, n, 0, :], in0=x1[:, n, :], scalar=st[:, n, 2:3], in1=gf[:, :],
                                         op0=ALU.mult, op1=ALU.mult).then_inc(normed, 1)
            dve.wait_ge(loaded, 32)
            for n in range(NL + 3):
                if n < NL:
                    second(n)
                if 1 <= n < NL + 1:
                    residual(n - 1)
                if n >= 3:
                    finish(n - 3)




def build(nc, w, out, upto=99):
    m = Shared()
    top = ExitStack()
    with top:
        used = []

        def sem(name):
            used.append(nc.alloc_semaphore(name))
            return used[-1]

        def fresh_semaphores():
            nc.all_engine_barrier()
            nc.clear_and_free_semaphores(used)
            used.clear()
            nc.all_engine_barrier()

        def place(stack, name, shape, dt=F32):
            return stack.enter_context(nc.sbuf_tensor(name, shape, dt))

        def dram(name, shape, dt=F32):
            return nc.dram_tensor(name, shape, dt, kind="Internal").ap()

        def run(*stages):
            for stage in stages:
                stage(nc, m, sem, w)

        m.out = out
        m.vals = dram("vals", [2, T, D])
        m.gates = dram("out_gates", [4, SEQ, D])
        m.mod_rows = dram("mod_spread", [P, 4 * D])
        m.h_kept = dram("h_kept", [P, KD, T])
        m.hm = dram("mlstm_out", [SEQ, D])
        m.og = dram("gla_out", [SEQ, D])
        m.x1 = dram("x_mixed", [SEQ, D])
        m.h2 = dram("moe_in", [SEQ, D])
        m.row_tok = dram("row_token", [(BLOCKS + 1) * P, 1], I32)
        m.y_rows = dram("expert_rows", [BLOCKS * P, D])
        m.ident = place(top, "ident", [P, P])
        m.ones = place(top, "ones", [P, P])
        m.before = place(top, "before", [P, P])
        m.logits = place(top, "logits", [P, NL, GROUPS + EXPERTS])
        m.vec = place(top, "vec", [P, KD, NVEC])
        m.mod_col = place(top, "mod_col", [P, 2 * KD, 2])
        m.a1 = place(top, "a1", [P, KD, 2])
        m.eps = place(top, "eps", [P, 1])
        m.weight = place(top, "weight", [P, TOP_K, NL])
        m.place_i = place(top, "place_i", [P, TOP_K, NL], I32)
        m.token = place(top, "token", [P, NL], I32)
        m.dest_i = place(top, "dest_i", [P, TOP_K, NL], I32)
        m.block_e = place(top, "block_e", [P, BLOCKS + 1], I32)
        with ExitStack() as gla:
            m.row_of = place(gla, "row_of", [GATE_ROWS, 2 * HEADS, P])
            m.level_mask = place(gla, "level_mask", [P, 2, LEVELS, HEADS * P // 2], mybir.dt.int8)
            m.restart = place(gla, "restart", [P, 2, 5 * P])
            run(constants, modulation)
            with ExitStack() as split:
                m.h_hi = place(split, "h_hi", [P, KD, T], F32R)
                m.h_lo = place(split, "h_lo", [P, KD, T], F32R)
                with ExitStack() as whole:
                    m.h_t = place(whole, "h_first", [P, KD, T])
                    run(norm_in)
                run(project_rows)
            fresh_semaphores()
            m.qg = place(gla, "qg", [P, HEADS, SEQ])
            m.kg = place(gla, "kg", [P, HEADS, T])
            m.lr = place(gla, "lr", [32, 2, T])
            m.w2 = place(gla, "w2", [32, 2, HEADS * DK])
            with ExitStack() as mls:
                m.qm = place(mls, "qm", [P, HEADS, SEQ])
                m.km = place(mls, "km", [P, HEADS, T])
                m.gate_i = place(mls, "gate_i", [GATE_ROWS, T])
                m.gate_f = place(mls, "gate_f", [GATE_ROWS, T])
                with ExitStack() as proj:
                    m.h_t = place(proj, "h_t", [P, KD, T])
                    run(project_qk, project_small)
                fresh_semaphores()
                m.gate_g = place(mls, "gate_g", [GATE_ROWS, T])
                m.neg_m = place(mls, "neg_m", [GATE_ROWS, T])
                m.w_inter = place(mls, "w_inter", [GATE_ROWS, T])
                m.g_col = place(mls, "g_col", [P, NT, GATE_ROWS])
                m.ws_col = place(mls, "ws_col", [P, NT, GATE_ROWS])
                m.emt_col = place(mls, "emt_col", [P, NT, GATE_ROWS])
                m.dec_all = place(mls, "dec_all", [P, 2 * HEADS, NT])
                run(gate_rows)
                if upto >= 1:
                    run(mlstm_scan)
            if upto >= 2:
                run(gla_scan)
        fresh_semaphores()
        if upto >= 3:
            run(mix_out)
        if upto >= 4:
            run(route, experts, combine)


_INS = ["x", "c", "ctx", "c_ctx", "w_mod", "b_mod", "g_norm1", "w_in", "ml_conv", "ml_conv_b", "b_mgate", "ml_norm",
        "gla_w2", "gla_b2", "gla_norm", "w_proj_m", "w_proj_g", "w_out", "g_norm2", "w_grp", "b_grp", "w_rexp",
        "b_rexp", "w_up", "w_down", "g_final"]


def kernel(**inputs):
    import numpy as _np
    import concourse.bacc as _bacc
    from concourse import mybir as _mybir
    from concourse.bass_utils import run_bass_kernel_spmd as _run

    nc = _bacc.Bacc("TRN2", target_bir_lowering=False, num_devices=1)
    arrays, w = {}, {}
    for name in _INS:
        a = _np.ascontiguousarray(inputs[name])
        arrays[f"in_{name}_dram"] = a
        w[name] = nc.dram_tensor(f"in_{name}_dram", a.shape, _mybir.dt.from_np(a.dtype), kind="ExternalInput").ap()
    out = nc.dram_tensor("out_0_dram", (1, SEQ, D), F32, kind="ExternalOutput").ap()
    build(nc, w, out)
    r = _run(nc, [arrays], core_ids=[0])
    return r.results[0]["out_0_dram"]
```
